# Optimizing a Trainium2 kernel written in Bass

```python
import math
import jax, jax.numpy as jnp
from jax import lax
import numpy as np

D_MODEL = 1024
BATCH = 1
SEQ = 512
DEPTH = 2

CONV_CH = D_MODEL // 2
CONV_WIDTH = 31
DIFF_HEADS = 4
DIFF_HEAD_DIM = (D_MODEL // 2) // DIFF_HEADS // 2
DIFF_QK = 2 * DIFF_HEADS * DIFF_HEAD_DIM
DIFF_V = DIFF_HEADS * 2 * DIFF_HEAD_DIM
ROPE_THETA = 500000.0
ROT_DIM = DIFF_HEAD_DIM // 4
GDN_HEADS = 4
GDN_HEAD_DIM = (D_MODEL // 2) // GDN_HEADS
GDN_W = GDN_HEADS * GDN_HEAD_DIM
GDN_CONV = 4
GDN_CHUNK = 64
FOX_HEADS = 4
FOX_HEAD_DIM = (D_MODEL // 2) // FOX_HEADS
FOX_W = FOX_HEADS * FOX_HEAD_DIM
Q_BLOCK = 128
D_FF = ((8 * D_MODEL + 3 * 256 - 1) // (3 * 256)) * 256
EVEN_IN = 2 * CONV_CH + 2 * DIFF_QK + DIFF_V
ODD_IN = 4 * GDN_W + 2 * GDN_HEADS + 3 * FOX_W + FOX_HEADS
MIX_W = CONV_CH + DIFF_V

kernel_name = 'hybrid_conformer_diffattn_gdn_fox'

def _split(t, sizes):
    return jnp.split(t, np.cumsum(sizes)[:-1].tolist(), axis=-1)

def rms_norm(x, w, eps=1e-6):
    xf = x.astype(jnp.float32)
    y = xf * lax.rsqrt(jnp.mean(xf * xf, axis=-1, keepdims=True) + eps)
    return (y * w.astype(jnp.float32)).astype(x.dtype)

def layer_norm(x, w, b, eps=1e-5):
    xf = x.astype(jnp.float32)
    mu = jnp.mean(xf, axis=-1, keepdims=True)
    xc = xf - mu
    var = jnp.mean(xc * xc, axis=-1, keepdims=True)
    return (xc * lax.rsqrt(var + eps) * w.astype(jnp.float32) + b.astype(jnp.float32)).astype(x.dtype)

def l2_normalize(x, eps=1e-6):
    xf = x.astype(jnp.float32)
    return xf * lax.rsqrt(jnp.sum(xf * xf, axis=-1, keepdims=True) + eps)

def causal_depthwise_conv(x, w):
    K, C = w.shape
    return lax.conv_general_dilated(
        x, w[:, None, :].astype(x.dtype), window_strides=(1,), padding=[(K - 1, 0)],
        dimension_numbers=('NWC', 'WIO', 'NWC'), feature_group_count=C)

def partial_rotary(x, pos):
    half = ROT_DIM // 2
    inv_freq = 1.0 / (ROPE_THETA ** (jnp.arange(half, dtype=jnp.float32) / half))
    ang = pos.astype(jnp.float32)[:, None] * inv_freq[None, :]
    cos = jnp.cos(ang)[None, :, None, :]
    sin = jnp.sin(ang)[None, :, None, :]
    x1 = x[..., :half].astype(jnp.float32)
    x2 = x[..., half:ROT_DIM].astype(jnp.float32)
    rot = jnp.concatenate([x1 * cos - x2 * sin, x2 * cos + x1 * sin], axis=-1)
    return jnp.concatenate([rot.astype(x.dtype), x[..., ROT_DIM:]], axis=-1)

def _block_mask(i, S):
    qpos = i * Q_BLOCK + jnp.arange(Q_BLOCK)
    return jnp.arange(S)[None, :] <= qpos[:, None]

def diff_attention(q, k, v, lam):
    B_, S, H2, Dh = q.shape
    H = H2 // 2
    nb = S // Q_BLOCK
    qb = q.reshape(B_, nb, Q_BLOCK, H2, Dh).transpose(1, 0, 3, 2, 4)
    scale = Dh ** -0.5

    def block(args):
        q_i, i = args
        s = jnp.einsum('bhqd,bkhd->bhqk', q_i, k).astype(jnp.float32) * scale
        s = jnp.where(_block_mask(i, S), s, -jnp.inf)
        p = jax.nn.softmax(s, axis=-1).reshape(B_, H, 2, Q_BLOCK, S)
        w = p[:, :, 0] - lam * p[:, :, 1]
        return jnp.einsum('bhqk,bkhe->bqhe', w.astype(v.dtype), v)

    o = lax.map(block, (qb, jnp.arange(nb)))
    return o.transpose(1, 0, 2, 3, 4).reshape(B_, S, H, 2 * Dh)

def forgetting_attention(q, k, v, log_f):
    B_, S, H, D = q.shape
    nb = S // Q_BLOCK
    c = jnp.cumsum(log_f, axis=1)
    qb = q.reshape(B_, nb, Q_BLOCK, H, D).transpose(1, 0, 3, 2, 4)
    cq = c.reshape(B_, nb, Q_BLOCK, H).transpose(1, 0, 3, 2)
    ck = c.transpose(0, 2, 1)
    scale = D ** -0.5

    def block(args):
        q_i, c_i, i = args
        s = jnp.einsum('bhqd,bkhd->bhqk', q_i, k).astype(jnp.float32) * scale
        s = s + c_i[..., None] - ck[:, :, None, :]
        s = jnp.where(_block_mask(i, S), s, -jnp.inf)
        p = jax.nn.softmax(s, axis=-1)
        return jnp.einsum('bhqk,bkhd->bqhd', p.astype(v.dtype), v)

    o = lax.map(block, (qb, cq, jnp.arange(nb)))
    return o.transpose(1, 0, 2, 3, 4).reshape(B_, S, H, D)

def gated_delta_rule(q, k, v, g, beta):
    f32 = jnp.float32
    B_, S, H, Dk = q.shape
    Dv = v.shape[-1]
    C = GDN_CHUNK
    nc = S // C

    def chunks(t):
        return t.astype(f32).reshape(B_, nc, C, H, -1).transpose(0, 3, 1, 2, 4)

    q = chunks(q) * (Dk ** -0.5)
    k = chunks(k)
    v = chunks(v)
    beta = chunks(beta[..., None])[..., 0]
    g = jnp.cumsum(chunks(g[..., None])[..., 0], axis=-1)
    idx = jnp.arange(C)
    causal = idx[:, None] >= idx[None, :]
    strict = idx[:, None] > idx[None, :]
    gdiff = g[..., :, None] - g[..., None, :]
    decay = jnp.where(causal, jnp.exp(jnp.where(causal, gdiff, 0.0)), 0.0)
    k_beta = k * beta[..., None]
    a_mat = jnp.where(strict, jnp.einsum('bhncd,bhned->bhnce', k_beta, k) * decay, 0.0)
    eye = jnp.eye(C, dtype=f32)
    t_inv = lax.linalg.triangular_solve(eye + a_mat, jnp.broadcast_to(eye, a_mat.shape),
                                        left_side=True, lower=True, unit_diagonal=True)
    u = jnp.einsum('bhnce,bhned->bhncd', t_inv, v * beta[..., None])
    w = jnp.einsum('bhnce,bhned->bhncd', t_inv, k_beta * jnp.exp(g)[..., None])
    qk = jnp.where(causal, jnp.einsum('bhncd,bhned->bhnce', q, k) * decay, 0.0)

    def step(state, xs):
        q_i, k_i, u_i, w_i, g_i, qk_i = xs
        v_new = u_i - jnp.einsum('bhcd,bhde->bhce', w_i, state)
        o_i = (jnp.einsum('bhcd,bhde->bhce', q_i * jnp.exp(g_i)[..., None], state)
               + jnp.einsum('bhce,bhed->bhcd', qk_i, v_new))
        g_last = g_i[..., -1:]
        state = (state * jnp.exp(g_last)[..., None]
                 + jnp.einsum('bhcd,bhce->bhde', k_i * jnp.exp(g_last - g_i)[..., None], v_new))
        return state, o_i

    xs = tuple(jnp.moveaxis(t, 2, 0) for t in (q, k, u, w, g, qk))
    state0 = jnp.zeros((B_, H, Dk, Dv), f32)
    _, o = lax.scan(step, state0, xs)
    return o.transpose(1, 0, 3, 2, 4).reshape(B_, S, H, Dv)

def even_mixer(h, pos, w_in, conv_w, conv_b, ln_w, ln_b, lq1, lk1, lq2, lk2, subln_w, lambda_init):
    B_, S, _ = h.shape
    a_val, a_gate, q, k, v = _split(h @ w_in, [CONV_CH, CONV_CH, DIFF_QK, DIFF_QK, DIFF_V])
    u = a_val * jax.nn.sigmoid(a_gate)
    u = causal_depthwise_conv(u, conv_w) + conv_b.astype(u.dtype)
    u = jax.nn.silu(layer_norm(u, ln_w, ln_b))
    q = partial_rotary(q.reshape(B_, S, 2 * DIFF_HEADS, DIFF_HEAD_DIM), pos)
    k = partial_rotary(k.reshape(B_, S, 2 * DIFF_HEADS, DIFF_HEAD_DIM), pos)
    v = v.reshape(B_, S, DIFF_HEADS, 2 * DIFF_HEAD_DIM)
    f32 = jnp.float32
    lam = (jnp.exp(jnp.sum(lq1.astype(f32) * lk1.astype(f32)))
           - jnp.exp(jnp.sum(lq2.astype(f32) * lk2.astype(f32))) + lambda_init)
    o = diff_attention(q, k, v, lam)
    o = rms_norm(o, subln_w) * (1.0 - lambda_init)
    return jnp.concatenate([u, o.reshape(B_, S, DIFF_V)], axis=-1)

def odd_mixer(h, sconv_w, w_in, a_log, dt_bias, gnorm_w, f_bias):
    B_, S, _ = h.shape
    f32 = jnp.float32
    qkv_c, z_c, b_c, a_c, q_d, k_d, v_d, f_d = _split(
        h @ w_in, [3 * GDN_W, GDN_W, GDN_HEADS, GDN_HEADS, FOX_W, FOX_W, FOX_W, FOX_HEADS])
    qkv_c = jax.nn.silu(causal_depthwise_conv(qkv_c, sconv_w))
    q_c, k_c, v_c = [t.reshape(B_, S, GDN_HEADS, GDN_HEAD_DIM) for t in _split(qkv_c, [GDN_W, GDN_W, GDN_W])]
    beta = jax.nn.sigmoid(b_c.astype(f32))
    g = -jnp.exp(a_log.astype(f32)) * jax.nn.softplus(a_c.astype(f32) + dt_bias.astype(f32))
    o_c = gated_delta_rule(l2_normalize(q_c), l2_normalize(k_c), v_c, g, beta).astype(h.dtype)
    o_c = rms_norm(o_c, gnorm_w) * jax.nn.silu(z_c.reshape(B_, S, GDN_HEADS, GDN_HEAD_DIM))
    log_f = jax.nn.log_sigmoid(f_d.astype(f32) + f_bias.astype(f32))
    o_d = forgetting_attention(q_d.reshape(B_, S, FOX_HEADS, FOX_HEAD_DIM),
                               k_d.reshape(B_, S, FOX_HEADS, FOX_HEAD_DIM),
                               v_d.reshape(B_, S, FOX_HEADS, FOX_HEAD_DIM), log_f)
    return jnp.concatenate([o_c.reshape(B_, S, GDN_W), o_d.reshape(B_, S, FOX_W)], axis=-1)

def setup_inputs(seed: int = 0) -> dict:
    key = jax.random.key(seed)
    ks = jax.random.split(key, 32)
    n_even = (DEPTH + 1) // 2
    n_odd = DEPTH // 2
    f32 = jnp.float32

    def nrm(k, shape, scale):
        return jax.random.normal(k, shape, f32) * scale

    dt = jnp.exp(jax.random.uniform(ks[17], (n_odd, GDN_HEADS), f32, math.log(1e-3), math.log(1e-1)))
    return {
        'x': nrm(ks[0], (BATCH, SEQ, D_MODEL), 1.0),
        'mix_norm_w': 1.0 + nrm(ks[1], (DEPTH, D_MODEL), 0.02),
        'ffn_norm_w': 1.0 + nrm(ks[2], (DEPTH, D_MODEL), 0.02),
        'final_norm_w': 1.0 + nrm(ks[3], (D_MODEL,), 0.02),
        'w_in_even': nrm(ks[4], (n_even, D_MODEL, EVEN_IN), D_MODEL ** -0.5),
        'conv_w': nrm(ks[5], (n_even, CONV_WIDTH, CONV_CH), CONV_WIDTH ** -0.5),
        'conv_b': nrm(ks[6], (n_even, CONV_CH), 0.02),
        'conv_ln_w': 1.0 + nrm(ks[7], (n_even, CONV_CH), 0.02),
        'conv_ln_b': nrm(ks[8], (n_even, CONV_CH), 0.02),
        'lambda_q1': nrm(ks[9], (n_even, DIFF_HEAD_DIM), 0.1),
        'lambda_k1': nrm(ks[10], (n_even, DIFF_HEAD_DIM), 0.1),
        'lambda_q2': nrm(ks[11], (n_even, DIFF_HEAD_DIM), 0.1),
        'lambda_k2': nrm(ks[12], (n_even, DIFF_HEAD_DIM), 0.1),
        'diff_subln_w': 1.0 + nrm(ks[13], (n_even, 2 * DIFF_HEAD_DIM), 0.02),
        'gdn_conv_w': nrm(ks[14], (n_odd, GDN_CONV, 3 * GDN_W), GDN_CONV ** -0.5),
        'w_in_odd': nrm(ks[15], (n_odd, D_MODEL, ODD_IN), D_MODEL ** -0.5),
        'gdn_a_log': jnp.log(jax.random.uniform(ks[16], (n_odd, GDN_HEADS), f32, 1.0, 16.0)),
        'gdn_dt_bias': dt + jnp.log(-jnp.expm1(-dt)),
        'gdn_norm_w': 1.0 + nrm(ks[18], (n_odd, GDN_HEAD_DIM), 0.02),
        'fox_forget_bias': nrm(ks[19], (n_odd, FOX_HEADS), 0.1),
        'w_out': nrm(ks[20], (DEPTH, MIX_W, D_MODEL), MIX_W ** -0.5),
        'w_gate': nrm(ks[21], (DEPTH, D_MODEL, D_FF), D_MODEL ** -0.5),
        'w_up': nrm(ks[22], (DEPTH, D_MODEL, D_FF), D_MODEL ** -0.5),
        'w_down': nrm(ks[23], (DEPTH, D_FF, D_MODEL), D_FF ** -0.5),
    }

def reference(x, mix_norm_w, ffn_norm_w, final_norm_w, w_in_even, conv_w, conv_b, conv_ln_w, conv_ln_b,
              lambda_q1, lambda_k1, lambda_q2, lambda_k2, diff_subln_w, gdn_conv_w, w_in_odd,
              gdn_a_log, gdn_dt_bias, gdn_norm_w, fox_forget_bias, w_out, w_gate, w_up, w_down):
    pos = jnp.arange(x.shape[1])
    for l in range(DEPTH):
        i = l // 2
        h = rms_norm(x, mix_norm_w[l])
        if l % 2 == 0:
            lambda_init = 0.8 - 0.6 * math.exp(-0.3 * l)
            y = even_mixer(h, pos, w_in_even[i], conv_w[i], conv_b[i], conv_ln_w[i], conv_ln_b[i],
                           lambda_q1[i], lambda_k1[i], lambda_q2[i], lambda_k2[i], diff_subln_w[i],
                           lambda_init)
        else:
            y = odd_mixer(h, gdn_conv_w[i], w_in_odd[i], gdn_a_log[i], gdn_dt_bias[i], gdn_norm_w[i],
                          fox_forget_bias[i])
        x = x + y @ w_out[l]
        h = rms_norm(x, ffn_norm_w[l])
        x = x + (jax.nn.silu(h @ w_gate[l]) * (h @ w_up[l])) @ w_down[l]
    return rms_norm(x, final_norm_w)


_drawn_inputs = setup_inputs


def setup_inputs(seed=0):
    import zlib

    import numpy as np

    out = dict(_drawn_inputs(seed))
    spreads = {}
    factors = {'ffn_norm_w': 3.038,
     'final_norm_w': 8.989,
     'conv_b': 2.944,
     'conv_ln_w': 5.114,
     'conv_ln_b': 6.334,
     'lambda_q1': 5.861,
     'lambda_k1': 8.0,
     'diff_subln_w': 4.659,
     'gdn_norm_w': 52.101,
     'fox_forget_bias': 31.203,
     'lambda_q2': 8.0,
     'lambda_k2': 8.0}
    for name, (base, spread) in spreads.items():
        noise = np.random.default_rng([zlib.crc32(name.encode()), seed]).standard_normal(out[name].shape)
        drawn = base * np.exp(spread * noise) if base else spread * noise
        out[name] = __import__('jax').numpy.asarray(drawn.astype(out[name].dtype))
    for name, factor in factors.items():
        out[name] = (out[name] * factor).astype(out[name].dtype)
    return out
```

```python
import math

import numpy as np
import concourse.bass as bass
from concourse import mybir

P = 128
S = 512
D = 1024
NB = S // P
KD = D // P
FF = 2816
KF = FF // P
H = 4
TAPS, GTAPS = 31, 4
TILE = 1024
BIG = -1.0e30

T_IN0 = 0
T_OUT0 = T_IN0 + 20
T_GU0 = T_OUT0 + KD
T_DN0 = T_GU0 + 2 * KF
T_IN1 = T_DN0 + KF
T_OUT1 = T_IN1 + 28
T_GU1 = T_OUT1 + KD
T_DN1 = T_GU1 + 2 * KF
N_TILES = T_DN1 + KF
E_IN0 = 0
E_OUT0 = E_IN0 + 20
E_GU0 = E_OUT0 + KD
E_DN0 = E_GU0 + 2 * KF
E_IN1 = E_DN0 + KD
E_OUT1 = E_IN1 + 28
E_GU1 = E_OUT1 + KD
E_DN1 = E_GU1 + 2 * KF
RING = 4
RAW = 2

V_NORM = 0
V_CONVW = 40
V_CONVB = V_CONVW + 4 * TAPS
V_LNW = V_CONVB + 4
V_LNB = V_LNW + 4
V_SUBLN = V_LNB + 4
V_GCONV = V_SUBLN + 1
V_GNORM = V_GCONV + 12 * GTAPS
V_LAM = V_GNORM + 1
N_VEC = V_LAM + 4
LEVELS = [1, 2, 4, 8, 16, 32, 64]
LAMBDA_INIT = 0.8 - 0.6 * math.exp(-0.3 * 0)


def shape_constants():
    r = np.arange(P)
    row, col = r[:, None], r[None, :]
    parts = [
        np.eye(P),
        (row <= col) * 1.0,
        np.ones((P, P)),
        np.where(col > row, BIG, 0.0),
        np.where(row > col, BIG, 0.0),
    ]
    for b in LEVELS:
        parts.append(((row // (2 * b) == col // (2 * b)) & (row % (2 * b) < b) & (col % (2 * b) >= b)) * 1.0)
    const = np.concatenate(parts, axis=1).astype(np.float32)
    half = 8
    inv = (1.0 / (np.float32(500000.0) ** (np.arange(half, dtype=np.float32) / half))).astype(np.float32)
    ang = np.arange(S, dtype=np.float32)[:, None] * inv[None, :]
    cos, sin = np.cos(ang).astype(np.float32).T, np.sin(ang).astype(np.float32).T
    rc, rs, perm = np.ones((P, S)), np.zeros((P, S)), np.zeros((P, P))
    for p in range(P):
        q = p % 64
        if q < half:
            rc[p], rs[p], perm[p + half, p] = cos[q], -sin[q], 1.0
        elif q < 2 * half:
            rc[p], rs[p], perm[p - half, p] = cos[q - half], sin[q - half], 1.0
    rope = np.concatenate([rc, rs, perm], axis=1).astype(np.float32)
    return const, rope


def build(nc, x_d, w_d, vec_d, row_d, wsm_d, const_d, rope_d, out_d):
    f32, f32r, i32 = mybir.dt.float32, mybir.dt.float32r, mybir.dt.int32
    ALU, ACT, AX = mybir.AluOpType, mybir.ActivationFunctionType, mybir.AxisListType
    DH = 128
    SC_FOX = float(DH) ** -0.5
    SC_DIFF = 0.125

    size = {f32: 4, f32r: 4}

    def at(name, shape, dt, offset):
        t = nc.alloc_sbuf_tensor_at(name, [P] + list(shape), dt, offset=offset)
        return t, offset + (int(np.prod(shape)) * size[dt] + 31) // 32 * 32

    base = 16512
    xT, p = at("xT", [KD, S], f32, base)
    raw, p = at("raw", [RAW, TILE], f32, p)
    wring, p = at("wring", [RING, 2, TILE], f32r, p)
    at_H = p
    HH, p = at("HH", [KD, 2, S], f32r, p)
    consts, p = at("consts", [5 + len(LEVELS), P], f32, p)
    at_work = p
    hbuf, p = at("hbuf", [2, S], f32, p)
    sqb, p = at("sqb", [2, S], f32, p)
    ssq, p = at("ssq", [S], f32, p)
    rstd, p = at("rstd", [S], f32, p)
    vec, p = at("vec", [N_VEC], f32, p)
    at_small = p
    p += 2848
    at_A = p
    AA, p = at("AA", [KF, 2, S], f32r, p)
    gbuf, p = at("gbuf", [2, S], f32, p)
    ubuf, p = at("ubuf", [2, S], f32, p)
    abuf, p = at("abuf", [S], f32, p)
    TOP = 229344
    assert p <= TOP, p
    q = at_small
    rtok, q = at("rtok", [NB], f32, q)
    nst, q = at("nst", [NB], f32, q)
    lam, q = at("lam", [8], f32, q)
    lst, q = at("lst", [8], f32, q)
    amax, q = at("amax", [2, 2], f32, q)
    asum, q = at("asum", [2, 2], f32, q)
    arec, q = at("arec", [2, 2], f32, q)
    ost, q = at("ost", [2, 16], f32, q)
    wsm, q = at("wsm", [2, KD * 12], f32r, q)
    rowv, q = at("rowv", [12], f32, q)
    srow, q = at("srow", [12], f32, q)
    baf, q = at("baf", [NB, 12], f32, q)
    z8, q = at("z8", [NB, 8], f32, q)
    e8, q = at("e8", [NB, 8], f32, q)
    sp8, q = at("sp8", [NB, 8], f32, q)
    expa, q = at("expa", [4], f32, q)
    beta, q = at("beta", [NB, H], f32, q)
    gtok, q = at("gtok", [NB, H], f32, q)
    lftok, q = at("lftok", [NB, H], f32, q)
    gcum, q = at("gcum", [3, NB, H], f32, q)
    gexp, q = at("gexp", [3, NB, H], f32, q)
    l2s, q = at("l2s", [NB, 8], f32, q)
    kscal, q = at("kscal", [3, NB, H], f32, q)
    qscal, q = at("qscal", [NB, H], f32, q)
    assert q <= at_A, (q, at_A)
    at_M = at_A + 8 * 2 * S * 4
    q = at_M
    rope, q = at("rope", [2 * S + P], f32, q)
    upad, q = at("upad", [4, S + TAPS - 1], f32, q)
    cacc, q = at("cacc", [4, S], f32, q)
    qk, q = at("qk", [8, S], f32, q)
    vtk, q = at("vtk", [NB, S], f32, q)
    WT, q = at("WT", [2, NB, S], f32, q)
    assert q <= TOP
    q = at_H
    pbuf, q = at("pbuf", [2, 2, S], f32, q)
    wbuf, q = at("wbuf", [2, S], f32, q)
    oT, q = at("oT", [H, S], f32, q)
    osq, q = at("osq", [H, S], f32, q)
    ytmp, q = at("ytmp", [2, S], f32, q)
    assert q <= at_H + 32768
    q = at_M
    qT, q = at("qT", [H, S], f32, q)
    kT, q = at("kT", [H, S], f32, q)
    ktok, q = at("ktok", [NB, H, P], f32, q)
    vtok, q = at("vtok", [NB, H, P], f32, q)
    at_z = q
    zT, q = at("zT", [H, S], f32, q)
    qd, q = at("qd", [H, S], f32, q)
    kd, q = at("kd", [H, S], f32, q)
    vd, q = at("vd", [NB, S], f32, q)
    cin, q = at("cin", [S + GTAPS - 1], f32, q)
    assert q <= TOP, (q, TOP)
    wraw, _ = at("wraw", [KD * 12], f32, at_z)
    q = at_A + 4 * 2 * S * 4
    G8, q = at("G8", [8, H, P], f32, q)
    assert q == at_M
    decay_b, NT_b, qkT_b, kbe_b, R_b, T_b, Z_b, St_b = [G8[:, n] for n in range(8)]
    G5, _ = at("G5", [5, H, P], f32, at_work)
    eg_b, kbT_b, qe_b, wT_b, vn_b = [G5[:, n] for n in range(5)]
    gsq, _ = at("gsq", [H, S], f32, at_H)
    outT, _ = at("outT", [KD, S], f32, at_H)
    q = at_H
    cb, q = at("cb", [H, S], f32, q)
    tbuf, q = at("tbuf", [2, S], f32, q)
    fbuf, q = at("fbuf", [2, S], f32, q)
    FT, q = at("FT", [2, NB, S], f32, q)
    assert q <= at_H + 32768

    PS = nc.alloc_psum_tensor("PS", [P, 8, S], f32)

    ident, cums, ones = consts[:, 0], consts[:, 1], consts[:, 2]
    cmask, dmask = consts[:, 3], consts[:, 4]
    lmask = {b: consts[:, 5 + n].bitcast(i32) for n, b in enumerate(LEVELS)}

    def over_heads(ap):
        return ap.unsqueeze(1).broadcast_to([P, H, P])

    def per_head(ap):
        return ap.unsqueeze(2).broadcast_to([P, H, P])

    def blk(b):
        return slice(b * P, (b + 1) * P)

    def hd(ps_bank):
        return PS[:, ps_bank].rearrange("p (h c) -> p h c", h=H)

    def vcol(n):
        return vec[:, n:n + 1]

    sems = {}

    def sem(name):
        if name not in sems:
            sems[name] = nc.alloc_semaphore(name)
        return sems[name]

    def slot_round(t):
        return t // RING + 1

    x_loaded = [sem(f"x_loaded{n}") for n in range(4)]
    const_loaded, vec_loaded, rope_loaded, small_loaded = map(sem, ("const_loaded", "vec_loaded", "rope_loaded", "small_loaded"))
    raw_loaded = [sem(f"raw_loaded{n}") for n in range(RAW)]
    hi_ready = [sem(f"hi_ready{n}") for n in range(RING)]
    lo_ready = [sem(f"lo_ready{n}") for n in range(RING)]
    tile_used, evacuated = sem("tile_used"), sem("evacuated")
    feed_mul, feed_hi, feed_sq, ssq_done, h_ready = map(sem, ("feed_mul", "feed_hi", "feed_sq", "ssq_done", "h_ready"))
    norm_sum, norm_ms, norm_sqrt, norm_tok, norm_bc, norm_rstd = map(
        sem, ("norm_sum", "norm_ms", "norm_sqrt", "norm_tok", "norm_bc", "norm_rstd"))
    y_ready = sem("y_ready")
    down_done = sem("down_done")
    out_done = sem("out_done")
    dchain = sem("dve_chain")

    UNITS = [(h, i) for h in range(H) for i in range(NB)]
    FINAL = 4

    block = nc.Block()
    block.__enter__()

    @block.sync
    def _(sp):
        for n in range(4):
            sp.dma_start(xT[:, 2 * n:2 * n + 2], x_d[:, 2 * n:2 * n + 2]).then_inc(x_loaded[n], 16)
        for t in range(RAW):
            sp.dma_start(raw[:, t], w_d[t]).then_inc(raw_loaded[t], 16)
        for t in range(RAW, RING):
            sp.wait_ge(hi_ready[t - RAW], 1)
            sp.wait_ge(lo_ready[t - RAW], 1)
            sp.dma_start(raw[:, t % RAW], w_d[t]).then_inc(raw_loaded[t % RAW], 16)
        with sp.Fori(1, N_TILES // RING) as r:
            for j in range(RING):
                behind = (j - RAW) % RING
                done = r if j < RAW else r + 1
                sp.wait_ge(hi_ready[behind], done)
                sp.wait_ge(lo_ready[behind], done)
                src = w_d[bass.ds(r * RING + j, 1)].rearrange("a p c -> (a p) c")
                sp.dma_start(raw[:, j % RAW], src).then_inc(raw_loaded[j % RAW], 16)
        for n in range(KD):
            sp.wait_ge(sem("out_ready"), n + 1)
            sp.dma_start(out_d[:, n], outT[:, n]).then_inc(out_done, 16)
        sp.wait_ge(out_done, 16 * KD)

    @block.gpsimd
    def _(pool):
        def lo(t):
            pool.wait_ge(hi_ready[t % RING], slot_round(t))
            if t >= RING:
                pool.wait_ge(tile_used, t - RING + 1)
            nc.gpsimd.tensor_tensor(wring[:, t % RING, 1], raw[:, t % RAW], wring[:, t % RING, 0].bitcast(f32),
                                    ALU.subtract).then_inc(lo_ready[t % RING], 1)

        def add_squares(s, n):
            if n == 0:
                return
            pool.wait_ge(feed_sq, KD * s + n + 1)
            if n == 1:
                if s:
                    pool.wait_ge(norm_sum, s)
                nc.gpsimd.tensor_tensor(ssq[:], sqb[:, 0], sqb[:, 1], ALU.add).then_inc(ssq_done, 1)
            else:
                pool.wait_ge(ssq_done, 7 * s + n - 1)
                nc.gpsimd.tensor_tensor(ssq[:], ssq[:], sqb[:, n % 2], ALU.add).then_inc(ssq_done, 1)

        for n in range(KD):
            add_squares(0, n)
            if n % 2:
                lo(n // 2)
        nc.gpsimd.memset(upad[:, :, 0:TAPS - 1], 0.0).then_inc(sem("pad_zero"), 1)
        for t in range(4, 24):
            lo(t)
        for n in range(KD):
            if n < 4:
                lo(T_OUT0 + RING + n)
            add_squares(1, n)
        for n in range(KD):
            add_squares(2, n)
        nc.gpsimd.memset(cin[:, 0:GTAPS - 1], 0.0).then_inc(sem("cin_zero"), 1)
        for t in range(T_IN1 + RING, T_OUT1 + RING):
            lo(t)
        pool.wait_ge(sem("gdn_scalars"), 1)
        nc.gpsimd.memset(St_b, 0.0).then_inc(sem("state_zero"), 1)
        for i in range(NB):
            pool.wait_ge(sem("tok_ready"), 8)
            if i:
                pool.wait_ge(sem("gdn_state_mm"), i)
            nc.gpsimd.tensor_tensor(kbe_b, ktok[:, i], per_head(kscal[:, 1, i]), ALU.mult).then_inc(sem("kbe_ready"), 1)
            nc.gpsimd.tensor_tensor(vtok[:, i], vtok[:, i], per_head(beta[:, i]), ALU.mult).then_inc(sem("vb_ready"), 1)
            nc.gpsimd.tensor_tensor(ktok[:, i], ktok[:, i], per_head(kscal[:, 2, i]), ALU.mult).then_inc(sem("kl_ready"), 1)
        for n in range(KD):
            if n < 4:
                lo(T_OUT1 + RING + n)
            add_squares(3, n)
        for n in range(KD):
            add_squares(4, n)

    @block.scalar
    def _(act):
        act.dma_start(vec[:], vec_d).then_inc(vec_loaded, 16)
        act.dma_start(consts[:].rearrange("p a b -> p (a b)"), const_d).then_inc(const_loaded, 16)
        act.dma_start(rope[:], rope_d).then_inc(rope_loaded, 16)
        act.dma_start(rowv[0:1, :], row_d).then_inc(small_loaded, 16)

        def hi(t):
            act.wait_ge(raw_loaded[t % RAW], 16 * (t // RAW + 1))
            if t >= RING:
                act.wait_ge(tile_used, t - RING + 1)
            nc.scalar.activation(wring[:, t % RING, 0], raw[:, t % RAW], ACT.Copy).then_inc(hi_ready[t % RING], 1)

        def feed(s, n):
            if s < FINAL:
                act.wait_ge(feed_mul, KD * s + n + 1)
                nc.scalar.activation(HH[:, n, 0], hbuf[:, n % 2], ACT.Copy).then_inc(feed_hi, 1)
            else:
                act.wait_ge(evacuated, E_DN1 + n + 1)
            if n >= 2:
                act.wait_ge(ssq_done, 7 * s + max(n - 2, 1))
            elif s:
                act.wait_ge(ssq_done, 7 * s)
            nc.scalar.activation(sqb[:, n % 2], xT[:, n], ACT.Square).then_inc(feed_sq, 1)

        def norm_root(s):
            act.wait_ge(norm_ms, s + 1)
            nc.scalar.activation(nst[:], nst[:], ACT.Sqrt).then_inc(norm_sqrt, 1)

        def ffn(s, tg, eg, last):
            g0 = KF * s
            with act.Fori(0, KF // 2) as r:
                for c in range(2):
                    done = r * 2 + (g0 + c + 1)
                    act.wait_ge(evacuated, r * RING + (eg + 2 * c + 1))
                    nc.scalar.activation(gbuf[:, c], gbuf[:, c], ACT.Silu).then_inc(sem("gate_silu"), 1)
                    for u in range(2):
                        j = 2 * c + u
                        t = tg + RING + j
                        if u:
                            act.wait_ge(sem("ffn_mul"), done)
                            nc.scalar.activation(AA[:, bass.ds(r * 2 + c, 1), 0].rearrange("p a b -> p (a b)"),
                                                 abuf[:], ACT.Copy).then_inc(sem("ffn_hi"), 1)
                        act.wait_ge(raw_loaded[t % RAW], r * (16 * RING // RAW) + 16 * (t // RAW + 1))
                        act.wait_ge(tile_used, r * RING + (t - RING + 1))
                        nc.scalar.activation(wring[:, t % RING, 0], raw[:, t % RAW], ACT.Copy).then_inc(hi_ready[t % RING], 1)
            td = tg + 2 * KF
            whole = KF // RING - (1 if last else 0)
            with act.Fori(0, whole) as r:
                for j in range(RING):
                    t = td + RING + j
                    act.wait_ge(raw_loaded[t % RAW], r * (16 * RING // RAW) + 16 * (t // RAW + 1))
                    act.wait_ge(tile_used, r * RING + (t - RING + 1))
                    nc.scalar.activation(wring[:, t % RING, 0], raw[:, t % RAW], ACT.Copy).then_inc(hi_ready[t % RING], 1)
            for t in range(td + RING + whole * RING, td + KF + (0 if last else RING)):
                hi(t)

        def token_root(k, cols):
            act.wait_ge(sem("stat_ms"), k)
            nc.scalar.activation(ost[:, 0, 0:cols], ost[:, 0, 0:cols], ACT.Sqrt).then_inc(sem("stat_root"), 1)

        for n in range(KD):
            feed(0, n)
            if n % 2:
                hi(n // 2)
        norm_root(0)
        act.wait_ge(sem("lam_sum"), 1)
        nc.scalar.activation(lam[:, 4:6], PS[:, 6, 0:2], ACT.Exp).then_inc(sem("lam_exp"), 1)
        for e in range(20):
            if e % 2 == 1 and e < 8:
                c = e // 2
                act.wait_ge(evacuated, e + 1)
                nc.scalar.activation(sqb[:, c % 2], sqb[:, c % 2], ACT.Sigmoid).then_inc(sem("gate_sig"), 1)
            hi(e + RING)

        def diff_exp(u):
            h, i = UNITS[u]
            n = (i + 1) * P
            for m in range(2):
                act.wait_ge(sem("diff_max"), 2 * u + m + 1)
                if u >= 2 and m == 0:
                    act.wait_ge(sem("diff_w"), u - 1)
                nc.scalar.activation(pbuf[:, u % 2, m, 0:n], PS[:, 4 + 2 * (u % 2) + m, 0:n], ACT.Exp,
                                     bias=amax[:, u % 2, m:m + 1],
                                     accum_out=asum[:, u % 2, m:m + 1]).then_inc(sem("diff_exp"), 1)

        def wt_copy(u, sem_t, sem_c, dst, bank, sem_pv):
            h, i = UNITS[u]
            act.wait_ge(sem(sem_t), u + 1)
            if h >= 2 and i == 0:
                act.wait_ge(sem(sem_pv), h - 1)
            nc.scalar.activation(dst[:, h % 2, 0:i + 1, blk(i)],
                                 PS[:, bank, 0:(i + 1) * P].rearrange("p (j c) -> p j c", c=P),
                                 ACT.Copy).then_inc(sem(sem_c), 1)

        diff_exp(0)
        for u, (h, i) in enumerate(UNITS):
            if u + 1 < len(UNITS):
                diff_exp(u + 1)
            wt_copy(u, "diff_t", "diff_wt", WT, u % 2, "diff_pv")
            if u == 4:
                for c in range(4):
                    act.wait_ge(sem("ln_centred"), c + 1)
                    nc.scalar.activation(upad[:, c, 0:S], cacc[:, c], ACT.Square).then_inc(sem("ln_sq"), 1)
            if u == 6:
                act.wait_ge(sem("ln_var"), 1)
                nc.scalar.activation(lst[:, 4:8], lst[:, 4:8], ACT.Sqrt).then_inc(sem("ln_root"), 1)
            if i == NB - 1:
                act.wait_ge(sem("diff_pv"), h + 1)
                nc.scalar.activation(oT[:, h], PS[:, 2], ACT.Copy).then_inc(sem("diff_o"), 1)
                nc.scalar.activation(osq[:, h], PS[:, 2], ACT.Square).then_inc(sem("diff_osq"), 1)
        token_root(1, 16)
        for c in range(4):
            act.wait_ge(sem("ln_scaled"), c + 1)
            if c >= 2:
                act.wait_ge(y_ready, c - 1)
            nc.scalar.activation(ytmp[:, c % 2], cacc[:, c], ACT.Silu, bias=vcol(V_LNB + c),
                                 scale=vcol(V_LNW + c)).then_inc(sem("y_tmp"), 1)
            act.wait_ge(sem("y_tmp"), c + 1)
            nc.scalar.activation(AA[:, c, 0], ytmp[:, c % 2], ACT.Copy).then_inc(sem("y_hi"), 1)
        for h in range(H):
            act.wait_ge(sem("y_scaled"), h + 1)
            nc.scalar.activation(AA[:, 4 + h, 0], oT[:, h], ACT.Copy).then_inc(sem("y_hi"), 1)
        for n in range(KD):
            if n < 4:
                hi(T_OUT0 + RING + n)
            feed(1, n)
            if n >= 4:
                hi(T_OUT0 + RING + n)
        norm_root(1)
        ffn(0, T_GU0, E_GU0, False)
        for n in range(KD):
            feed(2, n)
        act.dma_start(wraw[:], wsm_d).then_inc(sem("wraw_loaded"), 16)
        norm_root(2)
        for e in range(28):
            if 8 <= e < 16:
                k = e - 8
                act.wait_ge(sem("tok_t"), k + 1)
                nc.scalar.activation((ktok, vtok)[k // 4][:, :, k % 4], PS[:, 4 + k % 2].rearrange("p (b c) -> p b c", b=NB),
                                     ACT.Copy).then_inc(sem("tok_ready"), 1)
            if e < 12:
                h = e % H
                act.wait_ge(sem("gconv_done"), e + 1)
                if e >= 10:
                    act.wait_ge(sem("tok_t"), e - 5)
                dst = (qT[:, h], kT[:, h], sqb[:, e % 2])[e // 4]
                if e in (8, 9):
                    act.wait_ge(sem("l2_mm"), e - 1)
                nc.scalar.activation(dst, hbuf[:, e % 2], ACT.Silu).then_inc(sem("gsilu"), 1)
                if e < 8:
                    act.wait_ge(sem("gsilu"), e + 1)
                    if e >= 2:
                        act.wait_ge(sem("l2_mm"), e - 1)
                    nc.scalar.activation(sqb[:, e % 2], dst, ACT.Square).then_inc(sem("gsq"), 1)
            if e == 13:
                act.wait_ge(sem("l2_ms"), 1)
                nc.scalar.activation(l2s[:], l2s[:], ACT.Sqrt).then_inc(sem("l2_root"), 1)
            if e >= 24:
                act.wait_ge(evacuated, E_IN1 + e + 1)
                nc.scalar.activation(zT[:, e - 24], zT[:, e - 24], ACT.Silu).then_inc(sem("z_silu"), 1)
            hi(T_IN1 + RING + e)
            if e == 1:
                act.wait_ge(sem("wraw_loaded"), 16)
                nc.scalar.activation(wsm[:, 0], wraw[:], ACT.Copy).then_inc(sem("wsm_hi"), 1)
            if e == 3:
                act.wait_ge(sem("gate_args"), 1)
                nc.scalar.activation(e8[:], e8[:], ACT.Exp).then_inc(sem("gate_exp"), 1)
                nc.scalar.activation(expa[:], srow[:, 0:4], ACT.Exp).then_inc(sem("gate_exp"), 1)
                nc.scalar.activation(beta[:], baf[:, :, 0:4], ACT.Exp, scale=-1.0).then_inc(sem("gate_exp"), 1)
            if e == 4:
                act.wait_ge(sem("gate_one"), 1)
                nc.scalar.activation(e8[:], e8[:], ACT.Ln).then_inc(sem("gate_ln"), 1)
            if e == 7:
                act.wait_ge(sem("g_sums"), 1)
                for n in range(3):
                    nc.scalar.activation(gexp[:, n], gexp[:, n], ACT.Exp).then_inc(sem("g_exp"), 1)
        for i in range(NB):
            act.wait_ge(sem("gdn_bc"), i + 1)
            nc.scalar.activation(eg_b, hd(4), ACT.Exp).then_inc(sem("gdn_eg"), 1)
            act.wait_ge(sem("gdn_darg"), i + 1)
            nc.scalar.activation(decay_b, decay_b, ACT.Exp).then_inc(sem("gdn_dexp"), 1)
            for n, b in enumerate(LEVELS):
                if n:
                    act.wait_ge(sem("gdn_z_mm"), 6 * i + n)
                    nc.scalar.activation(Z_b, hd(4), ACT.Copy).then_inc(sem("gdn_z"), 1)
                if n + 1 < len(LEVELS):
                    act.wait_ge(sem("gdn_t_mm"), 6 * i + n + 1)
                    nc.scalar.activation(T_b, hd(6), ACT.Copy).then_inc(sem("gdn_t"), 1)
            act.wait_ge(sem("gdn_w_mm"), i + 1)
            nc.scalar.activation(wT_b, hd(5), ACT.Copy, scale=-1.0).then_inc(sem("gdn_w"), 1)
            act.wait_ge(sem("gdn_v_mm"), i + 1)
            nc.scalar.activation(vn_b, hd(4), ACT.Copy).then_inc(sem("gdn_v"), 1)
            act.wait_ge(sem("gdn_o_mm"), i + 1)
            nc.scalar.activation(qT[:, :, blk(i)], hd(6), ACT.Copy).then_inc(sem("gdn_o"), 1)
        act.wait_ge(sem("gdn_o"), NB)
        for h in range(H):
            nc.scalar.activation(gsq[:, h], qT[:, h], ACT.Square).then_inc(sem("gdn_osq"), 1)
        token_root(2, 16)
        for h in range(H):
            act.wait_ge(sem("gy_ready"), h + 1)
            nc.scalar.activation(AA[:, h, 0], qT[:, h], ACT.Copy).then_inc(sem("y_hi"), 1)

        def fox_exp(u):
            h, i = UNITS[u]
            n = (i + 1) * P
            act.wait_ge(sem("fox_min"), u + 1)
            if u >= 2:
                act.wait_ge(sem("fox_t"), u - 1)
            nc.scalar.activation(fbuf[:, u % 2, 0:n], tbuf[:, u % 2, 0:n], ACT.Exp, bias=amax[:, 0, u % 2:u % 2 + 1],
                                 scale=-1.0, accum_out=asum[:, 0, u % 2:u % 2 + 1]).then_inc(sem("fox_exp"), 1)

        fox_exp(0)
        for u, (h, i) in enumerate(UNITS):
            if u + 1 < len(UNITS):
                fox_exp(u + 1)
            wt_copy(u, "fox_t", "fox_wt", FT, 6 + u % 2, "fox_pv")
            if i == NB - 1:
                act.wait_ge(sem("fox_pv"), h + 1)
                nc.scalar.activation(AA[:, 4 + h, 0], PS[:, h % 2], ACT.Copy).then_inc(sem("y_hi"), 1)
        for n in range(KD):
            if n < 4:
                hi(T_OUT1 + RING + n)
            feed(3, n)
            if n >= 4:
                hi(T_OUT1 + RING + n)
        norm_root(3)
        ffn(1, T_GU1, E_GU1, True)
        for n in range(KD):
            feed(4, n)
        norm_root(4)

    @block.vector
    def _(dve):
        V = nc.vector
        seq = [0]

        def link(ins):
            seq[0] += 1
            ins.then_inc(dchain, 1)
            dve.wait_ge(dchain, seq[0])

        def feed_mul_(s, n):
            if n >= 2:
                dve.wait_ge(h_ready, KD * s + n - 1)
            V.tensor_scalar(hbuf[:, n % 2], xT[:, n], vcol(V_NORM + KD * s + n), None, ALU.mult).then_inc(feed_mul, 1)

        def feed_lo(s, n):
            dve.wait_ge(feed_hi, KD * s + n + 1)
            V.tensor_tensor(HH[:, n, 1], hbuf[:, n % 2], HH[:, n, 0].bitcast(f32), ALU.subtract).then_inc(h_ready, 1)

        def norm_finish(s, bank):
            dve.wait_ge(norm_sum, s + 1)
            V.tensor_scalar(nst[:], PS[:, bank, 0:NB], 1.0 / D, 1e-6, ALU.mult, ALU.add).then_inc(norm_ms, 1)
            dve.wait_ge(norm_sqrt, s + 1)
            V.reciprocal(rtok[:], nst[:]).then_inc(norm_tok, 1)
            dve.wait_ge(norm_bc, s + 1)
            V.tensor_copy(rstd[:], PS[:, bank]).then_inc(norm_rstd, 1)
            dve.wait_ge(norm_rstd, s + 1)

        def residual(n, e, bank):
            V.tensor_tensor(xT[:, n], xT[:, n], PS[:, bank], ALU.add).then_inc(evacuated, 1)
            dve.wait_ge(evacuated, e + 1)

        def ffn(s, tg, eg, last):
            with dve.Fori(0, KF // 2) as r:
                for c in range(2):
                    cnt = r * 2 + (KF * s + c + 1)
                    for u, buf in enumerate((gbuf, ubuf)):
                        dve.wait_ge(tile_used, r * RING + (tg + 2 * c + u + 1))
                        V.tensor_tensor(buf[:, c], PS[:, 2 * c + u], rstd[:], ALU.mult).then_inc(evacuated, 1)
                    dve.wait_ge(evacuated, r * RING + (eg + 2 * c + 2))
                    for u in range(2):
                        j = 2 * c + u
                        t = tg + RING + j
                        if u == 0:
                            dve.wait_ge(sem("gate_silu"), cnt)
                            V.tensor_tensor(abuf[:], gbuf[:, c], ubuf[:, c], ALU.mult).then_inc(sem("ffn_mul"), 1)
                        dve.wait_ge(hi_ready[t % RING], r + slot_round(t))
                        V.tensor_tensor(wring[:, t % RING, 1], raw[:, t % RAW], wring[:, t % RING, 0].bitcast(f32),
                                        ALU.subtract).then_inc(lo_ready[t % RING], 1)
                        if u == 0:
                            dve.wait_ge(sem("ffn_hi"), cnt)
                            V.tensor_tensor(AA[:, bass.ds(r * 2 + c, 1), 1].rearrange("p a b -> p (a b)"), abuf[:],
                                            AA[:, bass.ds(r * 2 + c, 1), 0].rearrange("p a b -> p (a b)").bitcast(f32),
                                            ALU.subtract).then_inc(sem("ffn_lo"), 1)
            td = tg + 2 * KF
            whole = KF // RING - (1 if last else 0)
            with dve.Fori(0, whole) as r:
                for j in range(RING):
                    t = td + RING + j
                    dve.wait_ge(hi_ready[t % RING], r + slot_round(t))
                    V.tensor_tensor(wring[:, t % RING, 1], raw[:, t % RAW], wring[:, t % RING, 0].bitcast(f32),
                                    ALU.subtract).then_inc(lo_ready[t % RING], 1)
            for t in range(td + RING + whole * RING, td + KF + (0 if last else RING)):
                lo(t)

        def lo(t):
            dve.wait_ge(hi_ready[t % RING], slot_round(t))
            V.tensor_tensor(wring[:, t % RING, 1], raw[:, t % RAW], wring[:, t % RING, 0].bitcast(f32),
                            ALU.subtract).then_inc(lo_ready[t % RING], 1)

        def down(s, td, e0):
            for n in range(KD):
                if n < KD - 1:
                    dve.wait_ge(down_done, (s // 2 - 1) * (KD - 1) + n + 1)
                else:
                    dve.wait_ge(tile_used, td + KF)
                residual(n, e0 + n, n)
                if s < FINAL:
                    feed_mul_(s, n)
                    if n:
                        feed_lo(s, n - 1)
            if s < FINAL:
                feed_lo(s, KD - 1)

        def out_proj(s, t0, e0):
            for n in range(KD):
                dve.wait_ge(tile_used, t0 + n + 1)
                residual(n, e0 + n, (e0 + n) % 4)
                feed_mul_(s, n)
                if n:
                    feed_lo(s, n - 1)
                if n >= 5:
                    lo(t0 + RING + n - 1)
            feed_lo(s, KD - 1)
            lo(t0 + RING + KD - 1)

        dve.wait_ge(vec_loaded, 16)
        for n in range(KD):
            dve.wait_ge(x_loaded[n // 2], 16)
            feed_mul_(0, n)
            if n:
                feed_lo(0, n - 1)
        feed_lo(0, KD - 1)
        V.tensor_tensor(lam[0:64, 0:1], vec[0:64, V_LAM:V_LAM + 1], vec[0:64, V_LAM + 1:V_LAM + 2], ALU.mult).then_inc(sem("lam_prod"), 1)
        V.tensor_tensor(lam[0:64, 1:2], vec[0:64, V_LAM + 2:V_LAM + 3], vec[0:64, V_LAM + 3:V_LAM + 4], ALU.mult).then_inc(sem("lam_prod"), 1)
        norm_finish(0, 7)
        dve.wait_ge(sem("lam_exp"), 1)
        link(V.tensor_tensor(lam[:, 6:7], lam[:, 5:6], lam[:, 4:5], ALU.subtract))
        link(V.tensor_scalar(lam[:, 7:8], lam[:, 6:7], -LAMBDA_INIT, None, ALU.add))
        def taps():
            for c in range(4):
                link(V.tensor_scalar(cacc[:, c], upad[:, c, 0:S], vcol(V_CONVW + TAPS * c), vcol(V_CONVB + c), ALU.mult, ALU.add))
                yield
                for k in range(1, TAPS):
                    ins = V.scalar_tensor_tensor(cacc[:, c], upad[:, c, k:k + S], vcol(V_CONVW + TAPS * c + k), cacc[:, c],
                                                 ALU.mult, ALU.add)
                    if k < TAPS - 1:
                        link(ins)
                    else:
                        ins.then_inc(sem("conv_done"), 1)
                        dve.wait_ge(sem("conv_done"), c + 1)
                    yield

        conv = taps()

        def pump(n):
            for _ in range(n):
                next(conv, None)

        def evac(e, t):
            dve.wait_ge(tile_used, t + 1)

        def rope_finish(j):
            dve.wait_ge(sem("rope_mm"), j + 1)
            src = hbuf[:, j % 2]
            V.tensor_tensor(qk[:, j], src, rope[:, 0:S], ALU.mult).then_inc(sem("rope_cos"), 1)
            V.tensor_tensor(sqb[:, j % 2], PS[:, 4 + j % 2], rope[:, S:2 * S], ALU.mult).then_inc(sem("rope_sin"), 1)
            dve.wait_ge(sem("rope_sin"), j + 1)
            V.tensor_tensor(qk[:, j], qk[:, j], sqb[:, j % 2], ALU.add).then_inc(sem("qk_ready"), 1)

        dve.wait_ge(sem("pad_zero"), 1)
        dve.wait_ge(rope_loaded, 16)
        for c in range(4):
            evac(2 * c, 2 * c)
            V.tensor_tensor(hbuf[:, c % 2], PS[:, (2 * c) % 4], rstd[:], ALU.mult).then_inc(evacuated, 1)
            evac(2 * c + 1, 2 * c + 1)
            V.tensor_tensor(sqb[:, c % 2], PS[:, (2 * c + 1) % 4], rstd[:], ALU.mult).then_inc(evacuated, 1)
            pump(6 if c else 0)
            dve.wait_ge(sem("gate_sig"), c + 1)
            link(V.tensor_tensor(upad[:, c, TAPS - 1:], hbuf[:, c % 2], sqb[:, c % 2], ALU.mult))
            pump(6)
        for j in range(8):
            e = 8 + j
            evac(e, e)
            V.scalar_tensor_tensor(hbuf[:, j % 2], PS[:, e % 4], SC_DIFF if j < 4 else 1.0, rstd[:], ALU.mult, ALU.mult).then_inc(evacuated, 1)
            pump(5)
            if j:
                rope_finish(j - 1)
        rope_finish(7)
        evac(19, 19)
        for b in range(NB):
            V.tensor_scalar(vtk[:, b], PS[:, b], rtok[:, b:b + 1], None, ALU.mult).then_inc(evacuated, 1)
        pump(10000)

        def diff_max(u):
            h, i = UNITS[u]
            n = (i + 1) * P
            dve.wait_ge(sem("diff_s"), u + 1)
            for m in range(2):
                V.tensor_reduce(amax[:, u % 2, m:m + 1], PS[:, 4 + 2 * (u % 2) + m, 0:n], AX.X, ALU.max,
                                negate=True).then_inc(sem("diff_max"), 1)

        def diff_combine(u):
            h, i = UNITS[u]
            n = (i + 1) * P
            dve.wait_ge(sem("diff_exp"), 2 * u + 2)
            link(V.reciprocal(arec[:, u % 2], asum[:, u % 2]))
            link(V.tensor_scalar(arec[:, u % 2, 1:2], arec[:, u % 2, 1:2], lam[:, 7:8], None, ALU.mult))
            link(V.tensor_scalar(pbuf[:, u % 2, 0, 0:n], pbuf[:, u % 2, 0, 0:n], arec[:, u % 2, 0:1], None, ALU.mult))
            if u >= 2:
                dve.wait_ge(sem("diff_t"), u - 1)
            V.scalar_tensor_tensor(wbuf[:, u % 2, 0:n], pbuf[:, u % 2, 1, 0:n], arec[:, u % 2, 1:2],
                                   pbuf[:, u % 2, 0, 0:n], ALU.mult, ALU.add).then_inc(sem("diff_w"), 1)

        diff_max(0)
        for u in range(len(UNITS)):
            if u + 1 < len(UNITS):
                diff_max(u + 1)
            diff_combine(u)
            if u == 1:
                dve.wait_ge(sem("ln_mean_mm"), 1)
                V.tensor_scalar(lst[:, 0:4], PS[:, 3, 0:4], 1.0 / 512, None, ALU.mult).then_inc(sem("ln_mean"), 1)
            if u == 3:
                dve.wait_ge(sem("ln_mean_bc"), 1)
                for c in range(4):
                    V.tensor_tensor(cacc[:, c], cacc[:, c], PS[:, 3], ALU.subtract).then_inc(sem("ln_centred"), 1)
            if u == 5:
                dve.wait_ge(sem("ln_var_mm"), 1)
                V.tensor_scalar(lst[:, 4:8], PS[:, 3, 0:4], 1.0 / 512, 1e-5, ALU.mult, ALU.add).then_inc(sem("ln_var"), 1)
            if u == 7:
                dve.wait_ge(sem("ln_root"), 1)
                V.reciprocal(lst[:, 4:8], lst[:, 4:8]).then_inc(sem("ln_rstd"), 1)
            if u == 9:
                dve.wait_ge(sem("ln_rstd_bc"), 1)
                for c in range(4):
                    V.tensor_tensor(cacc[:, c], cacc[:, c], PS[:, 3], ALU.mult).then_inc(sem("ln_scaled"), 1)

        def y_lo(k, chunk, src):
            dve.wait_ge(sem("y_hi"), k)
            V.tensor_tensor(AA[:, chunk, 1], src, AA[:, chunk, 0].bitcast(f32), ALU.subtract).then_inc(y_ready, 1)

        def token_stat(k, bank, scale, eps):
            dve.wait_ge(sem("stat_mm"), k)
            V.tensor_scalar(ost[:, 0], PS[:, bank, 0:16], scale, eps, ALU.mult, ALU.add).then_inc(sem("stat_ms"), 1)
            dve.wait_ge(sem("stat_root"), k)
            V.reciprocal(ost[:, 1], ost[:, 0]).then_inc(sem("stat_rec"), 1)

        token_stat(1, 3, 1.0 / P, 1e-6)
        link(V.tensor_scalar(arec[:, 0, 0:1], vcol(V_SUBLN), 1.0 - LAMBDA_INIT, None, ALU.mult))
        for c in range(4):
            y_lo(c + 1, c, ytmp[:, c % 2])
        for h in range(H):
            dve.wait_ge(sem("stat_bc"), h + 1)
            V.scalar_tensor_tensor(oT[:, h], oT[:, h], arec[:, 0, 0:1], PS[:, 4 + h], ALU.mult, ALU.mult).then_inc(sem("y_scaled"), 1)
        for h in range(H):
            y_lo(5 + h, 4 + h, oT[:, h])
        out_proj(1, T_OUT0, E_OUT0)
        norm_finish(1, 7)
        ffn(0, T_GU0, E_GU0, False)
        down(2, T_DN0, E_DN0)

        norm_finish(2, 7)

        def gates_1():
            dve.wait_ge(sem("baf_mm"), 1)
            V.tensor_copy(srow[:], PS[:, 6, 64:76]).then_inc(sem("gate_tmp"), 1)
            for b in range(NB):
                V.tensor_scalar(baf[:, b], PS[:, 6, 12 * b:12 * b + 12], rtok[:, b:b + 1], None, ALU.mult).then_inc(sem("gate_tmp"), 1)
            dve.wait_ge(sem("gate_tmp"), 5)
            V.tensor_tensor(z8[:, :, 0:4], baf[:, :, 4:8], srow[:, 4:8].unsqueeze(1).broadcast_to([P, NB, 4]), ALU.add)
            link(V.scalar_tensor_tensor(z8[:, :, 4:8], baf[:, :, 8:12], -1.0, srow[:, 8:12].unsqueeze(1).broadcast_to([P, NB, 4]),
                                        ALU.mult, ALU.subtract))
            V.scalar_tensor_tensor(e8[:], z8[:], -1.0, z8[:], ALU.mult, ALU.min).then_inc(sem("gate_args"), 1)

        def gates_2():
            dve.wait_ge(sem("gate_exp"), 3)
            V.tensor_scalar(e8[:], e8[:], 1.0, None, ALU.add).then_inc(sem("gate_one"), 1)
            link(V.tensor_scalar(beta[:], beta[:], 1.0, None, ALU.add))
            link(V.reciprocal(beta[:], beta[:]))
            dve.wait_ge(sem("gate_ln"), 1)
            link(V.scalar_tensor_tensor(sp8[:], z8[:], 0.0, e8[:], ALU.max, ALU.add))
            link(V.scalar_tensor_tensor(gtok[:], sp8[:, :, 0:4], -1.0, expa[:].unsqueeze(1).broadcast_to([P, NB, 4]),
                                        ALU.mult, ALU.mult))
            V.tensor_scalar(lftok[:], sp8[:, :, 4:8], -1.0, None, ALU.mult).then_inc(sem("g_ready"), 1)

        def gates_3():
            dve.wait_ge(sem("g_mm"), 1)
            link(V.tensor_copy(gcum[:].rearrange("p a b c -> p (a b c)"), PS[:, 6, 0:48]))
            V.tensor_tensor(gexp[:, 1], gcum[:, 1], gcum[:, 0], ALU.subtract)
            V.tensor_copy(gexp[:, 0], gcum[:, 0])
            V.tensor_copy(gexp[:, 2], gcum[:, 1]).then_inc(sem("g_sums"), 1)

        dve.wait_ge(sem("cin_zero"), 1)
        for e in range(12):
            bank = e % 4
            dve.wait_ge(tile_used, T_IN1 + e + 1)
            if e:
                dve.wait_ge(sem("gconv_done"), e)
            V.tensor_tensor(cin[:, GTAPS - 1:], PS[:, bank], rstd[:], ALU.mult).then_inc(evacuated, 1)
            dve.wait_ge(evacuated, E_IN1 + e + 1)
            if e >= 2:
                dve.wait_ge(sem("gsilu"), e - 1)
            link(V.tensor_scalar(hbuf[:, e % 2], cin[:, 0:S], vcol(V_GCONV + GTAPS * e), None, ALU.mult))
            for k in range(1, GTAPS):
                ins = V.scalar_tensor_tensor(hbuf[:, e % 2], cin[:, k:k + S], vcol(V_GCONV + GTAPS * e + k), hbuf[:, e % 2],
                                             ALU.mult, ALU.add)
                if k < GTAPS - 1:
                    link(ins)
                else:
                    ins.then_inc(sem("gconv_done"), 1)
            if e == 2:
                dve.wait_ge(sem("wsm_hi"), 1)
                V.tensor_tensor(wsm[:, 1], wraw[:], wsm[:, 0].bitcast(f32), ALU.subtract).then_inc(sem("wsm_lo"), 1)
            if e == 3:
                gates_1()
            if e == 4:
                gates_2()
            if e == 7:
                gates_3()
        for e in range(12, 28):
            bank = e % 4
            if e < 20:
                dve.wait_ge(tile_used, T_IN1 + e + 1)
                dst = qd[:, e - 12] if e < 16 else kd[:, e - 16]
                V.scalar_tensor_tensor(dst, PS[:, bank], SC_FOX if e < 16 else 1.0, rstd[:], ALU.mult, ALU.mult).then_inc(evacuated, 1)
            elif e < 24:
                dve.wait_ge(tile_used, T_IN1 + 24)
                V.tensor_scalar(vd[:, e - 20], PS[:, bank], rtok[:, e - 20:e - 19], None, ALU.mult).then_inc(evacuated, 1)
            else:
                dve.wait_ge(tile_used, T_IN1 + e + 1)
                V.tensor_tensor(zT[:, e - 24], PS[:, bank], rstd[:], ALU.mult).then_inc(evacuated, 1)
            if e == 13:
                dve.wait_ge(sem("l2_mm"), 8)
                V.tensor_scalar(l2s[:].rearrange("p a b -> p (a b)"), PS[:, 7, 0:32], 1e-6, None, ALU.add).then_inc(sem("l2_ms"), 1)
                dve.wait_ge(sem("l2_root"), 1)
                link(V.reciprocal(l2s[:], l2s[:]))
                dve.wait_ge(sem("g_exp"), 3)
                link(V.tensor_scalar(qscal[:], l2s[:, :, 0:4], SC_FOX, None, ALU.mult))
                link(V.tensor_tensor(kscal[:, 0], l2s[:, :, 4:8], beta[:], ALU.mult))
                link(V.tensor_tensor(kscal[:, 1], kscal[:, 0], gexp[:, 0], ALU.mult))
                V.tensor_tensor(kscal[:, 2], l2s[:, :, 4:8], gexp[:, 1], ALU.mult).then_inc(sem("gdn_scalars"), 1)
        dve.wait_ge(sem("state_zero"), 1)
        for i in range(NB):
            dve.wait_ge(sem("gdn_bc"), i + 1)
            V.tensor_tensor(kbT_b, kT[:, :, blk(i)], hd(5), ALU.mult).then_inc(sem("gdn_kb"), 1)
            V.tensor_tensor(qT[:, :, blk(i)], qT[:, :, blk(i)], hd(7), ALU.mult).then_inc(sem("gdn_qn"), 1)
            dve.wait_ge(sem("gdn_eg"), i + 1)
            link(V.tensor_tensor(decay_b, hd(4), per_head(gcum[:, 0, i]), ALU.subtract))
            V.scalar_tensor_tensor(decay_b, decay_b, 0.0, over_heads(dmask), ALU.min, ALU.add).then_inc(sem("gdn_darg"), 1)
            dve.wait_ge(sem("gdn_qn"), i + 1)
            V.tensor_tensor(qe_b, qT[:, :, blk(i)], eg_b, ALU.mult).then_inc(sem("gdn_q"), 1)
            dve.wait_ge(sem("gdn_dexp"), i + 1)
            link(V.tensor_tensor(decay_b, decay_b, per_head(l2s[:, i, 4:8]), ALU.mult))
            dve.wait_ge(sem("gdn_a_mm"), i + 1)
            link(V.scalar_tensor_tensor(NT_b, hd(4), -1.0, decay_b, ALU.mult, ALU.mult))
            V.tensor_tensor(qkT_b, hd(5), decay_b, ALU.mult).then_inc(sem("gdn_qk"), 1)
            link(V.tensor_copy(R_b, over_heads(ident)))
            for n, b in enumerate(LEVELS):
                data = NT_b
                if n:
                    dve.wait_ge(sem("gdn_r_mm"), 6 * i + n)
                    data = hd(5)
                V.copy_predicated(R_b, over_heads(lmask[b]), data).then_inc(sem("gdn_r"), 1)
            dve.wait_ge(sem("gdn_state_mm"), i + 1)
            dve.wait_ge(sem("gdn_o_mm"), i + 1)
            link(V.tensor_tensor(St_b, St_b, per_head(gexp[:, 2, i]), ALU.mult))
            V.tensor_tensor(St_b, St_b, hd(7), ALU.add).then_inc(sem("gdn_state"), 1)
        token_stat(2, 4, 1.0 / P, 1e-6)
        for h in range(H):
            dve.wait_ge(sem("stat_bc"), 4 + h + 1)
            link(V.scalar_tensor_tensor(qT[:, h], qT[:, h], vcol(V_GNORM), PS[:, h], ALU.mult, ALU.mult))
            dve.wait_ge(sem("z_silu"), h + 1)
            V.tensor_tensor(qT[:, h], qT[:, h], zT[:, h], ALU.mult).then_inc(sem("gy_ready"), 1)
        for h in range(H):
            y_lo(8 + h + 1, h, qT[:, h])
        for h in range(H):
            dve.wait_ge(sem("fox_cb_mm"), h + 1)
            V.tensor_copy(cb[:, h], PS[:, h]).then_inc(sem("fox_cb"), 1)

        def fox_min(u):
            h, i = UNITS[u]
            n = (i + 1) * P
            dve.wait_ge(sem("fox_s"), u + 1)
            if u >= 2:
                dve.wait_ge(sem("fox_exp"), u - 1)
            link(V.scalar_tensor_tensor(tbuf[:, u % 2, 0:n], cb[:, h, 0:n], gcum[:, 2, i, h:h + 1], PS[:, 4 + u % 2, 0:n],
                                        ALU.subtract, ALU.subtract))
            V.tensor_reduce(amax[:, 0, u % 2:u % 2 + 1], tbuf[:, u % 2, 0:n], AX.X, ALU.min).then_inc(sem("fox_min"), 1)

        def fox_scale(u):
            h, i = UNITS[u]
            n = (i + 1) * P
            dve.wait_ge(sem("fox_exp"), u + 1)
            link(V.reciprocal(arec[:, 0, u % 2:u % 2 + 1], asum[:, 0, u % 2:u % 2 + 1]))
            V.tensor_scalar(fbuf[:, u % 2, 0:n], fbuf[:, u % 2, 0:n], arec[:, 0, u % 2:u % 2 + 1], None, ALU.mult).then_inc(sem("fox_p"), 1)

        dve.wait_ge(sem("fox_cb"), H)
        fox_min(0)
        for u, (h, i) in enumerate(UNITS):
            if u + 1 < len(UNITS):
                fox_min(u + 1)
            fox_scale(u)
            if i == NB - 1:
                y_lo(12 + h + 1, 4 + h, PS[:, h % 2])
        out_proj(3, T_OUT1, E_OUT1)
        norm_finish(3, 7)
        ffn(1, T_GU1, E_GU1, True)
        down(4, T_DN1, E_DN1)
        norm_finish(4, 7)
        for n in range(KD):
            V.scalar_tensor_tensor(outT[:, n], xT[:, n], vcol(V_NORM + KD * FINAL + n), rstd[:], ALU.mult, ALU.mult).then_inc(sem("out_ready"), 1)

    @block.tensor
    def _(pe):
        def mm(out, lhsT, rhs, start=True, stop=True):
            return nc.tensor.matmul(out, lhsT, rhs, start=start, stop=stop)

        def product(out, w, x, start, stop):
            mm(out, w[0], x[0], start, False)
            mm(out, w[0], x[1], False, False)
            return mm(out, w[1], x[0], False, stop)

        def wpair(slot, cols):
            return wring[:, slot, 0, cols], wring[:, slot, 1, cols]

        def arrived(t):
            pe.wait_ge(hi_ready[t % RING], slot_round(t))
            pe.wait_ge(lo_ready[t % RING], slot_round(t))

        def stationary(t, e, src, feed=None):
            arrived(t)
            if e >= 4:
                pe.wait_ge(evacuated, e - 3)
            for k in range(KD):
                if feed is not None:
                    pe.wait_ge(h_ready, feed + k + 1)
                last = product(PS[:, e % 4], wpair(t % RING, blk(k)), (src[:, k, 0], src[:, k, 1]), k == 0, k == KD - 1)
            last.then_inc(tile_used, 1)

        def moving(t0, e0):
            for j in range(4):
                arrived(t0 + j)
                for m in range(2):
                    k = 2 * j + m
                    w = wpair((t0 + j) % RING, slice(m * S, (m + 1) * S))
                    for b in range(NB):
                        if k == 0:
                            pe.wait_ge(evacuated, e0 + b - 3)
                        last = product(PS[:, (e0 + b) % 4], (HH[:, k, 0, blk(b)], HH[:, k, 1, blk(b)]), w, k == 0, k == KD - 1)
                last.then_inc(tile_used, 1)

        def token_sum(out, src, k=0, n=1):
            return mm(out, src, ones[:, 0:1], k == 0, k == n - 1)

        def spread(out, col):
            return mm(out, col.to_broadcast([P, P]), ident)

        def norm_stats(s, bank):
            pe.wait_ge(ssq_done, 7 * (s + 1))
            for b in range(NB):
                last = token_sum(PS[:, bank, b:b + 1], ssq[:, blk(b)])
            last.then_inc(norm_sum, 1)

        def norm_spread(s, bank):
            pe.wait_ge(norm_tok, s + 1)
            for b in range(NB):
                last = spread(PS[:, bank, blk(b)], rtok[:, b:b + 1])
            last.then_inc(norm_bc, 1)

        pe.wait_ge(const_loaded, 16)
        for e in range(16):
            if e == 2:
                norm_stats(0, 7)
                pe.wait_ge(sem("lam_prod"), 2)
                mm(PS[:, 6, 0:2], ones[0:64, :], lam[0:64, 0:2]).then_inc(sem("lam_sum"), 1)
            if e == 3:
                norm_spread(0, 7)
            stationary(T_IN0 + e, E_IN0 + e, HH, feed=0 if e == 0 else None)

            def rope_mm(j):
                pe.wait_ge(rope_loaded, 16)
                pe.wait_ge(evacuated, 8 + j + 1)
                if j >= 2:
                    pe.wait_ge(sem("rope_sin"), j - 1)
                mm(PS[:, 4 + j % 2], rope[:, 2 * S:], hbuf[:, j % 2]).then_inc(sem("rope_mm"), 1)

            if e >= 9:
                rope_mm(e - 9)
        rope_mm(7)
        moving(T_IN0 + 16, E_IN0 + 16)

        def diff_scores(u):
            h, i = UNITS[u]
            n = (i + 1) * P
            if u >= 2:
                pe.wait_ge(sem("diff_exp"), 2 * (u - 1))
            for m in range(2):
                bank = 4 + 2 * (u % 2) + m
                part = slice(64 * m, 64 * m + 64)
                mm(PS[:, bank, 0:n], qk[part, h, blk(i)], qk[part, 4 + h, 0:n], True, False)
            for m in range(2):
                bank = 4 + 2 * (u % 2) + m
                last = mm(PS[:, bank, blk(i)], ident, cmask, False, True)
            last.then_inc(sem("diff_s"), 1)

        def transpose_w(u, src, bank):
            h, i = UNITS[u]
            for j in range(i + 1):
                last = nc.tensor.transpose(PS[:, bank, blk(j)], src[:, u % 2, blk(j)], ident)
            return last

        def weighted_values(h, wt, v, bank):
            for j in range(NB):
                last = mm(PS[:, bank, j * P:S], v[:, j, blk(h)], wt[:, h % 2, j, j * P:S], j == 0, j == NB - 1)
            return last

        pe.wait_ge(sem("qk_ready"), 8)
        pe.wait_ge(evacuated, 20)
        diff_scores(0)
        for u, (h, i) in enumerate(UNITS):
            if u + 1 < len(UNITS):
                diff_scores(u + 1)
            if u == 1:
                pe.wait_ge(sem("conv_done"), 4)
                for b in range(NB):
                    for c in range(4):
                        last = token_sum(PS[:, 3, b:b + 1], cacc[:, c, blk(b)], c, 4)
                last.then_inc(sem("ln_mean_mm"), 1)
            if u == 3:
                pe.wait_ge(sem("ln_mean"), 1)
                for b in range(NB):
                    last = spread(PS[:, 3, blk(b)], lst[:, b:b + 1])
                last.then_inc(sem("ln_mean_bc"), 1)
            if u == 5:
                pe.wait_ge(sem("ln_sq"), 4)
                for b in range(NB):
                    for c in range(4):
                        last = token_sum(PS[:, 3, b:b + 1], upad[:, c, blk(b)], c, 4)
                last.then_inc(sem("ln_var_mm"), 1)
            if u == 8:
                pe.wait_ge(sem("ln_rstd"), 1)
                for b in range(NB):
                    last = spread(PS[:, 3, blk(b)], lst[:, 4 + b:5 + b])
                last.then_inc(sem("ln_rstd_bc"), 1)
            pe.wait_ge(sem("diff_w"), u + 1)
            if u >= 2:
                pe.wait_ge(sem("diff_wt"), u - 1)
            transpose_w(u, wbuf, u % 2).then_inc(sem("diff_t"), 1)
            if i == NB - 1:
                pe.wait_ge(sem("diff_wt"), u + 1)
                if h:
                    pe.wait_ge(sem("diff_osq"), h)
                weighted_values(h, WT, vtk, 2).then_inc(sem("diff_pv"), 1)
        pe.wait_ge(sem("diff_osq"), H)
        pe.wait_ge(sem("ln_scaled"), 4)
        for b in range(NB):
            for h in range(H):
                last = token_sum(PS[:, 3, 4 * h + b:4 * h + b + 1], osq[:, h, blk(b)])
        last.then_inc(sem("stat_mm"), 1)
        pe.wait_ge(sem("stat_rec"), 1)
        for h in range(H):
            for b in range(NB):
                last = spread(PS[:, 4 + h, blk(b)], ost[:, 1, 4 * h + b:4 * h + b + 1])
            last.then_inc(sem("stat_bc"), 1)
        pe.wait_ge(y_ready, KD)
        for n in range(KD):
            stationary(T_OUT0 + n, E_OUT0 + n, AA)

        def ffn(s, tg, eg, norm):
            norm_stats(norm, 7)
            norm_spread(norm, 7)
            pe.wait_ge(h_ready, KD * (norm + 1))
            with pe.Fori(0, KF // 2) as r:
                for j in range(RING):
                    t = tg + j
                    slot = t % RING
                    pe.wait_ge(hi_ready[slot], r + slot_round(t))
                    pe.wait_ge(lo_ready[slot], r + slot_round(t))
                    pe.wait_ge(evacuated, r * RING + (eg + j - 3))
                    for k in range(KD):
                        last = product(PS[:, j], wpair(slot, blk(k)), (HH[:, k, 0], HH[:, k, 1]), k == 0, k == KD - 1)
                    last.then_inc(tile_used, 1)
            td = tg + 2 * KF
            pe.wait_ge(evacuated, eg + 2 * KF)
            for k in range(RING):
                arrived(td + k)
                pe.wait_ge(sem("ffn_lo"), KF * s + k + 1)
                for n in range(KD):
                    last = product(PS[:, n], wpair((td + k) % RING, blk(n)), (AA[:, k, 0], AA[:, k, 1]), k == 0, False)
                last.then_inc(tile_used, 1)
            with pe.Fori(1, KF // RING) as r:
                for j in range(RING):
                    t = td + j
                    pe.wait_ge(hi_ready[t % RING], r + slot_round(t))
                    pe.wait_ge(lo_ready[t % RING], r + slot_round(t))
                    pe.wait_ge(sem("ffn_lo"), r * RING + (KF * s + j + 1))
                    a = [AA[:, bass.ds(r * RING + j, 1), m].rearrange("p a b -> p (a b)") for m in range(2)]
                    for n in range(KD):
                        last = product(PS[:, n], wpair(t % RING, blk(n)), a, False, False)
                    last.then_inc(tile_used, 1)
            rest = range(KF // RING * RING, KF)
            for k in rest:
                arrived(td + k)
            pe.wait_ge(sem("ffn_lo"), KF * (s + 1))
            for n in range(KD):
                for k in rest:
                    last = product(PS[:, n], wpair((td + k) % RING, blk(n)), (AA[:, k, 0], AA[:, k, 1]), False, k == KF - 1)
                    if n == KD - 1:
                        last.then_inc(tile_used, 1)
                if n < KD - 1:
                    last.then_inc(down_done, 1)

        ffn(0, T_GU0, E_GU0, 1)

        for e in range(28):
            if e == 2:
                norm_stats(2, 7)
            if e == 3:
                norm_spread(2, 7)
            if 20 <= e < 24:
                if e == 20:
                    moving(T_IN1 + 20, E_IN1 + 20)
                continue
            stationary(T_IN1 + e, E_IN1 + e, HH, feed=2 * KD if e == 0 else None)
            if e == 3:
                pe.wait_ge(sem("wsm_lo"), 1)
                pe.wait_ge(small_loaded, 16)
                mm(PS[:, 6, 64:76], ones[0:1, :], rowv[0:1, :])
                for b in range(NB):
                    for k in range(KD):
                        w = wsm[:, 0, 12 * k:12 * k + 12], wsm[:, 1, 12 * k:12 * k + 12]
                        last = product(PS[:, 6, 12 * b:12 * b + 12], (HH[:, k, 0, blk(b)], HH[:, k, 1, blk(b)]), w, k == 0, k == KD - 1)
                last.then_inc(sem("baf_mm"), 1)
            if 4 <= e < 12:
                c = e - 4
                pe.wait_ge(sem("gsq"), c + 1)
                for b in range(NB):
                    last = token_sum(PS[:, 7, 8 * b + c:8 * b + c + 1], sqb[:, c % 2, blk(b)])
                last.then_inc(sem("l2_mm"), 1)
            if 8 <= e < 16:
                m = e - 8
                pe.wait_ge(sem("gsilu"), m + 5)
                if m >= 2:
                    pe.wait_ge(sem("tok_ready"), m - 1)
                src = kT[:, m] if m < H else sqb[:, m % 2]
                for b in range(NB):
                    last = nc.tensor.transpose(PS[:, 4 + m % 2, blk(b)], src[:, blk(b)], ident)
                last.then_inc(sem("tok_t"), 1)
            if e == 7:
                pe.wait_ge(sem("g_ready"), 1)
                g_all = gtok[:].rearrange("p a b -> p (a b)")
                mm(PS[:, 6, 0:16], cums, g_all)
                mm(PS[:, 6, 16:32], ones, g_all)
                for b in range(NB):
                    for j in range(b + 1):
                        last = mm(PS[:, 6, 32 + 4 * b:36 + 4 * b], cums if j == b else ones, lftok[:, j], j == 0, j == b)
                last.then_inc(sem("g_mm"), 1)

        def heads(out_bank, lhs, rhs):
            for h in range(H):
                last = mm(PS[:, out_bank, blk(h)], lhs(h), rhs(h))
            return last

        pe.wait_ge(sem("gdn_scalars"), 1)
        pe.wait_ge(sem("tok_ready"), 8)
        for i in range(NB):
            if i:
                pe.wait_ge(sem("gdn_state"), i)
                pe.wait_ge(sem("gdn_o"), i)
            for h in range(H):
                spread(PS[:, 4, blk(h)], gcum[:, 0, i, h:h + 1])
                spread(PS[:, 5, blk(h)], kscal[:, 0, i, h:h + 1])
                last = spread(PS[:, 7, blk(h)], qscal[:, i, h:h + 1])
            last.then_inc(sem("gdn_bc"), 1)
            pe.wait_ge(sem("gdn_q"), i + 1)
            heads(4, lambda h: kT[:, h, blk(i)], lambda h: kbT_b[:, h])
            heads(5, lambda h: kT[:, h, blk(i)], lambda h: qT[:, h, blk(i)]).then_inc(sem("gdn_a_mm"), 1)
            for n in range(len(LEVELS)):
                if n:
                    pe.wait_ge(sem("gdn_t"), 6 * i + n)
                    if n == 1:
                        pe.wait_ge(sem("gdn_qk"), i + 1)
                    heads(4, lambda h: NT_b[:, h], lambda h: T_b[:, h]).then_inc(sem("gdn_z_mm"), 1)
                    pe.wait_ge(sem("gdn_z"), 6 * i + n)
                    heads(5, lambda h: Z_b[:, h], lambda h: R_b[:, h]).then_inc(sem("gdn_r_mm"), 1)
                if n + 1 < len(LEVELS):
                    pe.wait_ge(sem("gdn_r"), 7 * i + n + 1)
                    for h in range(H):
                        last = nc.tensor.transpose(PS[:, 6, blk(h)], R_b[:, h], ident)
                    last.then_inc(sem("gdn_t_mm"), 1)
            pe.wait_ge(sem("gdn_r"), 7 * i + 7)
            pe.wait_ge(sem("kbe_ready"), i + 1)
            heads(5, lambda h: kbe_b[:, h], lambda h: R_b[:, h]).then_inc(sem("gdn_w_mm"), 1)
            pe.wait_ge(sem("vb_ready"), i + 1)
            pe.wait_ge(sem("gdn_w"), i + 1)
            pe.wait_ge(sem("state_zero"), 1)
            for h in range(H):
                mm(PS[:, 4, blk(h)], R_b[:, h], vtok[:, i, h], True, False)
                last = mm(PS[:, 4, blk(h)], wT_b[:, h], St_b[:, h], False, True)
            last.then_inc(sem("gdn_v_mm"), 1)
            pe.wait_ge(sem("gdn_v"), i + 1)
            for h in range(H):
                mm(PS[:, 6, blk(h)], St_b[:, h], qe_b[:, h], True, False)
                last = mm(PS[:, 6, blk(h)], vn_b[:, h], qkT_b[:, h], False, True)
            last.then_inc(sem("gdn_o_mm"), 1)
            pe.wait_ge(sem("kl_ready"), i + 1)
            heads(7, lambda h: ktok[:, i, h], lambda h: vn_b[:, h]).then_inc(sem("gdn_state_mm"), 1)
        pe.wait_ge(sem("gdn_osq"), H)
        for b in range(NB):
            for h in range(H):
                last = token_sum(PS[:, 4, 4 * h + b:4 * h + b + 1], gsq[:, h, blk(b)])
        last.then_inc(sem("stat_mm"), 1)
        pe.wait_ge(sem("stat_rec"), 2)
        pe.wait_ge(evacuated, E_OUT1)
        for h in range(H):
            for b in range(NB):
                last = spread(PS[:, h, blk(b)], ost[:, 1, 4 * h + b:4 * h + b + 1])
            last.then_inc(sem("stat_bc"), 1)

        pe.wait_ge(sem("gy_ready"), H)
        for h in range(H):
            for b in range(NB):
                last = spread(PS[:, h, blk(b)], gcum[:, 2, b, h:h + 1])
            last.then_inc(sem("fox_cb_mm"), 1)

        def fox_scores(u):
            h, i = UNITS[u]
            n = (i + 1) * P
            if u >= 2:
                pe.wait_ge(sem("fox_min"), u - 1)
            mm(PS[:, 4 + u % 2, 0:n], qd[:, h, blk(i)], kd[:, h, 0:n], True, False)
            mm(PS[:, 4 + u % 2, blk(i)], ident, cmask, False, True).then_inc(sem("fox_s"), 1)

        fox_scores(0)
        pe.wait_ge(sem("fox_cb"), H)
        for u, (h, i) in enumerate(UNITS):
            if u + 1 < len(UNITS):
                fox_scores(u + 1)
            pe.wait_ge(sem("fox_p"), u + 1)
            if u >= 2:
                pe.wait_ge(sem("fox_wt"), u - 1)
            transpose_w(u, fbuf, 6 + u % 2).then_inc(sem("fox_t"), 1)
            if i == NB - 1:
                pe.wait_ge(sem("fox_wt"), u + 1)
                if h >= 2:
                    pe.wait_ge(y_ready, 12 + h - 1)
                weighted_values(h, FT, vd, h % 2).then_inc(sem("fox_pv"), 1)
        pe.wait_ge(y_ready, 2 * KD)
        for n in range(KD):
            stationary(T_OUT1 + n, E_OUT1 + n, AA)
        ffn(1, T_GU1, E_GU1, 3)
        norm_stats(4, 7)
        norm_spread(4, 7)

    block.__exit__(None, None, None)


def kernel(x, mix_norm_w, ffn_norm_w, final_norm_w, w_in_even, conv_w, conv_b, conv_ln_w, conv_ln_b,
           lambda_q1, lambda_k1, lambda_q2, lambda_k2, diff_subln_w, gdn_conv_w, w_in_odd,
           gdn_a_log, gdn_dt_bias, gdn_norm_w, fox_forget_bias, w_out, w_gate, w_up, w_down):
    import concourse.bacc as bacc
    from concourse.bass_utils import run_bass_kernel_spmd

    f = np.asarray

    def chunks(w):
        k, n = w.shape
        return w.reshape(k // P, P, n // P, P).transpose(2, 1, 0, 3).reshape(n // P, P, k // P * P)

    def movers(w):
        return w.reshape(4, 2, P, S).transpose(0, 2, 1, 3).reshape(4, P, 2 * S)

    def ffn_tiles(l):
        gu = np.stack([chunks(f(w_gate)[l]), chunks(f(w_up)[l])], axis=1)
        return [gu.reshape(2 * KF, P, TILE), f(w_down)[l].reshape(KF, P, TILE)]

    we, wo = f(w_in_even)[0], f(w_in_odd)[0]
    val_gate = np.stack([chunks(we[:, 0:512]), chunks(we[:, 512:1024])], axis=1).reshape(8, P, TILE)
    stream = np.ascontiguousarray(np.concatenate(
        [val_gate, chunks(we[:, 1024:2048]), movers(we[:, 2048:2560]), chunks(f(w_out)[0])] + ffn_tiles(0)
        + [chunks(wo[:, 0:1536]), chunks(wo[:, 2056:3080]), movers(wo[:, 3080:3592]), chunks(wo[:, 1536:2048]),
           chunks(f(w_out)[1])] + ffn_tiles(1)))
    assert stream.shape == (N_TILES, P, TILE)
    small = np.ascontiguousarray(np.concatenate([wo[:, 2048:2056], wo[:, 3592:3596]], axis=1)
                                 .reshape(KD, P, 12).transpose(1, 0, 2).reshape(P, KD * 12))

    def cols(v):
        v = f(v)
        v = v.reshape(v.shape[0] // P, P, -1)
        return v.transpose(1, 0, 2).reshape(P, -1)

    norms = [cols(w) for w in (f(mix_norm_w)[0], f(ffn_norm_w)[0], f(mix_norm_w)[1], f(ffn_norm_w)[1], f(final_norm_w))]
    lams = np.zeros((P, 4), np.float32)
    for n, v in enumerate((lambda_q1, lambda_k1, lambda_q2, lambda_k2)):
        lams[0:64, n] = f(v)[0]
    vecs = np.ascontiguousarray(np.concatenate(
        norms + [cols(f(conv_w)[0].T), cols(f(conv_b)[0]), cols(f(conv_ln_w)[0]), cols(f(conv_ln_b)[0]),
                 cols(f(diff_subln_w)[0]), cols(f(gdn_conv_w)[0].T), cols(f(gdn_norm_w)[0]), lams], axis=1))
    assert vecs.shape == (P, N_VEC)
    row = np.concatenate([f(gdn_a_log)[0], f(gdn_dt_bias)[0], f(fox_forget_bias)[0]]).reshape(1, 12)
    xt = np.ascontiguousarray(f(x)[0].T.reshape(KD, P, S).transpose(1, 0, 2))
    const, rope = shape_constants()

    nc = bacc.Bacc("TRN2", target_bir_lowering=False, num_devices=1)
    f32 = mybir.dt.float32
    arrays = {"x_t": xt, "w_stream": stream, "vectors": vecs, "row": row, "w_small": small,
              "shape_const": const, "rope_const": rope}
    args = [nc.dram_tensor(n, a.shape, f32, kind="ExternalInput").ap() for n, a in arrays.items()]
    out = nc.dram_tensor("out_t", (P, KD, S), f32, kind="ExternalOutput").ap()
    build(nc, *args, out)
    r = run_bass_kernel_spmd(nc, [arrays], core_ids=[0])
    got = r.results[0]["out_t"]
    return np.ascontiguousarray(got.transpose(2, 1, 0).reshape(1, S, D))
```

```python
import math

import numpy as np
import concourse.bass as bass
from concourse import mybir

P = 128
S = 512
D = 1024
NB = S // P
KD = D // P
FF = 2816
KF = FF // P
H = 4
TAPS, GTAPS = 31, 4
TILE = 1024
BIG = -1.0e30

T_IN0 = 0
T_OUT0 = T_IN0 + 20
T_GU0 = T_OUT0 + KD
T_DN0 = T_GU0 + 2 * KF
T_IN1 = T_DN0 + KF
T_OUT1 = T_IN1 + 29
T_GU1 = T_OUT1 + KD
T_DN1 = T_GU1 + 2 * KF
N_TILES = T_DN1 + KF
E_IN0 = 0
E_OUT0 = E_IN0 + 20
E_GU0 = E_OUT0 + KD
E_DN0 = E_GU0 + 2 * KF
E_IN1 = E_DN0 + KD
E_OUT1 = E_IN1 + 28
E_GU1 = E_OUT1 + KD
E_DN1 = E_GU1 + 2 * KF
HEAD_TILE = 4
RING = 4
RAW = 2

V_NORM = 0
V_CONVW = 40
V_CONVB = V_CONVW + 4 * TAPS
V_LNW = V_CONVB + 4
V_LNB = V_LNW + 4
V_SUBLN = V_LNB + 4
V_GCONV = V_SUBLN + 1
V_GNORM = V_GCONV + 12 * GTAPS
V_LAM = V_GNORM + 1
N_VEC = V_LAM + 4
LEVELS = [1, 2, 4, 8, 16, 32, 64]


def odd_tile(e):
    return T_IN1 + e + (1 if e >= HEAD_TILE else 0)


PE_STEPS, ACT_STEPS, DVE_STEPS, POOL_STEPS = 25, 17, 18, 3
STEP_T0, STEP_Z1, STEP_W, STEP_V, STEP_O, STEP_S = 3, 4, 21, 22, 23, 24


def odd_order():
    gdn = []
    lag = 6
    pos = {0: [(i, k) for i in (0, 2) for k in range(PE_STEPS)], 1: [(i, k) for i in (1, 3) for k in range(PE_STEPS)]}
    for r in range(2 * PE_STEPS + lag):
        if r < len(pos[0]):
            gdn.append(pos[0][r])
        if 0 <= r - lag < len(pos[1]):
            gdn.append(pos[1][r - lag])
    fill = [("tile", e, part) for e in range(12, 28) for part in range(4)]
    order, nf = [], 0
    spread_over = len(gdn) - 14
    for n, (i, k) in enumerate(gdn):
        order.append(("gdn", i, k))
        while nf < len(fill) and nf < (n + 1) * len(fill) / spread_over:
            order.append(fill[nf])
            if fill[nf][2] == 3:
                order.append(("evac", fill[nf][1], 0))
            nf += 1
    return order
LAMBDA_INIT = 0.8 - 0.6 * math.exp(-0.3 * 0)


def shape_constants():
    r = np.arange(P)
    row, col = r[:, None], r[None, :]
    parts = [
        np.eye(P),
        (row <= col) * 1.0,
        np.ones((P, P)),
        np.where(col > row, BIG, 0.0),
        np.where(row > col, BIG, 0.0),
    ]
    for b in LEVELS:
        parts.append(((row // (2 * b) == col // (2 * b)) & (row % (2 * b) < b) & (col % (2 * b) >= b)) * 1.0)
    const = np.concatenate(parts, axis=1).astype(np.float32)
    half = 8
    inv = (1.0 / (np.float32(500000.0) ** (np.arange(half, dtype=np.float32) / half))).astype(np.float32)
    ang = np.arange(S, dtype=np.float32)[:, None] * inv[None, :]
    cos, sin = np.cos(ang).astype(np.float32).T, np.sin(ang).astype(np.float32).T
    rc, rs, perm = np.ones((P, S)), np.zeros((P, S)), np.zeros((P, P))
    for p in range(P):
        q = p % 64
        if q < half:
            rc[p], rs[p], perm[p + half, p] = cos[q], -sin[q], 1.0
        elif q < 2 * half:
            rc[p], rs[p], perm[p - half, p] = cos[q - half], sin[q - half], 1.0
    rope = np.concatenate([rc, rs, perm], axis=1).astype(np.float32)
    return const, rope


def build(nc, x_d, w_d, vec_d, row_d, const_d, rope_d, out_d):
    f32, f32r, i32 = mybir.dt.float32, mybir.dt.float32r, mybir.dt.int32
    ALU, ACT, AX = mybir.AluOpType, mybir.ActivationFunctionType, mybir.AxisListType
    DH = 128
    SC_FOX = float(DH) ** -0.5
    SC_DIFF = 0.125

    size = {f32: 4, f32r: 4}

    def at(name, shape, dt, offset):
        t = nc.alloc_sbuf_tensor_at(name, [P] + list(shape), dt, offset=offset)
        return t, offset + (int(np.prod(shape)) * size[dt] + 31) // 32 * 32

    base = 16512
    xT, p = at("xT", [KD, S], f32, base)
    raw, p = at("raw", [RAW, TILE], f32, p)
    wring, p = at("wring", [RING, 2, TILE], f32r, p)
    at_H = p
    HH, p = at("HH", [KD, 2, S], f32r, p)
    consts, p = at("consts", [5 + len(LEVELS), P], f32, p)
    at_work = p
    hbuf, p = at("hbuf", [2, S], f32, p)
    sqb, p = at("sqb", [2, S], f32, p)
    ssq, p = at("ssq", [S], f32, p)
    rstd, p = at("rstd", [S], f32, p)
    vec, p = at("vec", [N_VEC], f32, p)
    at_small = p
    p += 2848
    at_A = p
    AA, p = at("AA", [KF, 2, S], f32r, p)
    gbuf, p = at("gbuf", [2, S], f32, p)
    ubuf, p = at("ubuf", [2, S], f32, p)
    abuf, p = at("abuf", [S], f32, p)
    TOP = 229344
    assert p <= TOP, p
    q = at_small
    rtok, q = at("rtok", [NB], f32, q)
    nst, q = at("nst", [NB], f32, q)
    lam, q = at("lam", [8], f32, q)
    lst, q = at("lst", [8], f32, q)
    amax, q = at("amax", [2, 2], f32, q)
    asum, q = at("asum", [2, 2], f32, q)
    arec, q = at("arec", [2, 2], f32, q)
    ost, q = at("ost", [2, 16], f32, q)
    rowv, q = at("rowv", [12], f32, q)
    srow, q = at("srow", [12], f32, q)
    baf, q = at("baf", [NB, 12], f32, q)
    z8, q = at("z8", [NB, 8], f32, q)
    e8, q = at("e8", [NB, 8], f32, q)
    sp8, q = at("sp8", [NB, 8], f32, q)
    expa, q = at("expa", [4], f32, q)
    beta, q = at("beta", [NB, H], f32, q)
    gtok, q = at("gtok", [NB, H], f32, q)
    lftok, q = at("lftok", [NB, H], f32, q)
    gcum, q = at("gcum", [3, NB, H], f32, q)
    gexp, q = at("gexp", [3, NB, H], f32, q)
    l2s, q = at("l2s", [NB, 8], f32, q)
    kscal, q = at("kscal", [3, NB, H], f32, q)
    qscal, q = at("qscal", [NB, H], f32, q)
    assert q <= at_A, (q, at_A)
    at_M = at_A + 8 * 2 * S * 4
    q = at_M
    rope, q = at("rope", [2 * S + P], f32, q)
    upad, q = at("upad", [4, S + TAPS - 1], f32, q)
    cacc, q = at("cacc", [4, S], f32, q)
    qk, q = at("qk", [8, S], f32, q)
    vtk, q = at("vtk", [NB, S], f32, q)
    WT, q = at("WT", [2, NB, S], f32, q)
    assert q <= TOP
    q = at_H
    pbuf, q = at("pbuf", [2, 2, S], f32, q)
    wbuf, q = at("wbuf", [2, S], f32, q)
    oT, q = at("oT", [H, S], f32, q)
    osq, q = at("osq", [H, S], f32, q)
    ytmp, q = at("ytmp", [2, S], f32, q)
    assert q <= at_H + 32768
    q = at_M
    qT, q = at("qT", [H, S], f32, q)
    kT, q = at("kT", [H, S], f32, q)
    ktok, q = at("ktok", [NB, H, P], f32, q)
    vtok, q = at("vtok", [NB, H, P], f32, q)
    at_z = q
    zT, q = at("zT", [H, S], f32, q)
    qd, q = at("qd", [H, S], f32, q)
    kd, q = at("kd", [H, S], f32, q)
    vd, q = at("vd", [NB, S], f32, q)
    cin, q = at("cin", [S + GTAPS - 1], f32, q)
    assert q <= TOP, (q, TOP)
    hrow, _ = at("hrow", [S], f32, at_z)
    q = at_A + 4 * 2 * S * 4
    G8, q = at("G8", [8, H, P], f32, q)
    assert q == at_M
    G5, _ = at("G5", [5, H, P], f32, at_work)
    gbufs = [[G8[:, n] for n in range(6)], [G8[:, 6], G8[:, 7]] + [G5[:, n] for n in range(4)]]
    St_b = G5[:, 4]
    gsq, _ = at("gsq", [H, S], f32, at_work)
    outT, _ = at("outT", [KD, S], f32, at_H)
    q = at_H
    cb, q = at("cb", [H, S], f32, q)
    tbuf, q = at("tbuf", [2, S], f32, q)
    fbuf, q = at("fbuf", [2, S], f32, q)
    FT, q = at("FT", [2, NB, S], f32, q)
    assert q <= at_H + 32768

    PS = nc.alloc_psum_tensor("PS", [P, 8, S], f32)

    ident, cums, ones = consts[:, 0], consts[:, 1], consts[:, 2]
    cmask, dmask = consts[:, 3], consts[:, 4]
    lmask = {b: consts[:, 5 + n].bitcast(i32) for n, b in enumerate(LEVELS)}

    def over_heads(ap):
        return ap.unsqueeze(1).broadcast_to([P, H, P])

    def per_head(ap):
        return ap.unsqueeze(2).broadcast_to([P, H, P])

    def blk(b):
        return slice(b * P, (b + 1) * P)

    def hd(ps_bank):
        return PS[:, ps_bank].rearrange("p (h c) -> p h c", h=H)

    def vcol(n):
        return vec[:, n:n + 1]

    sems = {}

    def sem(name):
        if name not in sems:
            sems[name] = nc.alloc_semaphore(name)
        return sems[name]

    def slot_round(t):
        return t // RING + 1

    x_loaded = [sem(f"x_loaded{n}") for n in range(4)]
    gdn_mm, gdn_act, gdn_dve, gdn_pool = [[sem(f"gdn{n}_{e}") for n in range(2)] for e in ("products", "act", "dve", "pool")]
    const_loaded, vec_loaded, rope_loaded, small_loaded = map(sem, ("const_loaded", "vec_loaded", "rope_loaded", "small_loaded"))
    raw_loaded = [sem(f"raw_loaded{n}") for n in range(RAW)]
    hi_ready = [sem(f"hi_ready{n}") for n in range(RING)]
    lo_ready = [sem(f"lo_ready{n}") for n in range(RING)]
    tile_used, evacuated = sem("tile_used"), sem("evacuated")
    feed_mul, feed_hi, feed_sq, ssq_done, h_ready = map(sem, ("feed_mul", "feed_hi", "feed_sq", "ssq_done", "h_ready"))
    norm_sum, norm_ms, norm_sqrt, norm_tok, norm_bc, norm_rstd = map(
        sem, ("norm_sum", "norm_ms", "norm_sqrt", "norm_tok", "norm_bc", "norm_rstd"))
    y_ready = sem("y_ready")
    down_done = sem("down_done")
    out_done = sem("out_done")
    dchain = sem("dve_chain")

    UNITS = [(h, i) for h in range(H) for i in range(NB)]
    FINAL = 4

    block = nc.Block()
    block.__enter__()

    @block.sync
    def _(sp):
        for n in range(4):
            sp.dma_start(xT[:, 2 * n:2 * n + 2], x_d[:, 2 * n:2 * n + 2]).then_inc(x_loaded[n], 16)
        for t in range(RAW):
            sp.dma_start(raw[:, t], w_d[t]).then_inc(raw_loaded[t], 16)
        for t in range(RAW, RING):
            sp.wait_ge(hi_ready[t - RAW], 1)
            sp.wait_ge(lo_ready[t - RAW], 1)
            sp.dma_start(raw[:, t % RAW], w_d[t]).then_inc(raw_loaded[t % RAW], 16)
        with sp.Fori(1, N_TILES // RING) as r:
            for j in range(RING):
                behind = (j - RAW) % RING
                done = r if j < RAW else r + 1
                sp.wait_ge(hi_ready[behind], done)
                sp.wait_ge(lo_ready[behind], done)
                src = w_d[bass.ds(r * RING + j, 1)].rearrange("a p c -> (a p) c")
                sp.dma_start(raw[:, j % RAW], src).then_inc(raw_loaded[j % RAW], 16)
        for t in range(N_TILES // RING * RING, N_TILES):
            sp.wait_ge(hi_ready[(t - RAW) % RING], slot_round(t - RAW))
            sp.wait_ge(lo_ready[(t - RAW) % RING], slot_round(t - RAW))
            sp.dma_start(raw[:, t % RAW], w_d[t]).then_inc(raw_loaded[t % RAW], 16)
        for n in range(KD):
            sp.wait_ge(sem("out_ready"), n + 1)
            sp.dma_start(out_d[:, n], outT[:, n]).then_inc(out_done, 16)
        sp.wait_ge(out_done, 16 * KD)

    @block.gpsimd
    def _(pool):
        def lo(t):
            pool.wait_ge(hi_ready[t % RING], slot_round(t))
            if t >= RING:
                pool.wait_ge(tile_used, t - RING + 1)
            nc.gpsimd.tensor_tensor(wring[:, t % RING, 1], raw[:, t % RAW], wring[:, t % RING, 0].bitcast(f32),
                                    ALU.subtract).then_inc(lo_ready[t % RING], 1)

        def add_squares(s, n):
            if n == 0:
                return
            pool.wait_ge(feed_sq, KD * s + n + 1)
            if n == 1:
                if s:
                    pool.wait_ge(norm_sum, s)
                nc.gpsimd.tensor_tensor(ssq[:], sqb[:, 0], sqb[:, 1], ALU.add).then_inc(ssq_done, 1)
            else:
                pool.wait_ge(ssq_done, 7 * s + n - 1)
                nc.gpsimd.tensor_tensor(ssq[:], ssq[:], sqb[:, n % 2], ALU.add).then_inc(ssq_done, 1)

        for n in range(KD):
            add_squares(0, n)
            if n % 2:
                lo(n // 2)
        nc.gpsimd.memset(upad[:, :, 0:TAPS - 1], 0.0).then_inc(sem("pad_zero"), 1)
        for t in range(4, 24):
            lo(t)
        for n in range(KD):
            if n < 4:
                lo(T_OUT0 + RING + n)
            add_squares(1, n)
        for n in range(KD):
            add_squares(2, n)
        nc.gpsimd.memset(cin[:, 0:GTAPS - 1], 0.0).then_inc(sem("cin_zero"), 1)
        for e in range(12):
            lo(odd_tile(e) + RING)
            if e == HEAD_TILE - 1:
                lo(T_IN1 + HEAD_TILE + RING)
        pool.wait_ge(sem("gdn_scalars"), 1)
        nc.gpsimd.memset(St_b, 0.0).then_inc(sem("state_zero"), 1)
        pool.wait_ge(sem("tok_ready"), 8)
        for kind, a, b in odd_order():
            if kind == "evac":
                if a < 20 or a >= 24:
                    lo(odd_tile(a) + RING)
            if kind == "tile" and b == 3 and 20 <= a < 24:
                lo(odd_tile(a) + RING)
            if kind == "gdn":
                i, st = a, a % 2
                j = i // 2
                if b == 0:
                    nc.gpsimd.tensor_tensor(vtok[:, i], vtok[:, i], per_head(beta[:, i]), ALU.mult).then_inc(gdn_pool[st], 1)
                if b == STEP_W:
                    pool.wait_ge(gdn_mm[st], j * PE_STEPS + STEP_W - 1)
                    nc.gpsimd.tensor_tensor(gbufs[st][3], ktok[:, i], per_head(kscal[:, 1, i]), ALU.mult).then_inc(gdn_pool[st], 1)
                    pool.wait_ge(gdn_pool[st], j * POOL_STEPS + 2)
                    nc.gpsimd.tensor_tensor(ktok[:, i], ktok[:, i], per_head(kscal[:, 2, i]), ALU.mult).then_inc(gdn_pool[st], 1)
        for n in range(KD):
            if n < 4:
                lo(T_OUT1 + RING + n)
            add_squares(3, n)
        for n in range(KD):
            add_squares(4, n)

    @block.scalar
    def _(act):
        act.dma_start(vec[:], vec_d).then_inc(vec_loaded, 16)
        act.dma_start(consts[:].rearrange("p a b -> p (a b)"), const_d).then_inc(const_loaded, 16)
        act.dma_start(rope[:], rope_d).then_inc(rope_loaded, 16)
        act.dma_start(rowv[0:1, :], row_d).then_inc(small_loaded, 16)

        def hi(t):
            act.wait_ge(raw_loaded[t % RAW], 16 * (t // RAW + 1))
            if t >= RING:
                act.wait_ge(tile_used, t - RING + 1)
            nc.scalar.activation(wring[:, t % RING, 0], raw[:, t % RAW], ACT.Copy).then_inc(hi_ready[t % RING], 1)

        def feed(s, n):
            if s < FINAL:
                act.wait_ge(feed_mul, KD * s + n + 1)
                nc.scalar.activation(HH[:, n, 0], hbuf[:, n % 2], ACT.Copy).then_inc(feed_hi, 1)
            else:
                act.wait_ge(evacuated, E_DN1 + n + 1)
            if n >= 2:
                act.wait_ge(ssq_done, 7 * s + max(n - 2, 1))
            elif s:
                act.wait_ge(ssq_done, 7 * s)
            nc.scalar.activation(sqb[:, n % 2], xT[:, n], ACT.Square).then_inc(feed_sq, 1)

        def norm_root(s):
            act.wait_ge(norm_ms, s + 1)
            nc.scalar.activation(nst[:], nst[:], ACT.Sqrt).then_inc(norm_sqrt, 1)

        def ffn(s, tg, eg, last):
            g0 = KF * s
            with act.Fori(0, KF // 2) as r:
                for c in range(2):
                    done = r * 2 + (g0 + c + 1)
                    act.wait_ge(evacuated, r * RING + (eg + 2 * c + 1))
                    nc.scalar.activation(gbuf[:, c], gbuf[:, c], ACT.Silu).then_inc(sem("gate_silu"), 1)
                    for u in range(2):
                        j = 2 * c + u
                        t = tg + RING + j
                        if u:
                            act.wait_ge(sem("ffn_mul"), done)
                            nc.scalar.activation(AA[:, bass.ds(r * 2 + c, 1), 0].rearrange("p a b -> p (a b)"),
                                                 abuf[:], ACT.Copy).then_inc(sem("ffn_hi"), 1)
                        act.wait_ge(raw_loaded[t % RAW], r * (16 * RING // RAW) + 16 * (t // RAW + 1))
                        act.wait_ge(tile_used, r * RING + (t - RING + 1))
                        nc.scalar.activation(wring[:, t % RING, 0], raw[:, t % RAW], ACT.Copy).then_inc(hi_ready[t % RING], 1)
            td = tg + 2 * KF
            whole = KF // RING - (1 if last else 0)
            with act.Fori(0, whole) as r:
                for j in range(RING):
                    t = td + RING + j
                    act.wait_ge(raw_loaded[t % RAW], r * (16 * RING // RAW) + 16 * (t // RAW + 1))
                    act.wait_ge(tile_used, r * RING + (t - RING + 1))
                    nc.scalar.activation(wring[:, t % RING, 0], raw[:, t % RAW], ACT.Copy).then_inc(hi_ready[t % RING], 1)
            for t in range(td + RING + whole * RING, td + KF + (0 if last else RING)):
                hi(t)

        def token_root(k, cols):
            act.wait_ge(sem("stat_ms"), k)
            nc.scalar.activation(ost[:, 0, 0:cols], ost[:, 0, 0:cols], ACT.Sqrt).then_inc(sem("stat_root"), 1)

        for n in range(KD):
            feed(0, n)
            if n % 2:
                hi(n // 2)
        norm_root(0)
        act.wait_ge(sem("lam_sum"), 1)
        nc.scalar.activation(lam[:, 4:6], PS[:, 6, 0:2], ACT.Exp).then_inc(sem("lam_exp"), 1)
        for e in range(20):
            hi(e + RING)
            if e % 2 == 1 and e < 8:
                c = e // 2
                act.wait_ge(evacuated, e + 1)
                nc.scalar.activation(sqb[:, c % 2], sqb[:, c % 2], ACT.Sigmoid).then_inc(sem("gate_sig"), 1)

        def diff_exp(u):
            h, i = UNITS[u]
            n = (i + 1) * P
            for m in range(2):
                act.wait_ge(sem("diff_max"), u + 1)
                if u >= 2 and m == 0:
                    act.wait_ge(sem("diff_w"), u - 1)
                nc.scalar.activation(pbuf[:, u % 2, m, 0:n], PS[:, 4 + 2 * (u % 2) + m, 0:n], ACT.Exp,
                                     bias=amax[:, u % 2, m:m + 1],
                                     accum_out=asum[:, u % 2, m:m + 1]).then_inc(sem("diff_exp"), 1)

        def wt_copy(u, sem_t, sem_c, dst, bank, sem_pv):
            h, i = UNITS[u]
            act.wait_ge(sem(sem_t), u + 1)
            if h >= 2 and i == 0:
                act.wait_ge(sem(sem_pv), h - 1)
            nc.scalar.activation(dst[:, h % 2, 0:i + 1, blk(i)],
                                 PS[:, bank, 0:(i + 1) * P].rearrange("p (j c) -> p j c", c=P),
                                 ACT.Copy).then_inc(sem(sem_c), 1)

        diff_exp(0)
        for u, (h, i) in enumerate(UNITS):
            if u + 1 < len(UNITS):
                diff_exp(u + 1)
            wt_copy(u, "diff_t", "diff_wt", WT, u % 2, "diff_pv")
            if u == 4:
                for c in range(4):
                    act.wait_ge(sem("ln_centred"), c + 1)
                    nc.scalar.activation(upad[:, c, 0:S], cacc[:, c], ACT.Square).then_inc(sem("ln_sq"), 1)
            if u == 6:
                act.wait_ge(sem("ln_var"), 1)
                nc.scalar.activation(lst[:, 4:8], lst[:, 4:8], ACT.Sqrt).then_inc(sem("ln_root"), 1)
            if (i == 0 and h) or u == len(UNITS) - 1:
                g = h if u == len(UNITS) - 1 else h - 1
                act.wait_ge(sem("diff_pv"), g + 1)
                nc.scalar.activation(oT[:, g], PS[:, 2], ACT.Copy).then_inc(sem("diff_o"), 1)
                nc.scalar.activation(osq[:, g], PS[:, 2], ACT.Square).then_inc(sem("diff_osq"), 1)
        token_root(1, 16)
        for c in range(4):
            act.wait_ge(sem("ln_scaled"), c + 1)
            if c >= 2:
                act.wait_ge(y_ready, c - 1)
            nc.scalar.activation(ytmp[:, c % 2], cacc[:, c], ACT.Silu, bias=vcol(V_LNB + c),
                                 scale=vcol(V_LNW + c)).then_inc(sem("y_tmp"), 1)
            act.wait_ge(sem("y_tmp"), c + 1)
            nc.scalar.activation(AA[:, c, 0], ytmp[:, c % 2], ACT.Copy).then_inc(sem("y_hi"), 1)
        for h in range(H):
            act.wait_ge(sem("y_scaled"), h + 1)
            nc.scalar.activation(AA[:, 4 + h, 0], oT[:, h], ACT.Copy).then_inc(sem("y_hi"), 1)
        for n in range(KD):
            if n < 4:
                hi(T_OUT0 + RING + n)
            feed(1, n)
            if n >= 4:
                hi(T_OUT0 + RING + n)
        norm_root(1)
        ffn(0, T_GU0, E_GU0, False)
        for n in range(KD):
            feed(2, n)
        norm_root(2)
        for e in range(12):
            if e < HEAD_TILE:
                hi(odd_tile(e) + RING)
            if e == HEAD_TILE - 1:
                hi(T_IN1 + HEAD_TILE + RING)
            if e >= HEAD_TILE:
                hi(odd_tile(e) + RING)
            if e >= 8:
                m = e - 8
                act.wait_ge(sem("tok_t"), m + 1)
                nc.scalar.activation((ktok, vtok)[m // 4][:, :, m % 4], PS[:, 4 + m % 2].rearrange("p (b c) -> p b c", b=NB),
                                     ACT.Copy).then_inc(sem("tok_ready"), 1)
            h = e % H
            act.wait_ge(sem("gconv_done"), e + 1)
            if e >= 10:
                act.wait_ge(sem("tok_t"), e - 5)
            if e in (8, 9):
                act.wait_ge(sem("l2_mm"), e - 1)
            dst = (qT[:, h], kT[:, h], sqb[:, e % 2])[e // 4]
            nc.scalar.activation(dst, hbuf[:, e % 2], ACT.Silu).then_inc(sem("gsilu"), 1)
            if e < 8:
                act.wait_ge(sem("gsilu"), e + 1)
                if e >= 2:
                    act.wait_ge(sem("l2_mm"), e - 1)
                nc.scalar.activation(sqb[:, e % 2], dst, ACT.Square).then_inc(sem("gsq"), 1)
            if e == 5:
                act.wait_ge(sem("gate_args"), 1)
                nc.scalar.activation(e8[:], e8[:], ACT.Exp).then_inc(sem("gate_exp"), 1)
                nc.scalar.activation(expa[:], srow[:, 0:4], ACT.Exp).then_inc(sem("gate_exp"), 1)
                nc.scalar.activation(beta[:], baf[:, :, 0:4], ACT.Exp, scale=-1.0).then_inc(sem("gate_exp"), 1)
            if e == 6:
                act.wait_ge(sem("gate_one"), 1)
                nc.scalar.activation(e8[:], e8[:], ACT.Ln).then_inc(sem("gate_ln"), 1)
            if e == 9:
                act.wait_ge(sem("g_sums"), 1)
                for n in range(3):
                    nc.scalar.activation(gexp[:, n], gexp[:, n], ACT.Exp).then_inc(sem("g_exp"), 1)
        for m in range(4, 8):
            act.wait_ge(sem("tok_t"), m + 1)
            nc.scalar.activation(vtok[:, :, m % 4], PS[:, 4 + m % 2].rearrange("p (b c) -> p b c", b=NB),
                                 ACT.Copy).then_inc(sem("tok_ready"), 1)
        act.wait_ge(sem("l2_ms"), 1)
        nc.scalar.activation(l2s[:], l2s[:], ACT.Sqrt).then_inc(sem("l2_root"), 1)

        def gdn(i, k):
            st, j = i % 2, i // 2
            X, Y = 4 + 2 * st, 5 + 2 * st
            Zb, Tb, Rb = gbufs[st][0], gbufs[st][1], gbufs[st][2]

            def run(pe_step, out, bank, func=ACT.Copy, **kw):
                act.wait_ge(gdn_mm[st], j * PE_STEPS + pe_step + 1)
                nc.scalar.activation(out, hd(bank), func, **kw).then_inc(gdn_act[st], 1)

            if k == 0:
                if j:
                    act.wait_ge(gdn_dve[st], DVE_STEPS)
                run(0, Rb, X, ACT.Exp)
                act.wait_ge(gdn_dve[st], j * DVE_STEPS + 3)
                nc.scalar.activation(Zb, Zb, ACT.Exp).then_inc(gdn_act[st], 1)
            elif k == STEP_T0:
                run(k, Tb, X)
            elif STEP_Z1 <= k < STEP_W:
                if (k - STEP_Z1) % 3 == 0:
                    run(k, Zb, X)
                if (k - STEP_Z1) % 3 == 2:
                    run(k, Tb, X)
            elif k == STEP_W:
                run(k, Tb, X, scale=-1.0)
            elif k == STEP_V:
                run(k, Zb, Y)
            elif k == STEP_O:
                run(k, qT[:, :, blk(i)], X)

        for kind, a, b in odd_order():
            if kind == "gdn":
                gdn(a, b)
            elif kind == "tile" and b == 3 and 20 <= a < 24:
                hi(odd_tile(a) + RING)
            elif kind == "evac":
                if a < 20 or a >= 24:
                    hi(odd_tile(a) + RING)
        for h in range(H):
            act.wait_ge(evacuated, E_IN1 + 24 + h + 1)
            nc.scalar.activation(zT[:, h], zT[:, h], ACT.Silu).then_inc(sem("z_silu"), 1)
        act.wait_ge(gdn_act[0], 2 * ACT_STEPS)
        act.wait_ge(gdn_act[1], 2 * ACT_STEPS)
        act.wait_ge(gdn_dve[1], 2 * DVE_STEPS)
        for h in range(H):
            nc.scalar.activation(gsq[:, h], qT[:, h], ACT.Square).then_inc(sem("gdn_osq"), 1)
        token_root(2, 16)
        for h in range(H):
            act.wait_ge(sem("gy_ready"), h + 1)
            nc.scalar.activation(AA[:, h, 0], qT[:, h], ACT.Copy).then_inc(sem("y_hi"), 1)

        def fox_exp(u):
            h, i = UNITS[u]
            n = (i + 1) * P
            act.wait_ge(sem("fox_min"), u + 1)
            if u >= 2:
                act.wait_ge(sem("fox_t"), u - 1)
            nc.scalar.activation(fbuf[:, u % 2, 0:n], tbuf[:, u % 2, 0:n], ACT.Exp, bias=amax[:, 0, u % 2:u % 2 + 1],
                                 scale=-1.0, accum_out=asum[:, 0, u % 2:u % 2 + 1]).then_inc(sem("fox_exp"), 1)

        fox_exp(0)
        for u, (h, i) in enumerate(UNITS):
            if u + 1 < len(UNITS):
                fox_exp(u + 1)
            wt_copy(u, "fox_t", "fox_wt", FT, 6 + u % 2, "fox_pv")
            if (i == 0 and h) or u == len(UNITS) - 1:
                g = h if u == len(UNITS) - 1 else h - 1
                act.wait_ge(sem("fox_pv"), g + 1)
                nc.scalar.activation(AA[:, 4 + g, 0], PS[:, g % 2], ACT.Copy).then_inc(sem("y_hi"), 1)
        for n in range(KD):
            if n < 4:
                hi(T_OUT1 + RING + n)
            feed(3, n)
            if n >= 4:
                hi(T_OUT1 + RING + n)
        norm_root(3)
        ffn(1, T_GU1, E_GU1, True)
        for n in range(KD):
            feed(4, n)
        norm_root(4)

    @block.vector
    def _(dve):
        V = nc.vector
        seq = [0]

        def link(ins):
            seq[0] += 1
            ins.then_inc(dchain, 1)
            dve.wait_ge(dchain, seq[0])

        def feed_mul_(s, n):
            if n >= 2:
                dve.wait_ge(h_ready, KD * s + n - 1)
            V.tensor_scalar(hbuf[:, n % 2], xT[:, n], vcol(V_NORM + KD * s + n), None, ALU.mult).then_inc(feed_mul, 1)

        def feed_lo(s, n):
            dve.wait_ge(feed_hi, KD * s + n + 1)
            V.tensor_tensor(HH[:, n, 1], hbuf[:, n % 2], HH[:, n, 0].bitcast(f32), ALU.subtract).then_inc(h_ready, 1)

        def norm_finish(s, bank):
            dve.wait_ge(norm_sum, s + 1)
            V.tensor_scalar(nst[:], PS[:, bank, 0:NB], 1.0 / D, 1e-6, ALU.mult, ALU.add).then_inc(norm_ms, 1)
            dve.wait_ge(norm_sqrt, s + 1)
            V.reciprocal(rtok[:], nst[:]).then_inc(norm_tok, 1)
            dve.wait_ge(norm_bc, s + 1)
            V.tensor_copy(rstd[:], PS[:, bank]).then_inc(norm_rstd, 1)
            dve.wait_ge(norm_rstd, s + 1)

        def residual(n, e, bank):
            V.tensor_tensor(xT[:, n], xT[:, n], PS[:, bank], ALU.add).then_inc(evacuated, 1)
            dve.wait_ge(evacuated, e + 1)

        def ffn(s, tg, eg, last):
            with dve.Fori(0, KF // 2) as r:
                for c in range(2):
                    cnt = r * 2 + (KF * s + c + 1)
                    for u, buf in enumerate((gbuf, ubuf)):
                        dve.wait_ge(tile_used, r * RING + (tg + 2 * c + u + 1))
                        V.tensor_tensor(buf[:, c], PS[:, 2 * c + u], rstd[:], ALU.mult).then_inc(evacuated, 1)
                    dve.wait_ge(evacuated, r * RING + (eg + 2 * c + 2))
                    for u in range(2):
                        j = 2 * c + u
                        t = tg + RING + j
                        if u == 0:
                            dve.wait_ge(sem("gate_silu"), cnt)
                            V.tensor_tensor(abuf[:], gbuf[:, c], ubuf[:, c], ALU.mult).then_inc(sem("ffn_mul"), 1)
                        dve.wait_ge(hi_ready[t % RING], r + slot_round(t))
                        V.tensor_tensor(wring[:, t % RING, 1], raw[:, t % RAW], wring[:, t % RING, 0].bitcast(f32),
                                        ALU.subtract).then_inc(lo_ready[t % RING], 1)
                        if u == 0:
                            dve.wait_ge(sem("ffn_hi"), cnt)
                            V.tensor_tensor(AA[:, bass.ds(r * 2 + c, 1), 1].rearrange("p a b -> p (a b)"), abuf[:],
                                            AA[:, bass.ds(r * 2 + c, 1), 0].rearrange("p a b -> p (a b)").bitcast(f32),
                                            ALU.subtract).then_inc(sem("ffn_lo"), 1)
            td = tg + 2 * KF
            whole = KF // RING - (1 if last else 0)
            with dve.Fori(0, whole) as r:
                for j in range(RING):
                    t = td + RING + j
                    dve.wait_ge(hi_ready[t % RING], r + slot_round(t))
                    V.tensor_tensor(wring[:, t % RING, 1], raw[:, t % RAW], wring[:, t % RING, 0].bitcast(f32),
                                    ALU.subtract).then_inc(lo_ready[t % RING], 1)
            for t in range(td + RING + whole * RING, td + KF + (0 if last else RING)):
                lo(t)

        def lo(t):
            dve.wait_ge(hi_ready[t % RING], slot_round(t))
            V.tensor_tensor(wring[:, t % RING, 1], raw[:, t % RAW], wring[:, t % RING, 0].bitcast(f32),
                            ALU.subtract).then_inc(lo_ready[t % RING], 1)

        def down(s, td, e0):
            for n in range(KD):
                if n < KD - 1:
                    dve.wait_ge(down_done, (s // 2 - 1) * (KD - 1) + n + 1)
                else:
                    dve.wait_ge(tile_used, td + KF)
                residual(n, e0 + n, n)
                if s < FINAL:
                    feed_mul_(s, n)
                    if n:
                        feed_lo(s, n - 1)
            if s < FINAL:
                feed_lo(s, KD - 1)

        def out_proj(s, t0, e0):
            for n in range(KD):
                dve.wait_ge(tile_used, t0 + n + 1)
                residual(n, e0 + n, (e0 + n) % 4)
                feed_mul_(s, n)
                if n:
                    feed_lo(s, n - 1)
                if n >= 5:
                    lo(t0 + RING + n - 1)
            feed_lo(s, KD - 1)
            lo(t0 + RING + KD - 1)

        dve.wait_ge(vec_loaded, 16)
        for n in range(KD):
            dve.wait_ge(x_loaded[n // 2], 16)
            feed_mul_(0, n)
            if n:
                feed_lo(0, n - 1)
        feed_lo(0, KD - 1)
        V.tensor_tensor(lam[0:64, 0:1], vec[0:64, V_LAM:V_LAM + 1], vec[0:64, V_LAM + 1:V_LAM + 2], ALU.mult).then_inc(sem("lam_prod"), 1)
        V.tensor_tensor(lam[0:64, 1:2], vec[0:64, V_LAM + 2:V_LAM + 3], vec[0:64, V_LAM + 3:V_LAM + 4], ALU.mult).then_inc(sem("lam_prod"), 1)
        norm_finish(0, 7)
        dve.wait_ge(sem("lam_exp"), 1)
        link(V.tensor_tensor(lam[:, 6:7], lam[:, 5:6], lam[:, 4:5], ALU.subtract))
        link(V.tensor_scalar(lam[:, 7:8], lam[:, 6:7], -LAMBDA_INIT, None, ALU.add))
        def taps():
            for c in range(4):
                link(V.tensor_scalar(cacc[:, c], upad[:, c, 0:S], vcol(V_CONVW + TAPS * c), vcol(V_CONVB + c), ALU.mult, ALU.add))
                yield
                for k in range(1, TAPS):
                    ins = V.scalar_tensor_tensor(cacc[:, c], upad[:, c, k:k + S], vcol(V_CONVW + TAPS * c + k), cacc[:, c],
                                                 ALU.mult, ALU.add)
                    if k < TAPS - 1:
                        link(ins)
                    else:
                        ins.then_inc(sem("conv_done"), 1)
                        dve.wait_ge(sem("conv_done"), c + 1)
                    yield

        conv = taps()

        def pump(n):
            for _ in range(n):
                next(conv, None)

        def evac(e, t):
            dve.wait_ge(tile_used, t + 1)

        def rope_finish(j):
            dve.wait_ge(sem("rope_mm"), j + 1)
            src = hbuf[:, j % 2]
            V.tensor_tensor(qk[:, j], src, rope[:, 0:S], ALU.mult).then_inc(sem("rope_cos"), 1)
            V.tensor_tensor(sqb[:, j % 2], PS[:, 4 + j % 2], rope[:, S:2 * S], ALU.mult).then_inc(sem("rope_sin"), 1)
            dve.wait_ge(sem("rope_sin"), j + 1)
            V.tensor_tensor(qk[:, j], qk[:, j], sqb[:, j % 2], ALU.add).then_inc(sem("qk_ready"), 1)

        dve.wait_ge(sem("pad_zero"), 1)
        dve.wait_ge(rope_loaded, 16)
        for c in range(4):
            evac(2 * c, 2 * c)
            V.tensor_tensor(hbuf[:, c % 2], PS[:, (2 * c) % 4], rstd[:], ALU.mult).then_inc(evacuated, 1)
            evac(2 * c + 1, 2 * c + 1)
            V.tensor_tensor(sqb[:, c % 2], PS[:, (2 * c + 1) % 4], rstd[:], ALU.mult).then_inc(evacuated, 1)
            pump(7 if c else 0)
            dve.wait_ge(sem("gate_sig"), c + 1)
            link(V.tensor_tensor(upad[:, c, TAPS - 1:], hbuf[:, c % 2], sqb[:, c % 2], ALU.mult))
            pump(7 if c else 10)
        for j in range(8):
            e = 8 + j
            evac(e, e)
            V.scalar_tensor_tensor(hbuf[:, j % 2], PS[:, e % 4], SC_DIFF if j < 4 else 1.0, rstd[:], ALU.mult, ALU.mult).then_inc(evacuated, 1)
            pump(4)
            if j:
                rope_finish(j - 1)
        rope_finish(7)
        pump(30)
        evac(19, 19)
        for b in range(NB):
            V.tensor_scalar(vtk[:, b], PS[:, b], rtok[:, b:b + 1], None, ALU.mult).then_inc(evacuated, 1)
        pump(10000)

        def diff_max(u):
            h, i = UNITS[u]
            n = (i + 1) * P
            dve.wait_ge(sem("diff_s"), u + 1)
            bank = 4 + 2 * (u % 2)
            V.tensor_reduce(amax[:, u % 2], PS[:, bank:bank + 2, 0:n], AX.X, ALU.max, negate=True).then_inc(sem("diff_max"), 1)

        def diff_combine(u):
            h, i = UNITS[u]
            n = (i + 1) * P
            dve.wait_ge(sem("diff_exp"), 2 * u + 2)
            link(V.reciprocal(arec[:, u % 2], asum[:, u % 2]))
            link(V.tensor_scalar(arec[:, u % 2, 1:2], arec[:, u % 2, 1:2], lam[:, 7:8], None, ALU.mult))
            link(V.tensor_scalar(pbuf[:, u % 2, 0, 0:n], pbuf[:, u % 2, 0, 0:n], arec[:, u % 2, 0:1], None, ALU.mult))
            if u >= 2:
                dve.wait_ge(sem("diff_t"), u - 1)
            V.scalar_tensor_tensor(wbuf[:, u % 2, 0:n], pbuf[:, u % 2, 1, 0:n], arec[:, u % 2, 1:2],
                                   pbuf[:, u % 2, 0, 0:n], ALU.mult, ALU.add).then_inc(sem("diff_w"), 1)

        diff_max(0)
        for u in range(len(UNITS)):
            diff_combine(u)
            if u + 1 < len(UNITS):
                diff_max(u + 1)
            if u == 1:
                dve.wait_ge(sem("ln_mean_mm"), 1)
                V.tensor_scalar(lst[:, 0:4], PS[:, 3, 0:4], 1.0 / 512, None, ALU.mult).then_inc(sem("ln_mean"), 1)
            if u == 3:
                dve.wait_ge(sem("ln_mean_bc"), 1)
                for c in range(4):
                    V.tensor_tensor(cacc[:, c], cacc[:, c], PS[:, 3], ALU.subtract).then_inc(sem("ln_centred"), 1)
            if u == 5:
                dve.wait_ge(sem("ln_var_mm"), 1)
                V.tensor_scalar(lst[:, 4:8], PS[:, 3, 0:4], 1.0 / 512, 1e-5, ALU.mult, ALU.add).then_inc(sem("ln_var"), 1)
            if u == 7:
                dve.wait_ge(sem("ln_root"), 1)
                V.reciprocal(lst[:, 4:8], lst[:, 4:8]).then_inc(sem("ln_rstd"), 1)
            if u == 9:
                dve.wait_ge(sem("ln_rstd_bc"), 1)
                for c in range(4):
                    V.tensor_tensor(cacc[:, c], cacc[:, c], PS[:, 3], ALU.mult).then_inc(sem("ln_scaled"), 1)

        def y_lo(k, chunk, src):
            dve.wait_ge(sem("y_hi"), k)
            V.tensor_tensor(AA[:, chunk, 1], src, AA[:, chunk, 0].bitcast(f32), ALU.subtract).then_inc(y_ready, 1)

        def token_stat(k, bank, scale, eps):
            dve.wait_ge(sem("stat_mm"), k)
            V.tensor_scalar(ost[:, 0], PS[:, bank, 0:16], scale, eps, ALU.mult, ALU.add).then_inc(sem("stat_ms"), 1)
            dve.wait_ge(sem("stat_root"), k)
            V.reciprocal(ost[:, 1], ost[:, 0]).then_inc(sem("stat_rec"), 1)

        token_stat(1, 3, 1.0 / P, 1e-6)
        link(V.tensor_scalar(arec[:, 0, 0:1], vcol(V_SUBLN), 1.0 - LAMBDA_INIT, None, ALU.mult))
        for c in range(4):
            y_lo(c + 1, c, ytmp[:, c % 2])
        for h in range(H):
            dve.wait_ge(sem("stat_bc"), h + 1)
            V.scalar_tensor_tensor(oT[:, h], oT[:, h], arec[:, 0, 0:1], PS[:, 4 + h], ALU.mult, ALU.mult).then_inc(sem("y_scaled"), 1)
        for h in range(H):
            y_lo(5 + h, 4 + h, oT[:, h])
        out_proj(1, T_OUT0, E_OUT0)
        norm_finish(1, 7)
        ffn(0, T_GU0, E_GU0, False)
        down(2, T_DN0, E_DN0)

        norm_finish(2, 7)

        def gates_1():
            dve.wait_ge(sem("baf_mm"), 1)
            V.tensor_copy(srow[:], PS[:, 6, 64:76]).then_inc(sem("gate_tmp"), 1)
            V.tensor_copy(baf[:].rearrange("p a b -> p (a b)"), PS[:, 6, 0:48]).then_inc(sem("gate_tmp"), 1)
            dve.wait_ge(sem("gate_tmp"), 2)
            V.tensor_tensor(z8[:, :, 0:4], baf[:, :, 4:8], srow[:, 4:8].unsqueeze(1).broadcast_to([P, NB, 4]), ALU.add)
            link(V.scalar_tensor_tensor(z8[:, :, 4:8], baf[:, :, 8:12], -1.0, srow[:, 8:12].unsqueeze(1).broadcast_to([P, NB, 4]),
                                        ALU.mult, ALU.subtract))
            V.scalar_tensor_tensor(e8[:], z8[:], -1.0, z8[:], ALU.mult, ALU.min).then_inc(sem("gate_args"), 1)

        def gates_2():
            dve.wait_ge(sem("gate_exp"), 3)
            V.tensor_scalar(e8[:], e8[:], 1.0, None, ALU.add).then_inc(sem("gate_one"), 1)
            link(V.tensor_scalar(beta[:], beta[:], 1.0, None, ALU.add))
            link(V.reciprocal(beta[:], beta[:]))
            dve.wait_ge(sem("gate_ln"), 1)
            link(V.scalar_tensor_tensor(sp8[:], z8[:], 0.0, e8[:], ALU.max, ALU.add))
            link(V.scalar_tensor_tensor(gtok[:], sp8[:, :, 0:4], -1.0, expa[:].unsqueeze(1).broadcast_to([P, NB, 4]),
                                        ALU.mult, ALU.mult))
            V.tensor_scalar(lftok[:], sp8[:, :, 4:8], -1.0, None, ALU.mult).then_inc(sem("g_ready"), 1)

        def gates_3():
            dve.wait_ge(sem("g_mm"), 1)
            link(V.tensor_copy(gcum[:].rearrange("p a b c -> p (a b c)"), PS[:, 6, 0:48]))
            V.tensor_tensor(gexp[:, 1], gcum[:, 1], gcum[:, 0], ALU.subtract)
            V.tensor_copy(gexp[:, 0], gcum[:, 0])
            V.tensor_copy(gexp[:, 2], gcum[:, 1]).then_inc(sem("g_sums"), 1)

        dve.wait_ge(sem("cin_zero"), 1)
        for e in range(12):
            bank = e % 4
            dve.wait_ge(tile_used, odd_tile(e) + 1)
            if e:
                dve.wait_ge(sem("gconv_done"), e)
            V.tensor_tensor(cin[:, GTAPS - 1:], PS[:, bank], rstd[:], ALU.mult).then_inc(evacuated, 1)
            dve.wait_ge(evacuated, E_IN1 + e + 1)
            if e >= 2:
                dve.wait_ge(sem("gsilu"), e - 1)
            link(V.tensor_scalar(hbuf[:, e % 2], cin[:, 0:S], vcol(V_GCONV + GTAPS * e), None, ALU.mult))
            for k in range(1, GTAPS):
                ins = V.scalar_tensor_tensor(hbuf[:, e % 2], cin[:, k:k + S], vcol(V_GCONV + GTAPS * e + k), hbuf[:, e % 2],
                                             ALU.mult, ALU.add)
                if k < GTAPS - 1:
                    link(ins)
                else:
                    ins.then_inc(sem("gconv_done"), 1)
            if e == HEAD_TILE:
                dve.wait_ge(tile_used, T_IN1 + HEAD_TILE + 1)
                V.tensor_tensor(hrow[0:12, :], PS[0:12, 6], rstd[0:12, :], ALU.mult).then_inc(sem("head_rows"), 1)
            if e == 5:
                gates_1()
            if e == 6:
                gates_2()
            if e == 9:
                gates_3()
        dve.wait_ge(sem("l2_mm"), 8)
        V.tensor_scalar(l2s[:].rearrange("p a b -> p (a b)"), PS[:, 7, 0:32], 1e-6, None, ALU.add).then_inc(sem("l2_ms"), 1)
        dve.wait_ge(sem("l2_root"), 1)
        link(V.reciprocal(l2s[:], l2s[:]))
        dve.wait_ge(sem("g_exp"), 3)
        V.tensor_scalar(qscal[:], l2s[:, :, 0:4], SC_FOX, None, ALU.mult)
        link(V.tensor_tensor(kscal[:, 0], l2s[:, :, 4:8], beta[:], ALU.mult))
        V.tensor_tensor(kscal[:, 1], kscal[:, 0], gexp[:, 0], ALU.mult)
        V.tensor_tensor(kscal[:, 2], l2s[:, :, 4:8], gexp[:, 1], ALU.mult).then_inc(sem("gdn_scalars"), 1)

        def gdn(i, k):
            st, j = i % 2, i // 2
            X, Y = 4 + 2 * st, 5 + 2 * st
            decay, kbT, R, NT, qkT, qe = gbufs[st]
            eg = R
            base = j * DVE_STEPS
            mine = gdn_dve[st]

            def product(step):
                dve.wait_ge(gdn_mm[st], j * PE_STEPS + step + 1)

            if k == 0:
                if j:
                    dve.wait_ge(gdn_act[st], ACT_STEPS)
                    dve.wait_ge(mine, base)
                product(0)
                V.tensor_tensor(kbT, kT[:, :, blk(i)], hd(Y), ALU.mult).then_inc(mine, 1)
                dve.wait_ge(gdn_act[st], j * ACT_STEPS + 1)
                V.tensor_tensor(decay, hd(X), per_head(gcum[:, 0, i]), ALU.subtract).then_inc(mine, 1)
                dve.wait_ge(mine, base + 2)
                V.scalar_tensor_tensor(decay, decay, 0.0, over_heads(dmask), ALU.min, ALU.add).then_inc(mine, 1)
            elif k == 1:
                product(1)
                V.tensor_tensor(qT[:, :, blk(i)], qT[:, :, blk(i)], hd(X), ALU.mult).then_inc(mine, 1)
                dve.wait_ge(mine, base + 4)
                V.tensor_tensor(qe, qT[:, :, blk(i)], eg, ALU.mult).then_inc(mine, 1)
                dve.wait_ge(gdn_act[st], j * ACT_STEPS + 2)
                V.tensor_tensor(decay, decay, per_head(l2s[:, i, 4:8]), ALU.mult).then_inc(mine, 1)
            elif k == 2:
                product(2)
                dve.wait_ge(mine, base + 6)
                V.scalar_tensor_tensor(NT, hd(Y), -1.0, decay, ALU.mult, ALU.mult).then_inc(mine, 1)
                V.tensor_tensor(qkT, hd(X), decay, ALU.mult).then_inc(mine, 1)
                V.tensor_copy(R, over_heads(ident)).then_inc(mine, 1)
                dve.wait_ge(mine, base + 9)
                V.copy_predicated(R, over_heads(lmask[LEVELS[0]]), NT).then_inc(mine, 1)
            elif STEP_Z1 <= k < STEP_W and (k - STEP_Z1) % 3 == 1:
                n = (k - STEP_Z1) // 3 + 1
                product(k)
                V.copy_predicated(R, over_heads(lmask[LEVELS[n]]), hd(Y)).then_inc(mine, 1)
            elif k == STEP_S:
                product(STEP_O)
                V.tensor_tensor(St_b, St_b, per_head(gexp[:, 2, i]), ALU.mult).then_inc(mine, 1)
                product(k)
                dve.wait_ge(mine, base + 17)
                V.tensor_tensor(St_b, St_b, hd(Y), ALU.add).then_inc(mine, 1)

        dve.wait_ge(sem("state_zero"), 1)
        for kind, a, b in odd_order():
            if kind == "gdn":
                gdn(a, b)
            elif kind == "evac":
                bank = a % 4
                if a < 20:
                    dve.wait_ge(tile_used, odd_tile(a) + 1)
                    dst = qd[:, a - 12] if a < 16 else kd[:, a - 16]
                    V.scalar_tensor_tensor(dst, PS[:, bank], SC_FOX if a < 16 else 1.0, rstd[:], ALU.mult, ALU.mult).then_inc(evacuated, 1)
                elif a == 23:
                    dve.wait_ge(tile_used, odd_tile(23) + 1)
                    for c in range(NB):
                        V.tensor_scalar(vd[:, c], PS[:, c], rtok[:, c:c + 1], None, ALU.mult).then_inc(evacuated, 1)
                elif a >= 24:
                    dve.wait_ge(tile_used, odd_tile(a) + 1)
                    V.tensor_tensor(zT[:, a - 24], PS[:, bank], rstd[:], ALU.mult).then_inc(evacuated, 1)
        token_stat(2, 4, 1.0 / P, 1e-6)
        for h in range(H):
            dve.wait_ge(sem("stat_bc"), 4 + h + 1)
            link(V.scalar_tensor_tensor(qT[:, h], qT[:, h], vcol(V_GNORM), PS[:, h], ALU.mult, ALU.mult))
            dve.wait_ge(sem("z_silu"), h + 1)
            V.tensor_tensor(qT[:, h], qT[:, h], zT[:, h], ALU.mult).then_inc(sem("gy_ready"), 1)
        for h in range(H):
            y_lo(8 + h + 1, h, qT[:, h])
        for h in range(H):
            dve.wait_ge(sem("fox_cb_mm"), h + 1)
            V.tensor_copy(cb[:, h], PS[:, h]).then_inc(sem("fox_cb"), 1)

        def fox_min(u):
            h, i = UNITS[u]
            n = (i + 1) * P
            dve.wait_ge(sem("fox_s"), u + 1)
            if u >= 2:
                dve.wait_ge(sem("fox_exp"), u - 1)
            link(V.scalar_tensor_tensor(tbuf[:, u % 2, 0:n], cb[:, h, 0:n], gcum[:, 2, i, h:h + 1], PS[:, 4 + u % 2, 0:n],
                                        ALU.subtract, ALU.subtract))
            V.tensor_reduce(amax[:, 0, u % 2:u % 2 + 1], tbuf[:, u % 2, 0:n], AX.X, ALU.min).then_inc(sem("fox_min"), 1)

        def fox_scale(u):
            h, i = UNITS[u]
            n = (i + 1) * P
            dve.wait_ge(sem("fox_exp"), u + 1)
            link(V.reciprocal(arec[:, 0, u % 2:u % 2 + 1], asum[:, 0, u % 2:u % 2 + 1]))
            V.tensor_scalar(fbuf[:, u % 2, 0:n], fbuf[:, u % 2, 0:n], arec[:, 0, u % 2:u % 2 + 1], None, ALU.mult).then_inc(sem("fox_p"), 1)

        dve.wait_ge(sem("fox_cb"), H)
        fox_min(0)
        for u, (h, i) in enumerate(UNITS):
            fox_scale(u)
            if u + 1 < len(UNITS):
                fox_min(u + 1)
            if (i == 1 and h) or u == len(UNITS) - 1:
                g = h if u == len(UNITS) - 1 else h - 1
                y_lo(12 + g + 1, 4 + g, PS[:, g % 2])
        out_proj(3, T_OUT1, E_OUT1)
        norm_finish(3, 7)
        ffn(1, T_GU1, E_GU1, True)
        down(4, T_DN1, E_DN1)
        norm_finish(4, 7)
        for n in range(KD):
            V.scalar_tensor_tensor(outT[:, n], xT[:, n], vcol(V_NORM + KD * FINAL + n), rstd[:], ALU.mult, ALU.mult).then_inc(sem("out_ready"), 1)

    @block.tensor
    def _(pe):
        def mm(out, lhsT, rhs, start=True, stop=True):
            return nc.tensor.matmul(out, lhsT, rhs, start=start, stop=stop)

        def product(out, w, x, start, stop):
            mm(out, w[0], x[0], start, False)
            mm(out, w[0], x[1], False, False)
            return mm(out, w[1], x[0], False, stop)

        def wpair(slot, cols):
            return wring[:, slot, 0, cols], wring[:, slot, 1, cols]

        def arrived(t):
            pe.wait_ge(hi_ready[t % RING], slot_round(t))
            pe.wait_ge(lo_ready[t % RING], slot_round(t))

        def stationary(t, e, src, feed=None):
            arrived(t)
            if e >= 4:
                pe.wait_ge(evacuated, e - 3)
            for k in range(KD):
                if feed is not None:
                    pe.wait_ge(h_ready, feed + k + 1)
                last = product(PS[:, e % 4], wpair(t % RING, blk(k)), (src[:, k, 0], src[:, k, 1]), k == 0, k == KD - 1)
            last.then_inc(tile_used, 1)

        def moving(t0, e0):
            for j in range(4):
                arrived(t0 + j)
                for m in range(2):
                    k = 2 * j + m
                    w = wpair((t0 + j) % RING, slice(m * S, (m + 1) * S))
                    for b in range(NB):
                        if k == 0:
                            pe.wait_ge(evacuated, e0 + b - 3)
                        last = product(PS[:, (e0 + b) % 4], (HH[:, k, 0, blk(b)], HH[:, k, 1, blk(b)]), w, k == 0, k == KD - 1)
                last.then_inc(tile_used, 1)

        def token_sum(out, src, k=0, n=1):
            return mm(out, src, ones[:, 0:1], k == 0, k == n - 1)

        def spread(out, col):
            return mm(out, col.to_broadcast([P, P]), ident)

        def norm_stats(s, bank):
            pe.wait_ge(ssq_done, 7 * (s + 1))
            for b in range(NB):
                last = token_sum(PS[:, bank, b:b + 1], ssq[:, blk(b)])
            last.then_inc(norm_sum, 1)

        def norm_spread(s, bank):
            pe.wait_ge(norm_tok, s + 1)
            for b in range(NB):
                last = spread(PS[:, bank, blk(b)], rtok[:, b:b + 1])
            last.then_inc(norm_bc, 1)

        pe.wait_ge(const_loaded, 16)
        for e in range(16):
            if e == 1:
                norm_stats(0, 7)
            if e == 2:
                norm_spread(0, 7)
            if e == 3:
                pe.wait_ge(sem("lam_prod"), 2)
                mm(PS[:, 6, 0:2], ones[0:64, :], lam[0:64, 0:2]).then_inc(sem("lam_sum"), 1)
            stationary(T_IN0 + e, E_IN0 + e, HH, feed=0 if e == 0 else None)

            def rope_mm(j):
                pe.wait_ge(rope_loaded, 16)
                pe.wait_ge(evacuated, 8 + j + 1)
                if j >= 2:
                    pe.wait_ge(sem("rope_sin"), j - 1)
                mm(PS[:, 4 + j % 2], rope[:, 2 * S:], hbuf[:, j % 2]).then_inc(sem("rope_mm"), 1)

            if e >= 9:
                rope_mm(e - 9)
        rope_mm(7)
        moving(T_IN0 + 16, E_IN0 + 16)

        def diff_scores(u):
            h, i = UNITS[u]
            n = (i + 1) * P
            if u >= 2:
                pe.wait_ge(sem("diff_exp"), 2 * (u - 1))
            for m in range(2):
                bank = 4 + 2 * (u % 2) + m
                part = slice(64 * m, 64 * m + 64)
                mm(PS[:, bank, 0:n], qk[part, h, blk(i)], qk[part, 4 + h, 0:n], True, False)
            for m in range(2):
                bank = 4 + 2 * (u % 2) + m
                last = mm(PS[:, bank, blk(i)], ident, cmask, False, True)
            last.then_inc(sem("diff_s"), 1)

        def transpose_w(u, src, bank):
            h, i = UNITS[u]
            for j in range(i + 1):
                last = nc.tensor.transpose(PS[:, bank, blk(j)], src[:, u % 2, blk(j)], ident)
            return last

        def weighted_values(h, wt, v, bank):
            for j in range(NB):
                last = mm(PS[:, bank, j * P:S], v[:, j, blk(h)], wt[:, h % 2, j, j * P:S], j == 0, j == NB - 1)
            return last

        def diff_values(h):
            pe.wait_ge(sem("diff_wt"), NB * (h + 1))
            if h:
                pe.wait_ge(sem("diff_osq"), h)
            weighted_values(h, WT, vtk, 2).then_inc(sem("diff_pv"), 1)

        pe.wait_ge(sem("qk_ready"), 8)
        pe.wait_ge(evacuated, 20)
        diff_scores(0)
        for u, (h, i) in enumerate(UNITS):
            if u + 1 < len(UNITS):
                diff_scores(u + 1)
            if u == 1:
                pe.wait_ge(sem("conv_done"), 4)
                for b in range(NB):
                    for c in range(4):
                        last = token_sum(PS[:, 3, b:b + 1], cacc[:, c, blk(b)], c, 4)
                last.then_inc(sem("ln_mean_mm"), 1)
            if u == 3:
                pe.wait_ge(sem("ln_mean"), 1)
                for b in range(NB):
                    last = spread(PS[:, 3, blk(b)], lst[:, b:b + 1])
                last.then_inc(sem("ln_mean_bc"), 1)
            if u == 5:
                pe.wait_ge(sem("ln_sq"), 4)
                for b in range(NB):
                    for c in range(4):
                        last = token_sum(PS[:, 3, b:b + 1], upad[:, c, blk(b)], c, 4)
                last.then_inc(sem("ln_var_mm"), 1)
            if u == 8:
                pe.wait_ge(sem("ln_rstd"), 1)
                for b in range(NB):
                    last = spread(PS[:, 3, blk(b)], lst[:, 4 + b:5 + b])
                last.then_inc(sem("ln_rstd_bc"), 1)
            if i == 0 and h:
                diff_values(h - 1)
            pe.wait_ge(sem("diff_w"), u + 1)
            if u >= 2:
                pe.wait_ge(sem("diff_wt"), u - 1)
            transpose_w(u, wbuf, u % 2).then_inc(sem("diff_t"), 1)
        diff_values(H - 1)
        pe.wait_ge(sem("diff_osq"), H)
        pe.wait_ge(sem("ln_scaled"), 4)
        for b in range(NB):
            for h in range(H):
                last = token_sum(PS[:, 3, 4 * h + b:4 * h + b + 1], osq[:, h, blk(b)])
        last.then_inc(sem("stat_mm"), 1)
        pe.wait_ge(sem("stat_rec"), 1)
        for h in range(H):
            for b in range(NB):
                last = spread(PS[:, 4 + h, blk(b)], ost[:, 1, 4 * h + b:4 * h + b + 1])
            last.then_inc(sem("stat_bc"), 1)
        pe.wait_ge(y_ready, KD)
        for n in range(KD):
            stationary(T_OUT0 + n, E_OUT0 + n, AA)

        def ffn(s, tg, eg, norm):
            for j in range(RING):
                stationary(tg + j, eg + j, HH, feed=KD * norm if j == 0 else None)
                if j == 0:
                    norm_stats(norm, 7)
                if j == 1:
                    norm_spread(norm, 7)
            with pe.Fori(1, KF // 2) as r:
                for j in range(RING):
                    t = tg + j
                    slot = t % RING
                    pe.wait_ge(hi_ready[slot], r + slot_round(t))
                    pe.wait_ge(lo_ready[slot], r + slot_round(t))
                    pe.wait_ge(evacuated, r * RING + (eg + j - 3))
                    for k in range(KD):
                        last = product(PS[:, j], wpair(slot, blk(k)), (HH[:, k, 0], HH[:, k, 1]), k == 0, k == KD - 1)
                    last.then_inc(tile_used, 1)
            td = tg + 2 * KF
            pe.wait_ge(evacuated, eg + 2 * KF)
            for k in range(RING):
                arrived(td + k)
                pe.wait_ge(sem("ffn_lo"), KF * s + k + 1)
                for n in range(KD):
                    last = product(PS[:, n], wpair((td + k) % RING, blk(n)), (AA[:, k, 0], AA[:, k, 1]), k == 0, False)
                last.then_inc(tile_used, 1)
            with pe.Fori(1, KF // RING) as r:
                for j in range(RING):
                    t = td + j
                    pe.wait_ge(hi_ready[t % RING], r + slot_round(t))
                    pe.wait_ge(lo_ready[t % RING], r + slot_round(t))
                    pe.wait_ge(sem("ffn_lo"), r * RING + (KF * s + j + 1))
                    a = [AA[:, bass.ds(r * RING + j, 1), m].rearrange("p a b -> p (a b)") for m in range(2)]
                    for n in range(KD):
                        last = product(PS[:, n], wpair(t % RING, blk(n)), a, False, False)
                    last.then_inc(tile_used, 1)
            rest = range(KF // RING * RING, KF)
            for k in rest:
                arrived(td + k)
            pe.wait_ge(sem("ffn_lo"), KF * (s + 1))
            for n in range(KD):
                for k in rest:
                    last = product(PS[:, n], wpair((td + k) % RING, blk(n)), (AA[:, k, 0], AA[:, k, 1]), False, k == KF - 1)
                    if n == KD - 1:
                        last.then_inc(tile_used, 1)
                if n < KD - 1:
                    last.then_inc(down_done, 1)

        ffn(0, T_GU0, E_GU0, 1)

        def tok_transpose(m):
            pe.wait_ge(sem("gsilu"), m + 5)
            if m >= 2:
                pe.wait_ge(sem("tok_ready"), m - 1)
            src = kT[:, m] if m < H else sqb[:, m % 2]
            for b in range(NB):
                last = nc.tensor.transpose(PS[:, 4 + m % 2, blk(b)], src[:, blk(b)], ident)
            last.then_inc(sem("tok_t"), 1)

        for e in range(12):
            stationary(odd_tile(e), E_IN1 + e, HH, feed=2 * KD if e == 0 else None)
            if e == 0:
                norm_stats(2, 7)
            if e == 1:
                norm_spread(2, 7)
            if e == HEAD_TILE - 1:
                arrived(T_IN1 + HEAD_TILE)
                for k in range(KD):
                    last = product(PS[:, 6], wpair((T_IN1 + HEAD_TILE) % RING, blk(k)), (HH[:, k, 0], HH[:, k, 1]), k == 0, k == KD - 1)
                last.then_inc(tile_used, 1)
            if e == HEAD_TILE:
                pe.wait_ge(small_loaded, 16)
                pe.wait_ge(sem("head_rows"), 1)
                mm(PS[:, 6, 64:76], ones[0:1, :], rowv[0:1, :])
                for b in range(NB):
                    last = nc.tensor.transpose(PS[:, 6, 12 * b:12 * b + 12], hrow[0:12, blk(b)], ident[0:12, 0:12])
                last.then_inc(sem("baf_mm"), 1)
            if 4 <= e < 12:
                c = e - 4
                pe.wait_ge(sem("gsq"), c + 1)
                for b in range(NB):
                    last = token_sum(PS[:, 7, 8 * b + c:8 * b + c + 1], sqb[:, c % 2, blk(b)])
                last.then_inc(sem("l2_mm"), 1)
            if e == 8:
                pe.wait_ge(sem("g_ready"), 1)
                g_all = gtok[:].rearrange("p a b -> p (a b)")
                mm(PS[:, 6, 0:16], cums, g_all)
                mm(PS[:, 6, 16:32], ones, g_all)
                for b in range(NB):
                    for j in range(b + 1):
                        last = mm(PS[:, 6, 32 + 4 * b:36 + 4 * b], cums if j == b else ones, lftok[:, j], j == 0, j == b)
                last.then_inc(sem("g_mm"), 1)
            if e >= 7:
                tok_transpose(e - 7)
        for m in range(5, 8):
            tok_transpose(m)

        def heads(out_bank, lhs, rhs):
            for h in range(H):
                last = mm(PS[:, out_bank, blk(h)], lhs(h), rhs(h))
            return last

        def gdn(i, k):
            st, j = i % 2, i // 2
            X, Y = 4 + 2 * st, 5 + 2 * st
            decay, kbT, R, NT, qkT, qe = gbufs[st]
            Z, T, wT, vn, kbe = decay, kbT, kbT, decay, NT

            def dve_done(n):
                pe.wait_ge(gdn_dve[st], j * DVE_STEPS + n)

            def act_done(n):
                pe.wait_ge(gdn_act[st], j * ACT_STEPS + n)

            if k == 0:
                if j:
                    dve_done(0)
                    act_done(0)
                for h in range(H):
                    spread(PS[:, X, blk(h)], gcum[:, 0, i, h:h + 1])
                    last = spread(PS[:, Y, blk(h)], kscal[:, 0, i, h:h + 1])
            elif k == 1:
                dve_done(2)
                for h in range(H):
                    last = spread(PS[:, X, blk(h)], qscal[:, i, h:h + 1])
            elif k == 2:
                dve_done(5)
                heads(Y, lambda h: kT[:, h, blk(i)], lambda h: kbT[:, h])
                last = heads(X, lambda h: kT[:, h, blk(i)], lambda h: qT[:, h, blk(i)])
            elif k < STEP_W:
                n, what = ((k - STEP_Z1) // 3 + 1, (k - STEP_Z1) % 3) if k > STEP_T0 else (0, 2)
                if what == 0:
                    act_done(3 + 2 * (n - 1))
                    last = heads(X, lambda h: NT[:, h], lambda h: T[:, h])
                elif what == 1:
                    act_done(4 + 2 * (n - 1))
                    last = heads(Y, lambda h: Z[:, h], lambda h: R[:, h])
                else:
                    dve_done(10 + n)
                    for h in range(H):
                        last = nc.tensor.transpose(PS[:, X, blk(h)], R[:, h], ident)
            elif k == STEP_W:
                dve_done(16)
                pe.wait_ge(gdn_pool[st], j * POOL_STEPS + 2)
                last = heads(X, lambda h: kbe[:, h], lambda h: R[:, h])
            elif k == STEP_V:
                act_done(15)
                pe.wait_ge(sem("state_zero"), 1)
                if i:
                    pe.wait_ge(gdn_dve[(i - 1) % 2], ((i - 1) // 2 + 1) * DVE_STEPS)
                for h in range(H):
                    mm(PS[:, Y, blk(h)], R[:, h], vtok[:, i, h], True, False)
                    last = mm(PS[:, Y, blk(h)], wT[:, h], St_b[:, h], False, True)
            elif k == STEP_O:
                act_done(16)
                for h in range(H):
                    mm(PS[:, X, blk(h)], St_b[:, h], qe[:, h], True, False)
                    last = mm(PS[:, X, blk(h)], vn[:, h], qkT[:, h], False, True)
            elif k == STEP_S:
                pe.wait_ge(gdn_pool[st], j * POOL_STEPS + 3)
                last = heads(Y, lambda h: ktok[:, i, h], lambda h: vn[:, h])
            last.then_inc(gdn_mm[st], 1)

        def tile_part(e, part):
            t = odd_tile(e)
            if part == 0:
                arrived(t)
            if 20 <= e < 24:
                k = 2 * (e - 20) + part // 2
                w = wpair(t % RING, slice(k % 2 * S, (k % 2 + 1) * S))
                for b in (0, 1) if part % 2 == 0 else (2, 3):
                    if k == 0:
                        pe.wait_ge(evacuated, E_IN1 + 20 + b - 3)
                    last = product(PS[:, b], (HH[:, k, 0, blk(b)], HH[:, k, 1, blk(b)]), w, k == 0, k == KD - 1)
            else:
                if part == 0:
                    pe.wait_ge(evacuated, E_IN1 + e - 3)
                for k in (2 * part, 2 * part + 1):
                    last = product(PS[:, e % 4], wpair(t % RING, blk(k)), (HH[:, k, 0], HH[:, k, 1]), k == 0, k == KD - 1)
            if part == 3:
                last.then_inc(tile_used, 1)

        pe.wait_ge(sem("gdn_scalars"), 1)
        pe.wait_ge(sem("tok_ready"), 8)
        for kind, a, b in odd_order():
            if kind == "gdn":
                gdn(a, b)
            elif kind == "tile":
                tile_part(a, b)
        pe.wait_ge(sem("gdn_osq"), H)
        for b in range(NB):
            for h in range(H):
                last = token_sum(PS[:, 4, 4 * h + b:4 * h + b + 1], gsq[:, h, blk(b)])
        last.then_inc(sem("stat_mm"), 1)
        pe.wait_ge(sem("stat_rec"), 2)
        pe.wait_ge(evacuated, E_OUT1)
        for h in range(H):
            for b in range(NB):
                last = spread(PS[:, h, blk(b)], ost[:, 1, 4 * h + b:4 * h + b + 1])
            last.then_inc(sem("stat_bc"), 1)

        pe.wait_ge(sem("gy_ready"), H)
        for h in range(H):
            for b in range(NB):
                last = spread(PS[:, h, blk(b)], gcum[:, 2, b, h:h + 1])
            last.then_inc(sem("fox_cb_mm"), 1)

        def fox_scores(u):
            h, i = UNITS[u]
            n = (i + 1) * P
            if u >= 2:
                pe.wait_ge(sem("fox_min"), u - 1)
            mm(PS[:, 4 + u % 2, 0:n], qd[:, h, blk(i)], kd[:, h, 0:n], True, False)
            mm(PS[:, 4 + u % 2, blk(i)], ident, cmask, False, True).then_inc(sem("fox_s"), 1)

        def fox_values(h):
            pe.wait_ge(sem("fox_wt"), NB * (h + 1))
            if h >= 2:
                pe.wait_ge(y_ready, 12 + h - 1)
            weighted_values(h, FT, vd, h % 2).then_inc(sem("fox_pv"), 1)

        fox_scores(0)
        pe.wait_ge(sem("fox_cb"), H)
        for u, (h, i) in enumerate(UNITS):
            if u + 1 < len(UNITS):
                fox_scores(u + 1)
            if i == 0 and h:
                fox_values(h - 1)
            pe.wait_ge(sem("fox_p"), u + 1)
            if u >= 2:
                pe.wait_ge(sem("fox_wt"), u - 1)
            transpose_w(u, fbuf, 6 + u % 2).then_inc(sem("fox_t"), 1)
        fox_values(H - 1)
        pe.wait_ge(y_ready, 2 * KD)
        for n in range(KD):
            stationary(T_OUT1 + n, E_OUT1 + n, AA)
        ffn(1, T_GU1, E_GU1, 3)
        norm_stats(4, 7)
        norm_spread(4, 7)

    block.__exit__(None, None, None)


def kernel(x, mix_norm_w, ffn_norm_w, final_norm_w, w_in_even, conv_w, conv_b, conv_ln_w, conv_ln_b,
           lambda_q1, lambda_k1, lambda_q2, lambda_k2, diff_subln_w, gdn_conv_w, w_in_odd,
           gdn_a_log, gdn_dt_bias, gdn_norm_w, fox_forget_bias, w_out, w_gate, w_up, w_down):
    import concourse.bacc as bacc
    from concourse.bass_utils import run_bass_kernel_spmd

    f = np.asarray

    def chunks(w):
        k, n = w.shape
        return w.reshape(k // P, P, n // P, P).transpose(2, 1, 0, 3).reshape(n // P, P, k // P * P)

    def movers(w):
        return w.reshape(4, 2, P, S).transpose(0, 2, 1, 3).reshape(4, P, 2 * S)

    def ffn_tiles(l):
        gu = np.stack([chunks(f(w_gate)[l]), chunks(f(w_up)[l])], axis=1)
        return [gu.reshape(2 * KF, P, TILE), f(w_down)[l].reshape(KF, P, TILE)]

    we, wo = f(w_in_even)[0], f(w_in_odd)[0]
    heads = np.zeros((D, P), np.float32)
    heads[:, 0:8], heads[:, 8:12] = wo[:, 2048:2056], wo[:, 3592:3596]
    heads = chunks(heads)
    val_gate = np.stack([chunks(we[:, 0:512]), chunks(we[:, 512:1024])], axis=1).reshape(8, P, TILE)
    stream = np.ascontiguousarray(np.concatenate(
        [val_gate, chunks(we[:, 1024:2048]), movers(we[:, 2048:2560]), chunks(f(w_out)[0])] + ffn_tiles(0)
        + [chunks(wo[:, 0:512]), heads, chunks(wo[:, 512:1536]), chunks(wo[:, 2056:3080]), movers(wo[:, 3080:3592]), chunks(wo[:, 1536:2048]),
           chunks(f(w_out)[1])] + ffn_tiles(1)))
    assert stream.shape == (N_TILES, P, TILE)
    def cols(v):
        v = f(v)
        v = v.reshape(v.shape[0] // P, P, -1)
        return v.transpose(1, 0, 2).reshape(P, -1)

    norms = [cols(w) for w in (f(mix_norm_w)[0], f(ffn_norm_w)[0], f(mix_norm_w)[1], f(ffn_norm_w)[1], f(final_norm_w))]
    lams = np.zeros((P, 4), np.float32)
    for n, v in enumerate((lambda_q1, lambda_k1, lambda_q2, lambda_k2)):
        lams[0:64, n] = f(v)[0]
    vecs = np.ascontiguousarray(np.concatenate(
        norms + [cols(f(conv_w)[0].T), cols(f(conv_b)[0]), cols(f(conv_ln_w)[0]), cols(f(conv_ln_b)[0]),
                 cols(f(diff_subln_w)[0]), cols(f(gdn_conv_w)[0].T), cols(f(gdn_norm_w)[0]), lams], axis=1))
    assert vecs.shape == (P, N_VEC)
    row = np.concatenate([f(gdn_a_log)[0], f(gdn_dt_bias)[0], f(fox_forget_bias)[0]]).reshape(1, 12)
    xt = np.ascontiguousarray(f(x)[0].T.reshape(KD, P, S).transpose(1, 0, 2))
    const, rope = shape_constants()

    nc = bacc.Bacc("TRN2", target_bir_lowering=False, num_devices=1)
    f32 = mybir.dt.float32
    arrays = {"x_t": xt, "w_stream": stream, "vectors": vecs, "row": row,
              "shape_const": const, "rope_const": rope}
    args = [nc.dram_tensor(n, a.shape, f32, kind="ExternalInput").ap() for n, a in arrays.items()]
    out = nc.dram_tensor("out_t", (P, KD, S), f32, kind="ExternalOutput").ap()
    build(nc, *args, out)
    r = run_bass_kernel_spmd(nc, [arrays], core_ids=[0])
    got = r.results[0]["out_t"]
    return np.ascontiguousarray(got.transpose(2, 1, 0).reshape(1, S, D))
```

```python
import math

import numpy as np
import concourse.bass as bass
from concourse import mybir

P = 128
S = 512
D = 1024
NB = S // P
KD = D // P
FF = 2816
KF = FF // P
H = 4
TAPS, GTAPS = 31, 4
TILE = 1024
BIG = -1.0e30

T_IN0 = 0
T_OUT0 = T_IN0 + 20
T_GU0 = T_OUT0 + KD
T_DN0 = T_GU0 + 2 * KF
T_IN1 = T_DN0 + KF
T_OUT1 = T_IN1 + 29
T_GU1 = T_OUT1 + KD
T_DN1 = T_GU1 + 2 * KF
N_TILES = T_DN1 + KF
E_IN0 = 0
E_OUT0 = E_IN0 + 20
E_GU0 = E_OUT0 + KD
E_DN0 = E_GU0 + 2 * KF
E_IN1 = E_DN0 + KD
E_OUT1 = E_IN1 + 28
E_GU1 = E_OUT1 + KD
E_DN1 = E_GU1 + 2 * KF
HEAD_TILE = 4
RING = 4
HI_AFTER = (1, 5, 6, 7)
RAW = 2
LATE = KF % RING

V_NORM = 0
V_CONVW = 40
V_CONVB = V_CONVW + 4 * TAPS
V_LNW = V_CONVB + 4
V_LNB = V_LNW + 4
V_SUBLN = V_LNB + 4
V_GCONV = V_SUBLN + 1
V_GNORM = V_GCONV + 12 * GTAPS
V_LAM = V_GNORM + 1
N_VEC = V_LAM + 4
OUT_DVE = 5
SHARED = 8
PROD = 8
POOL_TAPS_V, POOL_TAPS = 2, 4
TAPS_VAL, TAPS_V, TAPS_QK, TAPS_UNIT, TAPS_LATE = 6, 5, 4, 5, 4
LN_FROM = 8
LAG = 6
FILL_STEPS = 75
FOX_RATE = 1.5
NORM_EVERY = 2
LEVELS = [1, 2, 4, 8, 16, 32, 64]


def odd_tile(e):
    return T_IN1 + e + (1 if e >= HEAD_TILE else 0)


PE_STEPS, ACT_STEPS, DVE_STEPS, POOL_STEPS = 25, 17, 18, 3
STEP_T0, STEP_Z1, STEP_W, STEP_V, STEP_O, STEP_S = 3, 4, 21, 22, 23, 24


def even_order():
    def tile(j, rope=None, extra=()):
        out = []
        for part in range(4):
            out.append(("qk", (j, part)))
            if part == 0 and rope is not None:
                out += [("taps", 1), ("rope", rope)]
            out += extra[part] if extra else []
        return out + [("qk_evac", j)]

    order = [("val_gate", c) for c in range(4)]
    for j in range(4):
        order += [("v", j), ("taps", TAPS_V)]
    order.append(("v_evac", 0))
    order += tile(0) + [("taps", TAPS_QK)] + tile(1, 0) + tile(2, 1, [[], [("diff_s", 0)], [("diff_s", 1), ("diff_m", 0)], [("diff_m", 1)]]) + [("taps", TAPS_QK)]
    late = [("ln_add", 0), None, None, ("ln_sum", 0), None] + [("ln_centre", c) for c in range(4)] + [
        None, ("ln_var_sum", 0), None, ("ln_var", 0), ("ln_root", 0), None, ("ln_rec", 0), ("ln_bc", 0), None] + [
        ("ln_scale", c) for c in range(4)]
    for u in range(H * NB - 2):
        more = u + 2 < H * NB
        first = [("diff_w", u)]
        if u < 5:
            order += first + tile(u + 3, u + 2, [[("taps", TAPS_UNIT)], [("diff_t", u)], [("diff_s", u + 2)], [("diff_m", u + 2)]])
        elif u == 5:
            order += first + [("rope", 7), ("diff_s", u + 2), ("diff_t", u), ("diff_m", u + 2), ("taps", TAPS_LATE)]
        else:
            if u == LN_FROM:
                order.append(("taps", 4 * TAPS))
            for item in [("diff_s", u + 2)] * more + first + [("diff_t", u)] + [("diff_m", u + 2)] * more:
                order.append(item)
                if u >= LN_FROM and late:
                    order.append(late.pop(0))
            if u < LN_FROM:
                order.append(("taps", TAPS_LATE))
        if u in (6, 9, 13):
            order.append(("diff_v", {6: 0, 9: 1, 13: 2}[u]))
    order += late + [("diff_w", 14), ("sub_sum", 0), ("diff_t", 14), ("sub_ms", 0), ("diff_w", 15), ("sub_root", 0), ("sub_rec", 0),
                     ("diff_t", 15), ("sub_bc", 0), ("diff_v", 3), ("sub_mul", 0), ("sub_bc", 1), ("sub_hi", 0), ("sub_mul", 1), ("sub_hi", 1),
                     ("sub_sum", 1), ("sub_ms", 1), ("sub_root", 1), ("sub_bc", 2), ("sub_mul", 2), ("sub_hi", 2), ("sub_rec", 1), ("sub_bc", 3),
                     ("sub_lo", 0), ("sub_lo", 1), ("sub_lo", 2), ("conv_silu", 0), ("sub_mul", 3)]
    order += [("conv_lo", c) for c in range(4)] + [("sub_hi", 3), ("sub_lo", 3)]
    out, m = [], 0
    for item in order:
        if item:
            out.append(item)
            n = POOL_TAPS_V if item[0] == "v" else POOL_TAPS if item[0] == "qk" and item[1][1] == 1 else 0
            if n and m < SHARED + TAPS:
                out.append(("shared_taps", (m, min(m + n, SHARED + TAPS))))
                m = min(m + n, SHARED + TAPS)
    assert m == SHARED + TAPS
    return out


def fox_order():
    order = [("fox_cb", 0), ("fox_s", 0), ("fox_s", 1), ("fox_m", 0), ("fox_m", 1)]
    for u in range(H * NB):
        h, i = u // NB, u % NB
        if i == 1 and h < H - 1:
            order.append(("fox_cb", h + 1))
        if u + 2 < H * NB:
            order.append(("fox_s", u + 2))
        order += [("fox_p", u), ("fox_t", u)]
        if u + 2 < H * NB:
            order.append(("fox_m", u + 2))
        if i == 0 and h:
            order.append(("fox_v", h - 1))
    return order + [("fox_v", H - 1)]


def odd_order():
    def tile(e):
        return [("tile", (e, part)) for part in range(4)] + [("evac", e)]

    streams = [[(i, k) for i in (n, n + 2) for k in range(PE_STEPS)] for n in range(2)]
    gdn = []
    for r in range(2 * PE_STEPS + LAG):
        if r < 2 * PE_STEPS:
            gdn.append(("gdn", streams[0][r]))
        if r >= LAG:
            gdn.append(("gdn", streams[1][r - LAG]))
    first = tile(12)
    order = [("l2", 0), ("tok", 6)] + first + [("tok", 7)]
    fill = [item for e in range(13, 28) for item in tile(e)] + [("z_silu", h) for h in range(H)]
    fox = fox_order()
    nf = nx = 0
    for n, step in enumerate(gdn):
        order.append(step)
        while nf < len(fill) and nf < (n + 1) * len(fill) / FILL_STEPS:
            order.append(fill[nf])
            nf += 1
        while nf == len(fill) and nx < len(fox) and nx < (n + 1 - FILL_STEPS) * FOX_RATE:
            order.append(fox[nx])
            nx += 1
    norm = [("norm_sq", 0), ("norm_sum", 0), ("norm_ms", 0), ("norm_root", 0), ("norm_rec", 0), ("norm_bc", 0)] + [
        ("norm_mul", 0), ("norm_mul", 1), ("norm_hi", 0), ("norm_mul", 2), ("norm_hi", 1), ("norm_lo", 0), ("norm_mul", 3),
        ("norm_hi", 2), ("norm_lo", 1), ("norm_hi", 3), ("norm_lo", 2), ("norm_lo", 3)]
    rest = fox[nx:]
    for n, item in enumerate(rest):
        if n % NORM_EVERY == 0 and norm:
            order.append(norm.pop(0))
        order.append(item)
    return order + norm

LAMBDA_INIT = 0.8 - 0.6 * math.exp(-0.3 * 0)


def shape_constants():
    r = np.arange(P)
    row, col = r[:, None], r[None, :]
    parts = [
        np.eye(P),
        (row <= col) * 1.0,
        np.ones((P, P)),
        np.where(col > row, BIG, 0.0),
        np.where(row > col, BIG, 0.0),
    ]
    for b in LEVELS:
        parts.append(((row // (2 * b) == col // (2 * b)) & (row % (2 * b) < b) & (col % (2 * b) >= b)) * 1.0)
    const = np.concatenate(parts, axis=1).astype(np.float32)
    half = 8
    inv = (1.0 / (np.float32(500000.0) ** (np.arange(half, dtype=np.float32) / half))).astype(np.float32)
    ang = np.arange(S, dtype=np.float32)[:, None] * inv[None, :]
    cos, sin = np.cos(ang).astype(np.float32).T, np.sin(ang).astype(np.float32).T
    rc, rs, perm = np.ones((P, S)), np.zeros((P, S)), np.zeros((P, P))
    for p in range(P):
        q = p % 64
        if q < half:
            rc[p], rs[p], perm[p + half, p] = cos[q], -sin[q], 1.0
        elif q < 2 * half:
            rc[p], rs[p], perm[p - half, p] = cos[q - half], sin[q - half], 1.0
    rope = np.concatenate([rc, rs, perm], axis=1).astype(np.float32)
    return const, rope


def build(nc, x_d, w_d, vec_d, row_d, const_d, rope_d, out_d):
    f32, f32r, i32, bf16 = mybir.dt.float32, mybir.dt.float32r, mybir.dt.int32, mybir.dt.bfloat16
    ALU, ACT, AX = mybir.AluOpType, mybir.ActivationFunctionType, mybir.AxisListType
    DH = 128
    SC_FOX = float(DH) ** -0.5
    SC_DIFF = 0.125

    size = {f32: 4, f32r: 4, bf16: 2}

    def at(name, shape, dt, offset):
        t = nc.alloc_sbuf_tensor_at(name, [P] + list(shape), dt, offset=offset)
        return t, offset + (int(np.prod(shape)) * size[dt] + 31) // 32 * 32

    base = 16512
    xT, p = at("xT", [KD, S], f32, base)
    raw, p = at("raw", [RAW, TILE], f32, p)
    wring, p = at("wring", [RING, 2, TILE], f32r, p)
    at_H = p
    HH, p = at("HH", [KD, 2, S], f32r, p)
    consts, p = at("consts", [5 + len(LEVELS), P], f32, p)
    at_work = p
    hbuf, p = at("hbuf", [2, S], f32, p)
    sqb, p = at("sqb", [2, S], f32, p)
    ssq, p = at("ssq", [S], f32, p)
    rstd, p = at("rstd", [S], f32, p)
    vec, p = at("vec", [N_VEC], f32, p)
    at_small = p
    p += 2848
    at_A = p
    AA, p = at("AA", [KF, 2, S], f32r, p)
    gbuf, p = at("gbuf", [2, S], f32, p)
    ubuf, p = at("ubuf", [2, S], f32, p)
    abuf, p = at("abuf", [S], f32, p)
    TOP = 229344
    assert p <= TOP, p
    q = at_small
    mask16, q = at("mask16", [2, P], bf16, q)
    rtok, q = at("rtok", [NB], f32, q)
    nst, q = at("nst", [NB], f32, q)
    lam, q = at("lam", [8], f32, q)
    lst, q = at("lst", [8], f32, q)
    amax, q = at("amax", [2, 2], f32, q)
    asum, q = at("asum", [2, 2], f32, q)
    arec, q = at("arec", [2, 2], f32, q)
    ost, q = at("ost", [2, 16], f32, q)
    subw, q = at("subw", [1], f32, q)
    rowv, q = at("rowv", [12], f32, q)
    srow, q = at("srow", [12], f32, q)
    baf, q = at("baf", [NB, 12], f32, q)
    z8, q = at("z8", [NB, 8], f32, q)
    e8, q = at("e8", [NB, 8], f32, q)
    sp8, q = at("sp8", [NB, 8], f32, q)
    expa, q = at("expa", [4], f32, q)
    beta, q = at("beta", [NB, H], f32, q)
    gtok, q = at("gtok", [NB, H], f32, q)
    lftok, q = at("lftok", [NB, H], f32, q)
    gcum, q = at("gcum", [3, NB, H], f32, q)
    gexp, q = at("gexp", [3, NB, H], f32, q)
    l2s, q = at("l2s", [NB, 8], f32, q)
    kscal, q = at("kscal", [3, NB, H], f32, q)
    qscal, q = at("qscal", [NB, H], f32, q)
    assert q <= at_A, (q, at_A)
    at_M = at_A + 8 * 2 * S * 4
    q = at_M
    rope, q = at("rope", [2 * S + P], f32, q)
    upad, q = at("upad", [4, S + TAPS - 1], f32, q)
    cacc, q = at("cacc", [4, S], f32, q)
    qk, q = at("qk", [8, S], f32, q)
    vtk, q = at("vtk", [NB, S], f32, q)
    WT, q = at("WT", [2, NB, S], f32, q)
    assert q <= TOP
    q = at_A
    pbuf, q = at("pbuf", [2, 2, S], f32, q)
    wbuf, q = at("wbuf", [2, S], f32, q)
    assert q <= at_A + 4 * 2 * S * 4
    prod, _ = at("prod", [PROD, S], f32, at_A + 4 * 2 * S * 4)
    q = at_H
    oT, q = at("oT", [H, S], f32, q)
    osq, q = at("osq", [H, S], f32, q)
    ytmp, q = at("ytmp", [4, S], f32, q)
    assert q <= at_H + 32768
    q = at_M
    qT, q = at("qT", [H, S], f32, q)
    kT, q = at("kT", [H, S], f32, q)
    ktok, q = at("ktok", [NB, H, P], f32, q)
    vtok, q = at("vtok", [NB, H, P], f32, q)
    at_z = q
    zT, q = at("zT", [H, S], f32, q)
    qd, q = at("qd", [H, S], f32, q)
    kd, q = at("kd", [H, S], f32, q)
    vd, q = at("vd", [NB, S], f32, q)
    cin, q = at("cin", [S + GTAPS - 1], f32, q)
    assert q <= TOP, (q, TOP)
    hrow, _ = at("hrow", [S], f32, at_z)
    q = at_A + 4 * 2 * S * 4
    G8, q = at("G8", [8, H, P], f32, q)
    assert q == at_M
    G5, _ = at("G5", [5, H, P], f32, at_work)
    gbufs = [[G8[:, n] for n in range(6)], [G8[:, 6], G8[:, 7]] + [G5[:, n] for n in range(4)]]
    St_b = G5[:, 4]
    gsq, _ = at("gsq", [H, S], f32, at_work)
    outT, _ = at("outT", [KD, S], f32, at_H)
    q = at_H
    cb, q = at("cb", [H, S], f32, q)
    tbuf, q = at("tbuf", [2, S], f32, q)
    fbuf, q = at("fbuf", [2, S], f32, q)
    FT, q = at("FT", [2, NB, S], f32, q)
    assert q <= at_H + 32768

    PS = nc.alloc_psum_tensor("PS", [P, 8, S], f32)

    ident, cums, ones = consts[:, 0], consts[:, 1], consts[:, 2]
    cmask, dmask = consts[:, 3], consts[:, 4]
    lmask = {b: consts[:, 5 + n].bitcast(i32) for n, b in enumerate(LEVELS)}

    def over_heads(ap):
        return ap.unsqueeze(1).broadcast_to([P, H, P])

    def per_head(ap):
        return ap.unsqueeze(2).broadcast_to([P, H, P])

    def blk(b):
        return slice(b * P, (b + 1) * P)

    def hd(ps_bank):
        return PS[:, ps_bank].rearrange("p (h c) -> p h c", h=H)

    def vcol(n):
        return vec[:, n:n + 1]

    def shared_tap(m):
        return (2, m) if m < SHARED else (3, m - SHARED)

    def added(m):
        return m if m < SHARED else m - 1

    sems = {}

    def sem(name):
        if name not in sems:
            sems[name] = nc.alloc_semaphore(name)
        return sems[name]

    def slot_round(t):
        return t // RING + 1

    x_loaded = [sem(f"x_loaded{n}") for n in range(4)]
    gdn_mm, gdn_act, gdn_dve, gdn_pool = [[sem(f"gdn{n}_{e}") for n in range(2)] for e in ("products", "act", "dve", "pool")]
    const_loaded, vec_loaded, rope_loaded, small_loaded = map(sem, ("const_loaded", "vec_loaded", "rope_loaded", "small_loaded"))
    raw_loaded = [sem(f"raw_loaded{n}") for n in range(RAW)]
    hi_ready = [sem(f"hi_ready{n}") for n in range(RING)]
    lo_ready = [sem(f"lo_ready{n}") for n in range(RING)]
    tile_used, evacuated = sem("tile_used"), sem("evacuated")
    feed_mul, feed_hi, feed_sq, ssq_done, h_ready = map(sem, ("feed_mul", "feed_hi", "feed_sq", "ssq_done", "h_ready"))
    norm_sum, norm_ms, norm_sqrt, norm_tok, norm_bc, norm_rstd = map(
        sem, ("norm_sum", "norm_ms", "norm_sqrt", "norm_tok", "norm_bc", "norm_rstd"))
    y_ready = sem("y_ready")
    down_done = sem("down_done")
    out_done = sem("out_done")
    dchain = sem("dve_chain")

    UNITS = [(h, i) for h in range(H) for i in range(NB)]
    FINAL = 4
    QK_BANK = (4, 5, 2, 3, 2, 3, 2, 3)
    DIFF_T, DIFF_V = 0, 1
    SUB_BANK = (3, 2, 3, 5)
    SUB_COLS = ((0, 12), (12, 16))
    FOX_T, FOX_V = 2, 3

    block = nc.Block()
    block.__enter__()

    @block.sync
    def _(sp):
        def load_x(n):
            sp.dma_start(xT[:, 2 * n:2 * n + 2], x_d[:, 2 * n:2 * n + 2]).then_inc(x_loaded[n], 16)

        sp.dma_start(vec[:], vec_d).then_inc(vec_loaded, 16)
        load_x(0)
        sp.dma_start(raw[:, 0], w_d[0]).then_inc(raw_loaded[0], 16)
        for n in range(1, 4):
            load_x(n)
        sp.dma_start(consts[:, 0:3].rearrange("p a b -> p (a b)"), const_d[:, 0:3 * P]).then_inc(const_loaded, 16)
        sp.dma_start(raw[:, 1], w_d[1]).then_inc(raw_loaded[1], 16)
        sp.dma_start(rowv[0:1, :], row_d).then_inc(small_loaded, 16)
        for t in range(RAW, RING):
            sp.wait_ge(hi_ready[t - RAW], 1)
            sp.wait_ge(lo_ready[t - RAW], 1)
            sp.dma_start(raw[:, t % RAW], w_d[t]).then_inc(raw_loaded[t % RAW], 16)
        sp.dma_start(rope[:], rope_d).then_inc(rope_loaded, 16)
        sp.dma_start(consts[:, 3:].rearrange("p a b -> p (a b)"), const_d[:, 3 * P:]).then_inc(sem("masks_loaded"), 16)
        with sp.Fori(1, N_TILES // RING) as r:
            for j in range(RING):
                behind = (j - RAW) % RING
                done = r if j < RAW else r + 1
                sp.wait_ge(hi_ready[behind], done)
                sp.wait_ge(lo_ready[behind], done)
                src = w_d[bass.ds(r * RING + j, 1)].rearrange("a p c -> (a p) c")
                sp.dma_start(raw[:, j % RAW], src).then_inc(raw_loaded[j % RAW], 16)
        for t in range(N_TILES // RING * RING, N_TILES):
            sp.wait_ge(hi_ready[(t - RAW) % RING], slot_round(t - RAW))
            sp.wait_ge(lo_ready[(t - RAW) % RING], slot_round(t - RAW))
            sp.dma_start(raw[:, t % RAW], w_d[t]).then_inc(raw_loaded[t % RAW], 16)
        for n in (0, 1, 5, 2, 3, 6, 4, 7):
            if n < OUT_DVE:
                sp.wait_ge(sem("out_ready"), n + 1)
            else:
                sp.wait_ge(sem("out_ready_pool"), n - OUT_DVE + 1)
            sp.dma_start(out_d[:, n], outT[:, n]).then_inc(out_done, 16)
        sp.wait_ge(out_done, 16 * KD)

    @block.gpsimd
    def _(pool):
        def lo(t):
            pool.wait_ge(hi_ready[t % RING], slot_round(t))
            if t >= RING:
                pool.wait_ge(tile_used, t - RING + 1)
            nc.gpsimd.tensor_tensor(wring[:, t % RING, 1], raw[:, t % RAW], wring[:, t % RING, 0].bitcast(f32),
                                    ALU.subtract).then_inc(lo_ready[t % RING], 1)

        def add_squares(s, n):
            if n == 0:
                return
            pool.wait_ge(feed_sq, KD * s + n + 1)
            if n == 1:
                if s:
                    pool.wait_ge(norm_sum, s)
                nc.gpsimd.tensor_tensor(ssq[:], sqb[:, 0], sqb[:, 1], ALU.add).then_inc(ssq_done, 1)
            else:
                pool.wait_ge(ssq_done, 7 * s + n - 1)
                nc.gpsimd.tensor_tensor(ssq[:], ssq[:], sqb[:, n % 2], ALU.add).then_inc(ssq_done, 1)

        for n in range(KD):
            add_squares(0, n)
        nc.gpsimd.memset(upad[:, :, 0:TAPS - 1], 0.0).then_inc(sem("pad_zero"), 1)
        def add_taps(m0, m1):
            for m in range(m0, m1):
                c, k = shared_tap(m)
                if k:
                    pool.wait_ge(sem("tap_product"), m + 1)
                    if k > 1:
                        pool.wait_ge(sem("conv_added"), added(m) - 1)
                    nc.gpsimd.tensor_tensor(cacc[:, c], cacc[:, c], prod[:, m % PROD], ALU.add).then_inc(sem("conv_added"), 1)

        for kind, a in even_order():
            if kind == "val_gate":
                lo(2 * a + RING)
                lo(2 * a + 1 + RING)
            elif kind == "v":
                lo(8 + a + RING)
            elif kind == "qk_evac":
                lo(12 + a + RING)
            elif kind == "shared_taps":
                add_taps(*a)
            elif kind == "ln_add":
                pool.wait_ge(sem("conv_done"), 3)
                pool.wait_ge(sem("conv_added"), added(SHARED + TAPS - 1))
                for c in range(1, 4):
                    if c > 1:
                        pool.wait_ge(sem("ln_chunks"), c - 1)
                    nc.gpsimd.tensor_tensor(prod[:, 0], cacc[:, 0] if c == 1 else prod[:, 0], cacc[:, c], ALU.add).then_inc(sem("ln_chunks"), 1)
            elif kind == "ln_centre" and a:
                pool.wait_ge(sem("ln_sq"), a + 1)
                if a > 1:
                    pool.wait_ge(sem("ln_squares"), a - 1)
                nc.gpsimd.tensor_tensor(prod[:, 1], upad[:, 0, 0:S] if a == 1 else prod[:, 1], upad[:, a, 0:S],
                                        ALU.add).then_inc(sem("ln_squares"), 1)
        for n in range(KD):
            if n < 4:
                lo(T_OUT0 + RING + n)
            add_squares(1, n)
        for n in range(KD):
            add_squares(2, n)
        nc.gpsimd.memset(cin[:, 0:GTAPS - 1], 0.0).then_inc(sem("cin_zero"), 1)
        for e in range(12):
            lo(odd_tile(e) + RING)
            if e == HEAD_TILE - 1:
                lo(T_IN1 + HEAD_TILE + RING)
        pool.wait_ge(sem("gdn_scalars"), 1)
        nc.gpsimd.memset(St_b, 0.0).then_inc(sem("state_zero"), 1)
        for kind, a in odd_order():
            if kind == "evac":
                lo(odd_tile(a) + RING)
            if kind == "gdn":
                i, b = a
                st, j = i % 2, i // 2
                if b == 0:
                    pool.wait_ge(sem("tok_ready"), 8)
                    nc.gpsimd.tensor_tensor(vtok[:, i], vtok[:, i], per_head(beta[:, i]), ALU.mult).then_inc(gdn_pool[st], 1)
                if b == STEP_W:
                    pool.wait_ge(gdn_mm[st], j * PE_STEPS + STEP_W - 1)
                    nc.gpsimd.tensor_tensor(gbufs[st][3], ktok[:, i], per_head(kscal[:, 1, i]), ALU.mult).then_inc(gdn_pool[st], 1)
                    pool.wait_ge(gdn_pool[st], j * POOL_STEPS + 2)
                    nc.gpsimd.tensor_tensor(ktok[:, i], ktok[:, i], per_head(kscal[:, 2, i]), ALU.mult).then_inc(gdn_pool[st], 1)
        for n in range(KD):
            if n < 4:
                lo(T_OUT1 + RING + n)
            add_squares(3, n)
        for n in range(KD):
            add_squares(4, n)
        for n in range(OUT_DVE, KD):
            pool.wait_ge(evacuated, E_DN1 + n + 1)
            nc.gpsimd.tensor_scalar(outT[:, n], xT[:, n], vcol(V_NORM + KD * FINAL + n), None, ALU.mult).then_inc(sem("out_weighted"), 1)
        pool.wait_ge(sem("out_weighted"), KD - OUT_DVE)
        pool.wait_ge(norm_rstd, FINAL + 1)
        for n in range(OUT_DVE, KD):
            nc.gpsimd.tensor_tensor(outT[:, n], outT[:, n], rstd[:], ALU.mult).then_inc(sem("out_ready_pool"), 1)

    @block.scalar
    def _(act):
        def hi(t):
            act.wait_ge(raw_loaded[t % RAW], 16 * (t // RAW + 1))
            if t >= RING:
                act.wait_ge(tile_used, t - RING + 1)
            nc.scalar.activation(wring[:, t % RING, 0], raw[:, t % RAW], ACT.Copy).then_inc(hi_ready[t % RING], 1)

        def feed(s, n):
            if s < FINAL:
                act.wait_ge(feed_mul, KD * s + n + 1)
                nc.scalar.activation(HH[:, n, 0], hbuf[:, n % 2], ACT.Copy).then_inc(feed_hi, 1)
            else:
                act.wait_ge(evacuated, E_DN1 + n + 1)
            if n >= 2:
                act.wait_ge(ssq_done, 7 * s + max(n - 2, 1))
            elif s:
                act.wait_ge(ssq_done, 7 * s)
            nc.scalar.activation(sqb[:, n % 2], xT[:, n], ACT.Square).then_inc(feed_sq, 1)

        def norm_root(s):
            act.wait_ge(norm_ms, s + 1)
            nc.scalar.activation(nst[:], nst[:], ACT.Sqrt).then_inc(norm_sqrt, 1)

        def ffn(s, tg, eg, last):
            g0 = KF * s
            with act.Fori(0, KF // 2) as r:
                for c in range(2):
                    done = r * 2 + (g0 + c + 1)
                    act.wait_ge(evacuated, r * RING + (eg + 2 * c + 1))
                    nc.scalar.activation(gbuf[:, c], gbuf[:, c], ACT.Silu).then_inc(sem("gate_silu"), 1)
                    for u in range(2):
                        j = 2 * c + u
                        t = tg + RING + j
                        if u:
                            act.wait_ge(sem("ffn_mul"), done)
                            nc.scalar.activation(AA[:, bass.ds(r * 2 + c, 1), 0].rearrange("p a b -> p (a b)"),
                                                 abuf[:], ACT.Copy).then_inc(sem("ffn_hi"), 1)
                        act.wait_ge(raw_loaded[t % RAW], r * (16 * RING // RAW) + 16 * (t // RAW + 1))
                        act.wait_ge(tile_used, r * RING + (t - RING + 1))
                        nc.scalar.activation(wring[:, t % RING, 0], raw[:, t % RAW], ACT.Copy).then_inc(hi_ready[t % RING], 1)
            td = tg + 2 * KF
            whole = KF // RING - (1 if last else 0)
            with act.Fori(0, whole) as r:
                for j in range(RING):
                    t = td + RING + j
                    act.wait_ge(raw_loaded[t % RAW], r * (16 * RING // RAW) + 16 * (t // RAW + 1))
                    act.wait_ge(tile_used, r * RING + (t - RING + 1))
                    nc.scalar.activation(wring[:, t % RING, 0], raw[:, t % RAW], ACT.Copy).then_inc(hi_ready[t % RING], 1)
            for t in range(td + RING + whole * RING, td + KF + (0 if last else RING - LATE)):
                hi(t)

        for n in range(KD):
            feed(0, n)
            if n in HI_AFTER:
                hi(HI_AFTER.index(n))
        norm_root(0)
        act.wait_ge(sem("lam_sum"), 1)
        nc.scalar.activation(lam[:, 4:6], PS[:, 6, 0:2], ACT.Exp).then_inc(sem("lam_exp"), 1)
        def diff_exp(u):
            n = (u % NB + 1) * P
            for m in range(2):
                act.wait_ge(sem("diff_max"), u + 1)
                if u >= 2 and m == 0:
                    act.wait_ge(sem("diff_w"), u - 1)
                nc.scalar.activation(pbuf[:, u % 2, m, 0:n], PS[:, 4 + 2 * (u % 2) + m, 0:n], ACT.Exp,
                                     bias=amax[:, u % 2, m:m + 1],
                                     accum_out=asum[:, u % 2, m:m + 1]).then_inc(sem("diff_exp"), 1)

        def wt_copy(u, sem_t, sem_c, dst, bank, sem_pv):
            h, i = UNITS[u]
            act.wait_ge(sem(sem_t), u + 1)
            if h >= 2 and i == 0:
                act.wait_ge(sem(sem_pv), h - 1)
            nc.scalar.activation(dst[:, h % 2, 0:i + 1, blk(i)],
                                 PS[:, bank, 0:(i + 1) * P].rearrange("p (j c) -> p j c", c=P),
                                 ACT.Copy).then_inc(sem(sem_c), 1)

        def multiply_taps(m0, m1):
            for m in range(m0, m1):
                c, k = shared_tap(m)
                if k == 0:
                    act.wait_ge(sem("gated"), c - 1)
                if m > PROD:
                    act.wait_ge(sem("conv_added"), added(m - PROD))
                w = vcol(V_CONVW + TAPS * c + k)
                if k == 0:
                    ins = nc.scalar.activation(cacc[:, c], upad[:, c, 0:S], ACT.Identity, bias=vcol(V_CONVB + c), scale=w)
                else:
                    ins = nc.scalar.activation(prod[:, m % PROD], upad[:, c, k:k + S], ACT.Copy, scale=w)
                ins.then_inc(sem("tap_product"), 1)

        for kind, a in even_order():
            if kind == "qk" and a == (0, 0):
                act.wait_ge(sem("masks_loaded"), 16)
                nc.scalar.activation(mask16[:, 0], ident, ACT.Copy).then_inc(sem("mask16"), 1)
                nc.scalar.activation(mask16[:, 1], cmask, ACT.Copy).then_inc(sem("mask16"), 1)
            if kind == "shared_taps":
                multiply_taps(*a)
            if kind == "val_gate":
                hi(2 * a + RING)
                hi(2 * a + 1 + RING)
                act.wait_ge(evacuated, 2 * a + 2)
                nc.scalar.activation(sqb[:, a % 2], sqb[:, a % 2], ACT.Sigmoid).then_inc(sem("gate_sig"), 1)
            elif kind == "v":
                hi(8 + a + RING)
            elif kind == "qk_evac":
                hi(12 + a + RING)
            elif kind == "diff_m":
                diff_exp(a)
            elif kind == "diff_t":
                wt_copy(a, "diff_t", "diff_wt", WT, DIFF_T, "diff_pv")
            elif kind == "diff_v":
                act.wait_ge(sem("diff_pv"), a + 1)
                nc.scalar.activation(oT[:, a], PS[:, DIFF_V], ACT.Copy)
                nc.scalar.activation(osq[:, a], PS[:, DIFF_V], ACT.Square).then_inc(sem("diff_osq"), 1)
            elif kind == "ln_centre":
                act.wait_ge(sem("ln_centred"), a + 1)
                nc.scalar.activation(upad[:, a, 0:S], cacc[:, a], ACT.Square).then_inc(sem("ln_sq"), 1)
            elif kind == "ln_root":
                act.wait_ge(sem("ln_var"), 1)
                nc.scalar.activation(lst[:, 4:8], lst[:, 4:8], ACT.Sqrt).then_inc(sem("ln_root"), 1)
            elif kind == "conv_silu":
                for c in range(4):
                    act.wait_ge(sem("ln_scaled"), c + 1)
                    nc.scalar.activation(ytmp[:, c], cacc[:, c], ACT.Silu, bias=vcol(V_LNB + c),
                                         scale=vcol(V_LNW + c)).then_inc(sem("y_tmp"), 1)
                for c in range(4):
                    act.wait_ge(sem("y_tmp"), c + 1)
                    nc.scalar.activation(AA[:, 4 + c, 0], ytmp[:, c], ACT.Copy).then_inc(sem("y_hi"), 1)
            elif kind == "sub_root":
                g = slice(*SUB_COLS[a])
                act.wait_ge(sem("stat_ms"), a + 1)
                nc.scalar.activation(ost[:, 0, g], ost[:, 0, g], ACT.Sqrt).then_inc(sem("stat_root"), 1)
            elif kind == "sub_hi":
                act.wait_ge(sem("y_scaled"), a + 1)
                nc.scalar.activation(AA[:, a, 0], oT[:, a], ACT.Copy).then_inc(sem("y_hi"), 1)
        for n in range(KD):
            if n < 4:
                hi(T_OUT0 + RING + n)
            feed(1, n)
            if n >= 4:
                hi(T_OUT0 + RING + n)
        norm_root(1)
        ffn(0, T_GU0, E_GU0, False)
        for n in range(KD):
            feed(2, n)
        for t in range(T_IN1 + RING - LATE, T_IN1 + RING):
            hi(t)
        norm_root(2)

        def tok_copy(m):
            act.wait_ge(sem("tok_t"), m + 1)
            nc.scalar.activation((ktok, vtok)[m // 4][:, :, m % 4], PS[:, 4 + m % 2].rearrange("p (b c) -> p b c", b=NB),
                                 ACT.Copy).then_inc(sem("tok_ready"), 1)

        for e in range(12):
            if e < HEAD_TILE:
                hi(odd_tile(e) + RING)
            if e == HEAD_TILE - 1:
                hi(T_IN1 + HEAD_TILE + RING)
            if e >= HEAD_TILE:
                hi(odd_tile(e) + RING)
            if e >= 7:
                tok_copy(e - 7)
            if e == 11:
                tok_copy(5)
            h = e % H
            act.wait_ge(sem("gconv_done"), e + 1)
            if e >= 10:
                act.wait_ge(sem("tok_t"), e - 5)
            if e in (8, 9):
                act.wait_ge(sem("l2_mm"), e - 1)
            dst = (qT[:, h], kT[:, h], sqb[:, e % 2])[e // 4]
            nc.scalar.activation(dst, hbuf[:, e % 2], ACT.Silu).then_inc(sem("gsilu"), 1)
            if e < 8:
                act.wait_ge(sem("gsilu"), e + 1)
                if e >= 2:
                    act.wait_ge(sem("l2_mm"), e - 1)
                nc.scalar.activation(sqb[:, e % 2], dst, ACT.Square).then_inc(sem("gsq"), 1)
            if e == 6:
                act.wait_ge(sem("gate_args"), 1)
                nc.scalar.activation(e8[:], e8[:], ACT.Exp).then_inc(sem("gate_exp"), 1)
                nc.scalar.activation(expa[:], srow[:, 0:4], ACT.Exp).then_inc(sem("gate_exp"), 1)
                nc.scalar.activation(beta[:], baf[:, :, 0:4], ACT.Exp, scale=-1.0).then_inc(sem("gate_exp"), 1)
            if e == 7:
                act.wait_ge(sem("gate_one"), 1)
                nc.scalar.activation(e8[:], e8[:], ACT.Ln).then_inc(sem("gate_ln"), 1)
            if e == 10:
                act.wait_ge(sem("g_sums"), 1)
                for n in range(3):
                    nc.scalar.activation(gexp[:, n], gexp[:, n], ACT.Exp).then_inc(sem("g_exp"), 1)
        def gdn(i, k):
            st, j = i % 2, i // 2
            X, Y = 4 + 2 * st, 5 + 2 * st
            Zb, Tb, Rb = gbufs[st][0], gbufs[st][1], gbufs[st][2]

            def run(pe_step, out, bank, func=ACT.Copy, **kw):
                act.wait_ge(gdn_mm[st], j * PE_STEPS + pe_step + 1)
                nc.scalar.activation(out, hd(bank), func, **kw).then_inc(gdn_act[st], 1)

            if k == 0:
                if j:
                    act.wait_ge(gdn_dve[st], DVE_STEPS)
                run(0, Rb, X, ACT.Exp)
                act.wait_ge(gdn_dve[st], j * DVE_STEPS + 3)
                nc.scalar.activation(Zb, Zb, ACT.Exp).then_inc(gdn_act[st], 1)
            elif k == STEP_T0:
                run(k, Tb, X)
            elif STEP_Z1 <= k < STEP_W:
                if (k - STEP_Z1) % 3 == 0:
                    run(k, Zb, X)
                if (k - STEP_Z1) % 3 == 2:
                    run(k, Tb, X)
            elif k == STEP_W:
                run(k, Tb, X, scale=-1.0)
            elif k == STEP_V:
                run(k, Zb, Y)
            elif k == STEP_O:
                run(k, qT[:, :, blk(i)], X)

        def fox_exp(u):
            n = (u % NB + 1) * P
            act.wait_ge(sem("fox_min"), u + 1)
            if u >= 2:
                act.wait_ge(sem("fox_t"), u - 1)
            nc.scalar.activation(fbuf[:, u % 2, 0:n], tbuf[:, u % 2, 0:n], ACT.Exp, bias=amax[:, 0, u % 2:u % 2 + 1],
                                 scale=-1.0, accum_out=asum[:, 0, u % 2:u % 2 + 1]).then_inc(sem("fox_exp"), 1)

        for kind, a in odd_order():
            if kind == "gdn":
                gdn(*a)
            elif kind == "evac":
                hi(odd_tile(a) + RING)
            elif kind == "tok":
                tok_copy(a)
            elif kind == "l2":
                act.wait_ge(sem("l2_ms"), 1)
                nc.scalar.activation(l2s[:], l2s[:], ACT.Sqrt).then_inc(sem("l2_root"), 1)
            elif kind == "z_silu":
                act.wait_ge(evacuated, E_IN1 + 24 + a + 1)
                nc.scalar.activation(zT[:, a], zT[:, a], ACT.Silu).then_inc(sem("z_silu"), 1)
            elif kind == "fox_m":
                fox_exp(a)
            elif kind == "fox_t":
                wt_copy(a, "fox_t", "fox_wt", FT, FOX_T, "fox_pv")
            elif kind == "fox_v":
                act.wait_ge(sem("fox_pv"), a + 1)
                nc.scalar.activation(AA[:, a, 0], PS[:, FOX_V], ACT.Copy).then_inc(sem("fox_hi"), 1)
            elif kind == "norm_sq":
                act.wait_ge(gdn_act[0], 2 * ACT_STEPS)
                act.wait_ge(gdn_act[1], 2 * ACT_STEPS)
                act.wait_ge(gdn_dve[1], 2 * DVE_STEPS)
                for h in range(H):
                    nc.scalar.activation(gsq[:, h], qT[:, h], ACT.Square).then_inc(sem("gdn_osq"), 1)
            elif kind == "norm_root":
                act.wait_ge(sem("stat_ms"), 3)
                nc.scalar.activation(ost[:, 0], ost[:, 0], ACT.Sqrt).then_inc(sem("stat_root"), 1)
            elif kind == "norm_hi":
                act.wait_ge(sem("gy_ready"), a + 1)
                nc.scalar.activation(AA[:, 4 + a, 0], qT[:, a], ACT.Copy).then_inc(sem("y_hi"), 1)
        for n in range(KD):
            if n < 4:
                hi(T_OUT1 + RING + n)
            feed(3, n)
            if n >= 4:
                hi(T_OUT1 + RING + n)
        norm_root(3)
        ffn(1, T_GU1, E_GU1, True)
        for n in range(KD):
            feed(4, n)
        norm_root(4)

    @block.vector
    def _(dve):
        V = nc.vector
        seq = [0]

        def link(ins):
            seq[0] += 1
            ins.then_inc(dchain, 1)
            dve.wait_ge(dchain, seq[0])

        def feed_mul_(s, n):
            if n >= 2:
                dve.wait_ge(h_ready, KD * s + n - 1)
            V.tensor_scalar(hbuf[:, n % 2], xT[:, n], vcol(V_NORM + KD * s + n), None, ALU.mult).then_inc(feed_mul, 1)

        def feed_lo(s, n):
            dve.wait_ge(feed_hi, KD * s + n + 1)
            V.tensor_tensor(HH[:, n, 1], hbuf[:, n % 2], HH[:, n, 0].bitcast(f32), ALU.subtract).then_inc(h_ready, 1)

        def norm_finish(s, bank):
            dve.wait_ge(norm_sum, s + 1)
            V.tensor_scalar(nst[:], PS[:, bank, 0:NB], 1.0 / D, 1e-6, ALU.mult, ALU.add).then_inc(norm_ms, 1)
            dve.wait_ge(norm_sqrt, s + 1)
            V.reciprocal(rtok[:], nst[:]).then_inc(norm_tok, 1)
            dve.wait_ge(norm_bc, s + 1)
            V.tensor_copy(rstd[:], PS[:, bank]).then_inc(norm_rstd, 1)
            dve.wait_ge(norm_rstd, s + 1)

        def residual(n, e, bank):
            V.tensor_tensor(xT[:, n], xT[:, n], PS[:, bank], ALU.add).then_inc(evacuated, 1)
            dve.wait_ge(evacuated, e + 1)

        def ffn(s, tg, eg, last):
            with dve.Fori(0, KF // 2) as r:
                for c in range(2):
                    cnt = r * 2 + (KF * s + c + 1)
                    for u, buf in enumerate((gbuf, ubuf)):
                        dve.wait_ge(tile_used, r * RING + (tg + 2 * c + u + 1))
                        V.tensor_tensor(buf[:, c], PS[:, 2 * c + u], rstd[:], ALU.mult).then_inc(evacuated, 1)
                    dve.wait_ge(evacuated, r * RING + (eg + 2 * c + 2))
                    for u in range(2):
                        j = 2 * c + u
                        t = tg + RING + j
                        if u == 0:
                            dve.wait_ge(sem("gate_silu"), cnt)
                            V.tensor_tensor(abuf[:], gbuf[:, c], ubuf[:, c], ALU.mult).then_inc(sem("ffn_mul"), 1)
                        dve.wait_ge(hi_ready[t % RING], r + slot_round(t))
                        V.tensor_tensor(wring[:, t % RING, 1], raw[:, t % RAW], wring[:, t % RING, 0].bitcast(f32),
                                        ALU.subtract).then_inc(lo_ready[t % RING], 1)
                        if u == 0:
                            dve.wait_ge(sem("ffn_hi"), cnt)
                            V.tensor_tensor(AA[:, bass.ds(r * 2 + c, 1), 1].rearrange("p a b -> p (a b)"), abuf[:],
                                            AA[:, bass.ds(r * 2 + c, 1), 0].rearrange("p a b -> p (a b)").bitcast(f32),
                                            ALU.subtract).then_inc(sem("ffn_lo"), 1)
            td = tg + 2 * KF
            whole = KF // RING - (1 if last else 0)
            with dve.Fori(0, whole) as r:
                for j in range(RING):
                    t = td + RING + j
                    dve.wait_ge(hi_ready[t % RING], r + slot_round(t))
                    V.tensor_tensor(wring[:, t % RING, 1], raw[:, t % RAW], wring[:, t % RING, 0].bitcast(f32),
                                    ALU.subtract).then_inc(lo_ready[t % RING], 1)
            for t in range(td + RING + whole * RING, td + KF + (0 if last else RING - LATE)):
                lo(t)

        def lo(t):
            dve.wait_ge(hi_ready[t % RING], slot_round(t))
            V.tensor_tensor(wring[:, t % RING, 1], raw[:, t % RAW], wring[:, t % RING, 0].bitcast(f32),
                            ALU.subtract).then_inc(lo_ready[t % RING], 1)

        def down(s, td, e0):
            for n in range(KD):
                if n < KD - 1:
                    dve.wait_ge(down_done, (s // 2 - 1) * (KD - 1) + n + 1)
                else:
                    dve.wait_ge(tile_used, td + KF)
                residual(n, e0 + n, n)
                if s < FINAL:
                    feed_mul_(s, n)
                    if n:
                        feed_lo(s, n - 1)
            if s < FINAL:
                feed_lo(s, KD - 1)

        def out_proj(s, t0, e0):
            for n in range(KD):
                dve.wait_ge(tile_used, t0 + n + 1)
                residual(n, e0 + n, (e0 + n) % 4)
                feed_mul_(s, n)
                if n:
                    feed_lo(s, n - 1)
                if n >= 5:
                    lo(t0 + RING + n - 1)
            feed_lo(s, KD - 1)
            lo(t0 + RING + KD - 1)

        dve.wait_ge(vec_loaded, 16)
        for n in range(KD):
            dve.wait_ge(x_loaded[n // 2], 16)
            feed_mul_(0, n)
            if n:
                feed_lo(0, n - 1)
            if n == HI_AFTER[0] + 1:
                lo(0)
        feed_lo(0, KD - 1)
        for t in range(1, RING):
            lo(t)
        V.tensor_tensor(lam[0:64, 0:1], vec[0:64, V_LAM:V_LAM + 1], vec[0:64, V_LAM + 1:V_LAM + 2], ALU.mult).then_inc(sem("lam_prod"), 1)
        V.tensor_tensor(lam[0:64, 1:2], vec[0:64, V_LAM + 2:V_LAM + 3], vec[0:64, V_LAM + 3:V_LAM + 4], ALU.mult).then_inc(sem("lam_prod"), 1)
        norm_finish(0, 7)
        dve.wait_ge(sem("lam_exp"), 1)
        link(V.tensor_tensor(lam[:, 6:7], lam[:, 5:6], lam[:, 4:5], ALU.subtract))
        link(V.tensor_scalar(lam[:, 7:8], lam[:, 6:7], -LAMBDA_INIT, None, ALU.add))
        def taps():
            tap, count = [0, 0, SHARED], [0] * 3
            turn = 0
            while True:
                open_ = [c for c in range(min(gated[0], 3)) if tap[c] < TAPS][:2]
                if not open_:
                    yield False
                    continue
                c = open_[turn % len(open_)]
                turn += 1
                k = tap[c]
                tap[c] += 1
                if k == 0:
                    ins = V.tensor_scalar(cacc[:, c], upad[:, c, 0:S], vcol(V_CONVW + TAPS * c), vcol(V_CONVB + c), ALU.mult, ALU.add)
                else:
                    if count[c]:
                        dve.wait_ge(dchain, count[c])
                    else:
                        dve.wait_ge(sem("conv_added"), added(SHARED - 1))
                    ins = V.scalar_tensor_tensor(cacc[:, c], upad[:, c, k:k + S], vcol(V_CONVW + TAPS * c + k), cacc[:, c],
                                                 ALU.mult, ALU.add)
                if k < TAPS - 1:
                    seq[0] += 1
                    count[c] = seq[0]
                    ins.then_inc(dchain, 1)
                else:
                    ins.then_inc(sem("conv_done"), 1)
                yield True

        gated = [0]
        conv = taps()

        def pump(n):
            for _ in range(n):
                if not next(conv):
                    break

        def val_gate(c):
            for m, buf in enumerate((hbuf, sqb)):
                dve.wait_ge(tile_used, 2 * c + m + 1)
                V.tensor_tensor(buf[:, c % 2], PS[:, (2 * c + m) % 4], rstd[:], ALU.mult).then_inc(evacuated, 1)
            pump(2 if c else 0)
            dve.wait_ge(sem("gate_sig"), c + 1)
            ins = V.tensor_tensor(upad[:, c, TAPS - 1:], hbuf[:, c % 2], sqb[:, c % 2], ALU.mult)
            if c < 2:
                link(ins)
            else:
                ins.then_inc(sem("gated"), 1)
            gated[0] += 1
            pump(TAPS_VAL)

        def rope_finish(j):
            dve.wait_ge(rope_loaded, 16)
            dve.wait_ge(sem("rope_mm"), j + 1)
            dst = qk[:, j // 2 + 4 * (j % 2)]
            V.tensor_tensor(dst, hbuf[:, j % 2], rope[:, 0:S], ALU.mult)
            V.tensor_tensor(sqb[:, j % 2], PS[:, QK_BANK[j]], rope[:, S:2 * S], ALU.mult).then_inc(sem("rope_sin"), 1)
            dve.wait_ge(sem("rope_sin"), j + 1)
            V.tensor_tensor(dst, dst, sqb[:, j % 2], ALU.add).then_inc(sem("qk_ready"), 1)

        def diff_max(u):
            n = (u % NB + 1) * P
            dve.wait_ge(sem("diff_s"), u + 1)
            bank = 4 + 2 * (u % 2)
            V.tensor_reduce(amax[:, u % 2], PS[:, bank:bank + 2, 0:n], AX.X, ALU.max, negate=True).then_inc(sem("diff_max"), 1)

        def diff_combine(u):
            n = (u % NB + 1) * P
            dve.wait_ge(sem("diff_exp"), 2 * u + 2)
            link(V.reciprocal(arec[:, u % 2], asum[:, u % 2]))
            link(V.tensor_scalar(arec[:, u % 2, 1:2], arec[:, u % 2, 1:2], lam[:, 7:8], None, ALU.mult))
            link(V.tensor_scalar(pbuf[:, u % 2, 0, 0:n], pbuf[:, u % 2, 0, 0:n], arec[:, u % 2, 0:1], None, ALU.mult))
            if u >= 2:
                dve.wait_ge(sem("diff_t"), u - 1)
            V.scalar_tensor_tensor(wbuf[:, u % 2, 0:n], pbuf[:, u % 2, 1, 0:n], arec[:, u % 2, 1:2],
                                   pbuf[:, u % 2, 0, 0:n], ALU.mult, ALU.add).then_inc(sem("diff_w"), 1)

        def y_lo(k, chunk, src):
            dve.wait_ge(sem("y_hi"), k)
            V.tensor_tensor(AA[:, chunk, 1], src, AA[:, chunk, 0].bitcast(f32), ALU.subtract).then_inc(y_ready, 1)

        dve.wait_ge(sem("pad_zero"), 1)
        for kind, a in even_order():
            if kind == "val_gate":
                val_gate(a)
            elif kind == "taps":
                pump(a)
            elif kind == "v_evac":
                dve.wait_ge(tile_used, 12)
                for b in range(NB):
                    V.tensor_scalar(vtk[:, b], PS[:, b], rtok[:, b:b + 1], None, ALU.mult).then_inc(evacuated, 1)
            elif kind == "qk_evac":
                dve.wait_ge(tile_used, 12 + a + 1)
                V.scalar_tensor_tensor(hbuf[:, a % 2], PS[:, QK_BANK[a]], 1.0 if a % 2 else SC_DIFF, rstd[:],
                                       ALU.mult, ALU.mult).then_inc(evacuated, 1)
            elif kind == "rope":
                rope_finish(a)
            elif kind == "diff_m":
                diff_max(a)
            elif kind == "diff_w":
                diff_combine(a)
            elif kind == "ln_centre":
                dve.wait_ge(sem("ln_mean_mm"), 1)
                V.scalar_tensor_tensor(cacc[:, a], PS[:, 3], -1.0 / 512, cacc[:, a], ALU.mult, ALU.add).then_inc(sem("ln_centred"), 1)
            elif kind == "ln_var":
                dve.wait_ge(sem("ln_var_mm"), 1)
                V.tensor_scalar(lst[:, 4:8], PS[:, 3, 0:4], 1.0 / 512, 1e-5, ALU.mult, ALU.add).then_inc(sem("ln_var"), 1)
            elif kind == "ln_rec":
                dve.wait_ge(sem("ln_root"), 1)
                V.reciprocal(lst[:, 4:8], lst[:, 4:8]).then_inc(sem("ln_rstd"), 1)
            elif kind == "ln_scale":
                dve.wait_ge(sem("ln_rstd_bc"), 1)
                V.tensor_tensor(cacc[:, a], cacc[:, a], PS[:, 3], ALU.mult).then_inc(sem("ln_scaled"), 1)
            elif kind == "conv_lo":
                y_lo(4 + a, 4 + a, ytmp[:, a])
            elif kind == "sub_ms":
                g = slice(*SUB_COLS[a])
                dve.wait_ge(sem("stat_mm"), a + 1)
                V.tensor_scalar(ost[:, 0, g], PS[:, (2, 4)[a], g], 1.0 / P, 1e-6, ALU.mult, ALU.add).then_inc(sem("stat_ms"), 1)
                if a == 0:
                    link(V.tensor_scalar(subw[:], vcol(V_SUBLN), 1.0 - LAMBDA_INIT, None, ALU.mult))
            elif kind == "sub_rec":
                g = slice(*SUB_COLS[a])
                dve.wait_ge(sem("stat_root"), a + 1)
                V.reciprocal(ost[:, 1, g], ost[:, 0, g]).then_inc(sem("stat_rec"), 1)
            elif kind == "sub_mul":
                dve.wait_ge(sem("stat_bc"), a + 1)
                V.scalar_tensor_tensor(oT[:, a], oT[:, a], subw[:], PS[:, SUB_BANK[a]], ALU.mult, ALU.mult).then_inc(sem("y_scaled"), 1)
            elif kind == "sub_lo":
                y_lo(a + 1 if a < 3 else 8, a, oT[:, a])
        out_proj(1, T_OUT0, E_OUT0)
        norm_finish(1, 7)
        ffn(0, T_GU0, E_GU0, False)
        down(2, T_DN0, E_DN0)
        for t in range(T_IN1 + RING - LATE, T_IN1 + RING):
            lo(t)

        norm_finish(2, 7)

        def gates_1():
            dve.wait_ge(sem("baf_mm"), 1)
            V.tensor_copy(srow[:], PS[:, 6, 64:76]).then_inc(sem("gate_tmp"), 1)
            V.tensor_copy(baf[:].rearrange("p a b -> p (a b)"), PS[:, 6, 0:48]).then_inc(sem("gate_tmp"), 1)
            dve.wait_ge(sem("gate_tmp"), 2)
            V.tensor_tensor(z8[:, :, 0:4], baf[:, :, 4:8], srow[:, 4:8].unsqueeze(1).broadcast_to([P, NB, 4]), ALU.add)
            link(V.scalar_tensor_tensor(z8[:, :, 4:8], baf[:, :, 8:12], -1.0, srow[:, 8:12].unsqueeze(1).broadcast_to([P, NB, 4]),
                                        ALU.mult, ALU.subtract))
            V.scalar_tensor_tensor(e8[:], z8[:], -1.0, z8[:], ALU.mult, ALU.min).then_inc(sem("gate_args"), 1)

        def gates_2():
            dve.wait_ge(sem("gate_exp"), 3)
            V.tensor_scalar(e8[:], e8[:], 1.0, None, ALU.add).then_inc(sem("gate_one"), 1)
            link(V.tensor_scalar(beta[:], beta[:], 1.0, None, ALU.add))
            link(V.reciprocal(beta[:], beta[:]))

        def gates_3():
            dve.wait_ge(sem("gate_ln"), 1)
            link(V.scalar_tensor_tensor(sp8[:], z8[:], 0.0, e8[:], ALU.max, ALU.add))
            link(V.scalar_tensor_tensor(gtok[:], sp8[:, :, 0:4], -1.0, expa[:].unsqueeze(1).broadcast_to([P, NB, 4]),
                                        ALU.mult, ALU.mult))
            V.tensor_scalar(lftok[:], sp8[:, :, 4:8], -1.0, None, ALU.mult).then_inc(sem("g_ready"), 1)

        def gates_4():
            dve.wait_ge(sem("g_mm"), 1)
            link(V.tensor_copy(gcum[:].rearrange("p a b c -> p (a b c)"), PS[:, 6, 0:48]))
            V.tensor_tensor(gexp[:, 1], gcum[:, 1], gcum[:, 0], ALU.subtract)
            V.tensor_copy(gexp[:, 0], gcum[:, 0])
            V.tensor_copy(gexp[:, 2], gcum[:, 1]).then_inc(sem("g_sums"), 1)

        dve.wait_ge(sem("cin_zero"), 1)
        for e in range(12):
            bank = e % 4
            dve.wait_ge(tile_used, odd_tile(e) + 1)
            if e:
                dve.wait_ge(sem("gconv_done"), e)
            V.tensor_tensor(cin[:, GTAPS - 1:], PS[:, bank], rstd[:], ALU.mult).then_inc(evacuated, 1)
            dve.wait_ge(evacuated, E_IN1 + e + 1)
            if e >= 2:
                dve.wait_ge(sem("gsilu"), e - 1)
            link(V.tensor_scalar(hbuf[:, e % 2], cin[:, 0:S], vcol(V_GCONV + GTAPS * e), None, ALU.mult))
            for k in range(1, GTAPS):
                ins = V.scalar_tensor_tensor(hbuf[:, e % 2], cin[:, k:k + S], vcol(V_GCONV + GTAPS * e + k), hbuf[:, e % 2],
                                             ALU.mult, ALU.add)
                if k < GTAPS - 1:
                    link(ins)
                else:
                    ins.then_inc(sem("gconv_done"), 1)
            if e == HEAD_TILE:
                dve.wait_ge(tile_used, T_IN1 + HEAD_TILE + 1)
                V.tensor_tensor(hrow[0:12, :], PS[0:12, 6], rstd[0:12, :], ALU.mult).then_inc(sem("head_rows"), 1)
            if e == 6:
                gates_1()
            if e == 7:
                gates_2()
            if e == 8:
                gates_3()
            if e == 10:
                gates_4()
        def gdn(i, k):
            st, j = i % 2, i // 2
            X, Y = 4 + 2 * st, 5 + 2 * st
            decay, kbT, R, NT, qkT, qe = gbufs[st]
            eg = R
            base = j * DVE_STEPS
            mine = gdn_dve[st]

            def product(step):
                dve.wait_ge(gdn_mm[st], j * PE_STEPS + step + 1)

            if k == 0:
                if j:
                    dve.wait_ge(gdn_act[st], ACT_STEPS)
                    dve.wait_ge(mine, base)
                product(0)
                V.tensor_tensor(kbT, kT[:, :, blk(i)], hd(Y), ALU.mult).then_inc(mine, 1)
                dve.wait_ge(gdn_act[st], j * ACT_STEPS + 1)
                V.tensor_tensor(decay, hd(X), per_head(gcum[:, 0, i]), ALU.subtract).then_inc(mine, 1)
                dve.wait_ge(mine, base + 2)
                V.scalar_tensor_tensor(decay, decay, 0.0, over_heads(dmask), ALU.min, ALU.add).then_inc(mine, 1)
            elif k == 1:
                product(1)
                V.tensor_tensor(qT[:, :, blk(i)], qT[:, :, blk(i)], hd(X), ALU.mult).then_inc(mine, 1)
                dve.wait_ge(mine, base + 4)
                V.tensor_tensor(qe, qT[:, :, blk(i)], eg, ALU.mult).then_inc(mine, 1)
                dve.wait_ge(gdn_act[st], j * ACT_STEPS + 2)
                V.tensor_tensor(decay, decay, per_head(l2s[:, i, 4:8]), ALU.mult).then_inc(mine, 1)
            elif k == 2:
                product(2)
                dve.wait_ge(mine, base + 6)
                V.scalar_tensor_tensor(NT, hd(Y), -1.0, decay, ALU.mult, ALU.mult).then_inc(mine, 1)
                V.tensor_tensor(qkT, hd(X), decay, ALU.mult).then_inc(mine, 1)
                V.tensor_copy(R, over_heads(ident)).then_inc(mine, 1)
                dve.wait_ge(mine, base + 9)
                V.copy_predicated(R, over_heads(lmask[LEVELS[0]]), NT).then_inc(mine, 1)
            elif STEP_Z1 <= k < STEP_W and (k - STEP_Z1) % 3 == 1:
                n = (k - STEP_Z1) // 3 + 1
                product(k)
                V.copy_predicated(R, over_heads(lmask[LEVELS[n]]), hd(Y)).then_inc(mine, 1)
            elif k == STEP_S:
                product(STEP_O)
                V.tensor_tensor(St_b, St_b, per_head(gexp[:, 2, i]), ALU.mult).then_inc(mine, 1)
                product(k)
                dve.wait_ge(mine, base + 17)
                V.tensor_tensor(St_b, St_b, hd(Y), ALU.add).then_inc(mine, 1)

        def fox_min(u):
            h, i = UNITS[u]
            n = (i + 1) * P
            dve.wait_ge(sem("fox_s"), u + 1)
            if u >= 2:
                dve.wait_ge(sem("fox_exp"), u - 1)
            link(V.scalar_tensor_tensor(tbuf[:, u % 2, 0:n], cb[:, h, 0:n], gcum[:, 2, i, h:h + 1], PS[:, u % 2, 0:n],
                                        ALU.subtract, ALU.subtract))
            V.tensor_reduce(amax[:, 0, u % 2:u % 2 + 1], tbuf[:, u % 2, 0:n], AX.X, ALU.min).then_inc(sem("fox_min"), 1)

        def fox_scale(u):
            n = (u % NB + 1) * P
            dve.wait_ge(sem("fox_exp"), u + 1)
            link(V.reciprocal(arec[:, 0, u % 2:u % 2 + 1], asum[:, 0, u % 2:u % 2 + 1]))
            V.tensor_scalar(fbuf[:, u % 2, 0:n], fbuf[:, u % 2, 0:n], arec[:, 0, u % 2:u % 2 + 1], None, ALU.mult).then_inc(sem("fox_p"), 1)

        def odd_evac(e):
            dve.wait_ge(tile_used, odd_tile(e) + 1)
            if e < 20:
                dst = qd[:, e - 12] if e < 16 else kd[:, e - 16]
                V.scalar_tensor_tensor(dst, PS[:, e % 4], SC_FOX if e < 16 else 1.0, rstd[:], ALU.mult, ALU.mult).then_inc(evacuated, 1)
            elif e == 23:
                for c in range(NB):
                    V.tensor_scalar(vd[:, c], PS[:, c], rtok[:, c:c + 1], None, ALU.mult).then_inc(evacuated, 1)
            elif e >= 24:
                V.tensor_tensor(zT[:, e - 24], PS[:, e % 4], rstd[:], ALU.mult).then_inc(evacuated, 1)

        def rest(kind, a):
            if kind == "fox_cb":
                dve.wait_ge(sem("fox_cb_mm"), a + 1)
                V.tensor_copy(cb[:, a], PS[:, FOX_V]).then_inc(sem("fox_cb"), 1)
                dve.wait_ge(sem("fox_cb"), a + 1)
            elif kind == "fox_m":
                fox_min(a)
            elif kind == "fox_p":
                fox_scale(a)
            elif kind == "fox_v":
                dve.wait_ge(sem("fox_hi"), a + 1)
                V.tensor_tensor(AA[:, a, 1], PS[:, FOX_V], AA[:, a, 0].bitcast(f32), ALU.subtract).then_inc(sem("fox_y"), 1)
            elif kind == "norm_ms":
                dve.wait_ge(sem("stat_mm"), 3)
                V.tensor_scalar(ost[:, 0], PS[:, 4, 0:16], 1.0 / P, 1e-6, ALU.mult, ALU.add).then_inc(sem("stat_ms"), 1)
            elif kind == "norm_rec":
                dve.wait_ge(sem("stat_root"), 3)
                V.reciprocal(ost[:, 1], ost[:, 0]).then_inc(sem("stat_rec"), 1)
            elif kind == "norm_mul":
                dve.wait_ge(sem("stat_bc"), 4 + a + 1)
                link(V.scalar_tensor_tensor(qT[:, a], qT[:, a], vcol(V_GNORM), PS[:, 4 + a], ALU.mult, ALU.mult))
                dve.wait_ge(sem("z_silu"), a + 1)
                V.tensor_tensor(qT[:, a], qT[:, a], zT[:, a], ALU.mult).then_inc(sem("gy_ready"), 1)
            elif kind == "norm_lo":
                y_lo(8 + a + 1, 4 + a, qT[:, a])

        for kind, a in odd_order():
            if kind == "gdn":
                if a == (0, 0):
                    dve.wait_ge(sem("state_zero"), 1)
                gdn(*a)
            elif kind == "evac":
                odd_evac(a)
            elif kind == "l2":
                dve.wait_ge(sem("l2_mm"), 8)
                V.tensor_scalar(l2s[:].rearrange("p a b -> p (a b)"), PS[:, 7, 0:32], 1e-6, None, ALU.add).then_inc(sem("l2_ms"), 1)
                dve.wait_ge(sem("l2_root"), 1)
                link(V.reciprocal(l2s[:], l2s[:]))
                dve.wait_ge(sem("g_exp"), 3)
                V.tensor_scalar(qscal[:], l2s[:, :, 0:4], SC_FOX, None, ALU.mult)
                link(V.tensor_tensor(kscal[:, 0], l2s[:, :, 4:8], beta[:], ALU.mult))
                V.tensor_tensor(kscal[:, 1], kscal[:, 0], gexp[:, 0], ALU.mult)
                V.tensor_tensor(kscal[:, 2], l2s[:, :, 4:8], gexp[:, 1], ALU.mult).then_inc(sem("gdn_scalars"), 1)
            else:
                rest(kind, a)
        out_proj(3, T_OUT1, E_OUT1)
        norm_finish(3, 7)
        ffn(1, T_GU1, E_GU1, True)
        down(4, T_DN1, E_DN1)
        norm_finish(4, 7)
        for n in range(OUT_DVE):
            V.scalar_tensor_tensor(outT[:, n], xT[:, n], vcol(V_NORM + KD * FINAL + n), rstd[:], ALU.mult, ALU.mult).then_inc(sem("out_ready"), 1)

    @block.tensor
    def _(pe):
        def mm(out, lhsT, rhs, start=True, stop=True):
            return nc.tensor.matmul(out, lhsT, rhs, start=start, stop=stop)

        def product(out, w, x, start, stop):
            mm(out, w[0], x[0], start, False)
            mm(out, w[0], x[1], False, False)
            return mm(out, w[1], x[0], False, stop)

        def wpair(slot, cols):
            return wring[:, slot, 0, cols], wring[:, slot, 1, cols]

        def arrived(t):
            pe.wait_ge(hi_ready[t % RING], slot_round(t))
            pe.wait_ge(lo_ready[t % RING], slot_round(t))

        def stationary(t, e, src, feed=None):
            arrived(t)
            if e >= 4:
                pe.wait_ge(evacuated, e - 3)
            for k in range(KD):
                if feed is not None:
                    pe.wait_ge(h_ready, feed + k + 1)
                last = product(PS[:, e % 4], wpair(t % RING, blk(k)), (src[:, k, 0], src[:, k, 1]), k == 0, k == KD - 1)
            last.then_inc(tile_used, 1)

        def moving(t0, j, e0):
            arrived(t0 + j)
            for m in range(2):
                k = 2 * j + m
                w = wpair((t0 + j) % RING, slice(m * S, (m + 1) * S))
                for b in range(NB):
                    if k == 0:
                        pe.wait_ge(evacuated, e0 + b - 3)
                    last = product(PS[:, (e0 + b) % 4], (HH[:, k, 0, blk(b)], HH[:, k, 1, blk(b)]), w, k == 0, k == KD - 1)
            last.then_inc(tile_used, 1)

        def token_sum(out, src):
            return mm(out, src, ones[:, 0:1])

        def spread(out, col):
            return mm(out, col.to_broadcast([P, P]), ident)

        def norm_stats(s, bank):
            pe.wait_ge(ssq_done, 7 * (s + 1))
            for b in range(NB):
                last = token_sum(PS[:, bank, b:b + 1], ssq[:, blk(b)])
            last.then_inc(norm_sum, 1)

        def norm_spread(s, bank):
            pe.wait_ge(norm_tok, s + 1)
            for b in range(NB):
                last = spread(PS[:, bank, blk(b)], rtok[:, b:b + 1])
            last.then_inc(norm_bc, 1)

        def diff_scores(u):
            h, i = UNITS[u]
            n = (i + 1) * P
            if u >= 2:
                pe.wait_ge(sem("diff_exp"), 2 * (u - 1))
            for m in range(2):
                bank = 4 + 2 * (u % 2) + m
                part = slice(64 * m, 64 * m + 64)
                mm(PS[:, bank, 0:n], qk[part, h, blk(i)], qk[part, 4 + h, 0:n], True, False)
            for m in range(2):
                bank = 4 + 2 * (u % 2) + m
                last = mm(PS[:, bank, blk(i)], mask16[:, 0], mask16[:, 1], False, True)
            last.then_inc(sem("diff_s"), 1)

        def transpose_w(u, src, bank):
            h, i = UNITS[u]
            for j in range(i + 1):
                last = nc.tensor.transpose(PS[:, bank, blk(j)], src[:, u % 2, blk(j)], ident)
            return last

        def weighted_values(h, wt, v, bank):
            for j in range(NB):
                last = mm(PS[:, bank, j * P:S], v[:, j, blk(h)], wt[:, h % 2, j, j * P:S], j == 0, j == NB - 1)
            return last

        for kind, a in even_order():
            if kind == "val_gate":
                for e in (2 * a, 2 * a + 1):
                    if e == 2:
                        pe.wait_ge(const_loaded, 16)
                        norm_stats(0, 7)
                    if e == 3:
                        norm_spread(0, 7)
                        pe.wait_ge(sem("lam_prod"), 2)
                        mm(PS[:, 6, 0:2], ones[0:64, :], lam[0:64, 0:2]).then_inc(sem("lam_sum"), 1)
                    stationary(T_IN0 + e, E_IN0 + e, HH, feed=0 if e == 0 else None)
            elif kind == "v":
                moving(T_IN0 + 8, a, E_IN0 + 8)
            elif kind == "qk":
                j, part = a
                t = T_IN0 + 12 + j
                if part == 0:
                    arrived(t)
                    if j in (2, 3):
                        pe.wait_ge(evacuated, 8 + j + 1)
                    elif j > 3:
                        pe.wait_ge(sem("qk_ready"), j - 1)
                for k in (2 * part, 2 * part + 1):
                    last = product(PS[:, QK_BANK[j]], wpair(t % RING, blk(k)), (HH[:, k, 0], HH[:, k, 1]), k == 0, k == KD - 1)
                if part == 3:
                    last.then_inc(tile_used, 1)
            elif kind == "rope":
                pe.wait_ge(rope_loaded, 16)
                pe.wait_ge(evacuated, 12 + a + 1)
                mm(PS[:, QK_BANK[a]], rope[:, 2 * S:], hbuf[:, a % 2]).then_inc(sem("rope_mm"), 1)
            elif kind == "diff_s":
                if a == 0:
                    pe.wait_ge(sem("mask16"), 2)
                if a % NB == 0:
                    pe.wait_ge(sem("qk_ready"), 2 * (a // NB) + 2)
                diff_scores(a)
            elif kind == "diff_t":
                pe.wait_ge(sem("diff_w"), a + 1)
                if a:
                    pe.wait_ge(sem("diff_wt"), a)
                transpose_w(a, wbuf, DIFF_T).then_inc(sem("diff_t"), 1)
            elif kind == "diff_v":
                pe.wait_ge(sem("diff_wt"), NB * (a + 1))
                if a:
                    pe.wait_ge(sem("diff_osq"), a)
                weighted_values(a, WT, vtk, DIFF_V).then_inc(sem("diff_pv"), 1)
            elif kind == "ln_sum":
                pe.wait_ge(sem("ln_chunks"), 3)
                pe.wait_ge(sem("qk_ready"), 8)
                mm(PS[:, 3], ones, prod[:, 0]).then_inc(sem("ln_mean_mm"), 1)
            elif kind == "ln_var_sum":
                pe.wait_ge(sem("ln_squares"), 3)
                for b in range(NB):
                    last = token_sum(PS[:, 3, b:b + 1], prod[:, 1, blk(b)])
                last.then_inc(sem("ln_var_mm"), 1)
            elif kind == "ln_bc":
                pe.wait_ge(sem("ln_rstd"), 1)
                for b in range(NB):
                    last = spread(PS[:, 3, blk(b)], lst[:, 4 + b:5 + b])
                last.then_inc(sem("ln_rstd_bc"), 1)
            elif kind == "sub_sum":
                heads_ = range(3) if a == 0 else (3,)
                pe.wait_ge(sem("diff_osq"), heads_[-1] + 1)
                for h in heads_:
                    for b in range(NB):
                        last = token_sum(PS[:, (2, 4)[a], 4 * h + b:4 * h + b + 1], osq[:, h, blk(b)])
                last.then_inc(sem("stat_mm"), 1)
            elif kind == "sub_bc":
                pe.wait_ge(sem("stat_rec"), 1 + a // 3)
                if a < 3:
                    pe.wait_ge(sem("ln_scaled"), 4)
                if a == 2:
                    pe.wait_ge(sem("y_scaled"), 1)
                for b in range(NB):
                    last = spread(PS[:, SUB_BANK[a], blk(b)], ost[:, 1, 4 * a + b:4 * a + b + 1])
                last.then_inc(sem("stat_bc"), 1)

        def out_proj(t0, e0, slots, ready):
            def part(n, some):
                for k in some:
                    if n == 0 or k == slots[-1]:
                        pe.wait_ge(*ready(k))
                    last = product(PS[:, (e0 + n) % 4], wpair((t0 + n) % RING, blk((k + 4) % KD)), (AA[:, k, 0], AA[:, k, 1]),
                                   k == slots[0], k == slots[-1])
                if k == slots[-1]:
                    last.then_inc(tile_used, 1)

            for n in range(2):
                arrived(t0 + n)
                pe.wait_ge(evacuated, e0 + n - 3)
                part(n, slots[:-1])
            for n in range(2):
                part(n, slots[-1:])
            for n in range(2, KD):
                arrived(t0 + n)
                pe.wait_ge(evacuated, e0 + n - 3)
                part(n, slots)

        out_proj(T_OUT0, E_OUT0, (0, 1, 2, 4, 5, 6, 7, 3), lambda k: (y_ready, {0: 1, 1: 2, 2: 3, 3: 8}.get(k, k)))

        def ffn(s, tg, eg, norm):
            for j in range(RING):
                stationary(tg + j, eg + j, HH, feed=KD * norm if j == 0 else None)
                if j == 0:
                    norm_stats(norm, 7)
                if j == 1:
                    norm_spread(norm, 7)
            with pe.Fori(1, KF // 2) as r:
                for j in range(RING):
                    t = tg + j
                    slot = t % RING
                    pe.wait_ge(hi_ready[slot], r + slot_round(t))
                    pe.wait_ge(lo_ready[slot], r + slot_round(t))
                    pe.wait_ge(evacuated, r * RING + (eg + j - 3))
                    for k in range(KD):
                        last = product(PS[:, j], wpair(slot, blk(k)), (HH[:, k, 0], HH[:, k, 1]), k == 0, k == KD - 1)
                    last.then_inc(tile_used, 1)
            td = tg + 2 * KF
            pe.wait_ge(evacuated, eg + 2 * KF)
            for k in range(RING):
                arrived(td + k)
                pe.wait_ge(sem("ffn_lo"), KF * s + k + 1)
                for n in range(KD):
                    last = product(PS[:, n], wpair((td + k) % RING, blk(n)), (AA[:, k, 0], AA[:, k, 1]), k == 0, False)
                last.then_inc(tile_used, 1)
            with pe.Fori(1, KF // RING) as r:
                for j in range(RING):
                    t = td + j
                    pe.wait_ge(hi_ready[t % RING], r + slot_round(t))
                    pe.wait_ge(lo_ready[t % RING], r + slot_round(t))
                    pe.wait_ge(sem("ffn_lo"), r * RING + (KF * s + j + 1))
                    a = [AA[:, bass.ds(r * RING + j, 1), m].rearrange("p a b -> p (a b)") for m in range(2)]
                    for n in range(KD):
                        last = product(PS[:, n], wpair(t % RING, blk(n)), a, False, False)
                    last.then_inc(tile_used, 1)
            rest = range(KF // RING * RING, KF)
            for k in rest:
                arrived(td + k)
            pe.wait_ge(sem("ffn_lo"), KF * (s + 1))
            for n in range(KD):
                for k in rest:
                    last = product(PS[:, n], wpair((td + k) % RING, blk(n)), (AA[:, k, 0], AA[:, k, 1]), False, k == KF - 1)
                    if n == KD - 1:
                        last.then_inc(tile_used, 1)
                if n < KD - 1:
                    last.then_inc(down_done, 1)

        ffn(0, T_GU0, E_GU0, 1)

        def tok_transpose(m):
            pe.wait_ge(sem("gsilu"), m + 5)
            if m >= 2:
                pe.wait_ge(sem("tok_ready"), m - 1)
            src = kT[:, m] if m < H else sqb[:, m % 2]
            for b in range(NB):
                last = nc.tensor.transpose(PS[:, 4 + m % 2, blk(b)], src[:, blk(b)], ident)
            last.then_inc(sem("tok_t"), 1)

        for e in range(12):
            stationary(odd_tile(e), E_IN1 + e, HH, feed=2 * KD if e == 0 else None)
            if e == 0:
                norm_stats(2, 7)
            if e == 1:
                norm_spread(2, 7)
            if e == HEAD_TILE - 1:
                arrived(T_IN1 + HEAD_TILE)
                for k in range(KD):
                    last = product(PS[:, 6], wpair((T_IN1 + HEAD_TILE) % RING, blk(k)), (HH[:, k, 0], HH[:, k, 1]), k == 0, k == KD - 1)
                last.then_inc(tile_used, 1)
            if e == HEAD_TILE + 1:
                pe.wait_ge(small_loaded, 16)
                pe.wait_ge(sem("head_rows"), 1)
                mm(PS[:, 6, 64:76], ones[0:1, :], rowv[0:1, :])
                for b in range(NB):
                    last = nc.tensor.transpose(PS[:, 6, 12 * b:12 * b + 12], hrow[0:12, blk(b)], ident[0:12, 0:12])
                last.then_inc(sem("baf_mm"), 1)
            if 2 <= e < 10:
                c = e - 2
                pe.wait_ge(sem("gsq"), c + 1)
                for b in range(NB):
                    last = token_sum(PS[:, 7, 8 * b + c:8 * b + c + 1], sqb[:, c % 2, blk(b)])
                last.then_inc(sem("l2_mm"), 1)
            if e == 9:
                pe.wait_ge(sem("g_ready"), 1)
                g_all = gtok[:].rearrange("p a b -> p (a b)")
                mm(PS[:, 6, 0:16], cums, g_all)
                mm(PS[:, 6, 16:32], ones, g_all)
                for b in range(NB):
                    for j in range(b + 1):
                        last = mm(PS[:, 6, 32 + 4 * b:36 + 4 * b], cums if j == b else ones, lftok[:, j], j == 0, j == b)
                last.then_inc(sem("g_mm"), 1)
            if e >= 6:
                tok_transpose(e - 6)

        def heads(out_bank, lhs, rhs):
            for h in range(H):
                last = mm(PS[:, out_bank, blk(h)], lhs(h), rhs(h))
            return last

        def gdn(i, k):
            st, j = i % 2, i // 2
            X, Y = 4 + 2 * st, 5 + 2 * st
            decay, kbT, R, NT, qkT, qe = gbufs[st]
            Z, T, wT, vn, kbe = decay, kbT, kbT, decay, NT

            def dve_done(n):
                pe.wait_ge(gdn_dve[st], j * DVE_STEPS + n)

            def act_done(n):
                pe.wait_ge(gdn_act[st], j * ACT_STEPS + n)

            if k == 0:
                if j:
                    dve_done(0)
                    act_done(0)
                for h in range(H):
                    spread(PS[:, X, blk(h)], gcum[:, 0, i, h:h + 1])
                    last = spread(PS[:, Y, blk(h)], kscal[:, 0, i, h:h + 1])
            elif k == 1:
                dve_done(2)
                for h in range(H):
                    last = spread(PS[:, X, blk(h)], qscal[:, i, h:h + 1])
            elif k == 2:
                dve_done(5)
                heads(Y, lambda h: kT[:, h, blk(i)], lambda h: kbT[:, h])
                last = heads(X, lambda h: kT[:, h, blk(i)], lambda h: qT[:, h, blk(i)])
            elif k < STEP_W:
                n, what = ((k - STEP_Z1) // 3 + 1, (k - STEP_Z1) % 3) if k > STEP_T0 else (0, 2)
                if what == 0:
                    act_done(3 + 2 * (n - 1))
                    last = heads(X, lambda h: NT[:, h], lambda h: T[:, h])
                elif what == 1:
                    act_done(4 + 2 * (n - 1))
                    last = heads(Y, lambda h: Z[:, h], lambda h: R[:, h])
                else:
                    dve_done(10 + n)
                    for h in range(H):
                        last = nc.tensor.transpose(PS[:, X, blk(h)], R[:, h], ident)
            elif k == STEP_W:
                dve_done(16)
                pe.wait_ge(gdn_pool[st], j * POOL_STEPS + 2)
                last = heads(X, lambda h: kbe[:, h], lambda h: R[:, h])
            elif k == STEP_V:
                act_done(15)
                pe.wait_ge(sem("state_zero"), 1)
                if i:
                    pe.wait_ge(gdn_dve[(i - 1) % 2], ((i - 1) // 2 + 1) * DVE_STEPS)
                for h in range(H):
                    mm(PS[:, Y, blk(h)], R[:, h], vtok[:, i, h], True, False)
                    last = mm(PS[:, Y, blk(h)], wT[:, h], St_b[:, h], False, True)
            elif k == STEP_O:
                act_done(16)
                for h in range(H):
                    mm(PS[:, X, blk(h)], St_b[:, h], qe[:, h], True, False)
                    last = mm(PS[:, X, blk(h)], vn[:, h], qkT[:, h], False, True)
            elif k == STEP_S:
                pe.wait_ge(gdn_pool[st], j * POOL_STEPS + 3)
                last = heads(Y, lambda h: ktok[:, i, h], lambda h: vn[:, h])
            last.then_inc(gdn_mm[st], 1)

        def tile_part(e, part):
            t = odd_tile(e)
            if part == 0:
                arrived(t)
            if 20 <= e < 24:
                k = 2 * (e - 20) + part // 2
                w = wpair(t % RING, slice(k % 2 * S, (k % 2 + 1) * S))
                for b in (0, 1) if part % 2 == 0 else (2, 3):
                    if k == 0:
                        pe.wait_ge(evacuated, E_IN1 + 20 + b - 3)
                    last = product(PS[:, b], (HH[:, k, 0, blk(b)], HH[:, k, 1, blk(b)]), w, k == 0, k == KD - 1)
            else:
                if part == 0:
                    pe.wait_ge(evacuated, E_IN1 + e - 3)
                for k in (2 * part, 2 * part + 1):
                    last = product(PS[:, e % 4], wpair(t % RING, blk(k)), (HH[:, k, 0], HH[:, k, 1]), k == 0, k == KD - 1)
            if part == 3:
                last.then_inc(tile_used, 1)

        def fox_scores(u):
            h, i = UNITS[u]
            n = (i + 1) * P
            if u >= 2:
                pe.wait_ge(sem("fox_min"), u - 1)
            mm(PS[:, u % 2, 0:n], qd[:, h, blk(i)], kd[:, h, 0:n], True, False)
            mm(PS[:, u % 2, blk(i)], mask16[:, 0], mask16[:, 1], False, True).then_inc(sem("fox_s"), 1)

        for kind, a in odd_order():
            if kind == "gdn":
                if a == (0, 0):
                    pe.wait_ge(sem("gdn_scalars"), 1)
                    pe.wait_ge(sem("tok_ready"), 8)
                gdn(*a)
            elif kind == "tile":
                tile_part(*a)
            elif kind == "tok":
                tok_transpose(a)
            elif kind == "fox_cb":
                if a == 0:
                    pe.wait_ge(evacuated, E_OUT1)
                if a >= 2:
                    pe.wait_ge(sem("fox_y"), a - 1)
                for b in range(NB):
                    last = spread(PS[:, FOX_V, blk(b)], gcum[:, 2, b, a:a + 1])
                last.then_inc(sem("fox_cb_mm"), 1)
            elif kind == "fox_s":
                fox_scores(a)
            elif kind == "fox_t":
                pe.wait_ge(sem("fox_p"), a + 1)
                if a:
                    pe.wait_ge(sem("fox_wt"), a)
                transpose_w(a, fbuf, FOX_T).then_inc(sem("fox_t"), 1)
            elif kind == "fox_v":
                pe.wait_ge(sem("fox_wt"), NB * (a + 1))
                pe.wait_ge(sem("fox_cb"), min(a + 2, H))
                if a:
                    pe.wait_ge(sem("fox_y"), a)
                weighted_values(a, FT, vd, FOX_V).then_inc(sem("fox_pv"), 1)
            elif kind == "norm_sum":
                pe.wait_ge(sem("gdn_osq"), H)
                for b in range(NB):
                    for h in range(H):
                        last = token_sum(PS[:, 4, 4 * h + b:4 * h + b + 1], gsq[:, h, blk(b)])
                last.then_inc(sem("stat_mm"), 1)
            elif kind == "norm_bc":
                pe.wait_ge(sem("stat_rec"), 3)
                for h in range(H):
                    for b in range(NB):
                        last = spread(PS[:, 4 + h, blk(b)], ost[:, 1, 4 * h + b:4 * h + b + 1])
                    last.then_inc(sem("stat_bc"), 1)
        out_proj(T_OUT1, E_OUT1, (4, 5, 6, 7, 0, 1, 2, 3), lambda k: (y_ready, KD + k - 3) if k >= 4 else (sem("fox_y"), k + 1))
        ffn(1, T_GU1, E_GU1, 3)
        norm_stats(4, 7)
        norm_spread(4, 7)

    block.__exit__(None, None, None)


def kernel(x, mix_norm_w, ffn_norm_w, final_norm_w, w_in_even, conv_w, conv_b, conv_ln_w, conv_ln_b,
           lambda_q1, lambda_k1, lambda_q2, lambda_k2, diff_subln_w, gdn_conv_w, w_in_odd,
           gdn_a_log, gdn_dt_bias, gdn_norm_w, fox_forget_bias, w_out, w_gate, w_up, w_down):
    import concourse.bacc as bacc
    from concourse.bass_utils import run_bass_kernel_spmd

    f = np.asarray

    def chunks(w):
        k, n = w.shape
        return w.reshape(k // P, P, n // P, P).transpose(2, 1, 0, 3).reshape(n // P, P, k // P * P)

    def movers(w):
        return w.reshape(4, 2, P, S).transpose(0, 2, 1, 3).reshape(4, P, 2 * S)

    def ffn_tiles(l):
        gu = np.stack([chunks(f(w_gate)[l]), chunks(f(w_up)[l])], axis=1)
        return [gu.reshape(2 * KF, P, TILE), f(w_down)[l].reshape(KF, P, TILE)]

    we, wo = f(w_in_even)[0], f(w_in_odd)[0]
    heads = np.zeros((D, P), np.float32)
    heads[:, 0:8], heads[:, 8:12] = wo[:, 2048:2056], wo[:, 3592:3596]
    heads = chunks(heads)
    val_gate = np.stack([chunks(we[:, 0:512]), chunks(we[:, 512:1024])], axis=1).reshape(8, P, TILE)
    query_key = np.stack([chunks(we[:, 1024:1536]), chunks(we[:, 1536:2048])], axis=1).reshape(8, P, TILE)
    stream = np.ascontiguousarray(np.concatenate(
        [val_gate, movers(we[:, 2048:2560]), query_key, chunks(f(w_out)[0])] + ffn_tiles(0)
        + [chunks(wo[:, 0:512]), heads, chunks(wo[:, 512:1536]), chunks(wo[:, 2056:3080]), movers(wo[:, 3080:3592]), chunks(wo[:, 1536:2048]),
           chunks(f(w_out)[1])] + ffn_tiles(1)))
    assert stream.shape == (N_TILES, P, TILE)
    def cols(v):
        v = f(v)
        v = v.reshape(v.shape[0] // P, P, -1)
        return v.transpose(1, 0, 2).reshape(P, -1)

    norms = [cols(w) for w in (f(mix_norm_w)[0], f(ffn_norm_w)[0], f(mix_norm_w)[1], f(ffn_norm_w)[1], f(final_norm_w))]
    lams = np.zeros((P, 4), np.float32)
    for n, v in enumerate((lambda_q1, lambda_k1, lambda_q2, lambda_k2)):
        lams[0:64, n] = f(v)[0]
    vecs = np.ascontiguousarray(np.concatenate(
        norms + [cols(f(conv_w)[0].T), cols(f(conv_b)[0]), cols(f(conv_ln_w)[0]), cols(f(conv_ln_b)[0]),
                 cols(f(diff_subln_w)[0]), cols(f(gdn_conv_w)[0].T), cols(f(gdn_norm_w)[0]), lams], axis=1))
    assert vecs.shape == (P, N_VEC)
    row = np.concatenate([f(gdn_a_log)[0], f(gdn_dt_bias)[0], f(fox_forget_bias)[0]]).reshape(1, 12)
    xt = np.ascontiguousarray(f(x)[0].T.reshape(KD, P, S).transpose(1, 0, 2))
    const, rope = shape_constants()

    nc = bacc.Bacc("TRN2", target_bir_lowering=False, num_devices=1)
    f32 = mybir.dt.float32
    arrays = {"x_t": xt, "w_stream": stream, "vectors": vecs, "row": row,
              "shape_const": const, "rope_const": rope}
    args = [nc.dram_tensor(n, a.shape, f32, kind="ExternalInput").ap() for n, a in arrays.items()]
    out = nc.dram_tensor("out_t", (P, KD, S), f32, kind="ExternalOutput").ap()
    build(nc, *args, out)
    r = run_bass_kernel_spmd(nc, [arrays], core_ids=[0])
    got = r.results[0]["out_t"]
    return np.ascontiguousarray(got.transpose(2, 1, 0).reshape(1, S, D))
```
